# Optimizing a Trainium2 kernel written in Bass

```python
import jax
import jax.numpy as jnp
from jax import lax
import numpy as np

D_MODEL = 1024
BATCH = 1
SEQ = 1024
DEPTH = 2

GRID_W = 64
CTX_LEN = 256
ML_HEADS = 4
ML_DH = D_MODEL // 16
ML_W = ML_HEADS * ML_DH
ML_CONV = 3
HG_HEADS = 4
HG_DK = D_MODEL // 16
HG_DV = D_MODEL // 16
HG_WK = HG_HEADS * HG_DK
HG_W = HG_HEADS * HG_DV
MLA_HEADS = 8
MLA_NOPE = D_MODEL // 16
MLA_ROPE = D_MODEL // 32
MLA_DQK = MLA_NOPE + MLA_ROPE
MLA_DV = D_MODEL // 16
MLA_W = MLA_HEADS * MLA_DV
MLA_Q_RANK = D_MODEL // 4
MLA_KV_RANK = D_MODEL // 8
MIX_W = ML_W + HG_W + MLA_W
N_EXPERTS = 16
EC_CAPACITY = 2
D_EXPERT = D_MODEL
CHUNK = 64
Q_BLOCK = 128
ROPE_THETA = 10000.0
EPS = 1e-6
IN_SPLITS = (2 * ML_W, ML_W, ML_W, 4 * ML_HEADS,
             HG_WK, HG_W, HG_W, 2 * HG_WK,
             MLA_Q_RANK, MLA_KV_RANK, MLA_ROPE)
D_IN = sum(IN_SPLITS)

kernel_name = 'hybrid_mlstm_hgrn2_mla_ecmoe_dit'

def _rms(x, g):
    xf = x.astype(jnp.float32)
    y = xf * lax.rsqrt(jnp.mean(xf * xf, axis=-1, keepdims=True) + EPS)
    return (y * g.astype(jnp.float32)).astype(x.dtype)

def _heads(a, n_heads):
    b, n, _ = a.shape
    return a.reshape(b, n, n_heads, -1).transpose(0, 2, 1, 3)

def _merge_heads(a):
    b, h, n, d = a.shape
    return a.transpose(0, 2, 1, 3).reshape(b, n, h * d)

def _head_norm_merge(a, g):
    b, h, n, d = a.shape
    return _rms(a.transpose(0, 2, 1, 3), g.reshape(h, d)).reshape(b, n, h * d)

def _dwconv(a, w, bias):
    ch = a.shape[-1]
    y = lax.conv_general_dilated(a, w[:, None, :].astype(a.dtype), window_strides=(1,), padding='SAME',
                                 dimension_numbers=('NWC', 'WIO', 'NWC'), feature_group_count=ch)
    return y + bias.astype(a.dtype)

def _split_proj(h, w_in, b_in):
    points = np.cumsum(IN_SPLITS)[:-1].tolist()
    return jnp.split(h @ w_in + b_in, points, axis=-1)

def _rope_tables(pos):
    half = MLA_ROPE // 2
    inv = ROPE_THETA ** (-jnp.arange(0, half, 2, dtype=jnp.float32) / half)
    ang = pos.astype(jnp.float32)[:, None] * inv[None, :]
    ang = jnp.concatenate([ang, ang], axis=-1)
    return jnp.cos(ang), jnp.sin(ang)

def _rotate(x, cos, sin):
    x1, x2 = jnp.split(x, 2, axis=-1)
    return (x * cos + jnp.concatenate([-x2, x1], axis=-1) * sin).astype(x.dtype)

def _axial_rope(x, rope):
    cos_r, sin_r, cos_c, sin_c = rope
    x_nope, x_row, x_col = jnp.split(x, [MLA_NOPE, MLA_NOPE + MLA_ROPE // 2], axis=-1)
    return jnp.concatenate([x_nope, _rotate(x_row, cos_r, sin_r), _rotate(x_col, cos_c, sin_c)], axis=-1)

def _to_chunks(a):
    b, h, n = a.shape[:3]
    return jnp.moveaxis(a.reshape((b, h, n // CHUNK, CHUNK) + a.shape[3:]), 2, 0)

def _from_chunks(y):
    nc, b, h, l = y.shape[:4]
    return jnp.moveaxis(y, 0, 2).reshape((b, h, nc * l) + y.shape[4:])

def _chunked_scan(out_fn, update_fn, inputs, state0):
    def step(state, chunk):
        return update_fn(state, chunk), out_fn(state, chunk)
    state, ys = lax.scan(step, state0, tuple(_to_chunks(a) for a in inputs))
    return _from_chunks(ys), state

def _mlstm_out(state, chunk):
    c_mat, n_vec, m = state
    q, k, v, log_f, ig = chunk
    L = log_f.shape[-1]
    seen = jnp.tril(jnp.ones((L, L), dtype=bool))
    b = jnp.cumsum(log_f, axis=-1)
    d = jnp.where(seen, b[..., :, None] - b[..., None, :] + ig[..., None, :], -jnp.inf)
    inter = b + m[..., None]
    m_t = jnp.maximum(inter, d.max(axis=-1))
    w_tok = jnp.exp(d - m_t[..., None])
    w_st = jnp.exp(inter - m_t)
    s = jnp.einsum('bhtd,bhsd->bhts', q, k) * w_tok
    num = jnp.einsum('bhts,bhsv->bhtv', s, v) + w_st[..., None] * jnp.einsum('bhtk,bhkv->bhtv', q, c_mat)
    den = s.sum(axis=-1) + w_st * jnp.einsum('bhtk,bhk->bht', q, n_vec)
    return num / jnp.maximum(jnp.abs(den), jnp.exp(-m_t))[..., None]

def _mlstm_update(state, chunk):
    c_mat, n_vec, m = state
    _, k, v, log_f, ig = chunk
    b = jnp.cumsum(log_f, axis=-1)
    b_end = b[..., -1]
    w_log = b_end[..., None] - b + ig
    m_new = jnp.maximum(b_end + m, w_log.max(axis=-1))
    w_tok = jnp.exp(w_log - m_new[..., None])
    w_st = jnp.exp(b_end + m - m_new)
    c_new = w_st[..., None, None] * c_mat + jnp.einsum('bhs,bhsk,bhsv->bhkv', w_tok, k, v)
    n_new = w_st[..., None] * n_vec + jnp.einsum('bhs,bhsk->bhk', w_tok, k)
    return (c_new, n_new, m_new)

def _hgrn_out(s_mat, chunk):
    q, k, v, log_f = chunk
    L = log_f.shape[-2]
    seen = jnp.tril(jnp.ones((L, L), dtype=bool))[:, :, None]
    b = jnp.cumsum(log_f, axis=-2)
    dec = jnp.exp(jnp.where(seen, b[..., :, None, :] - b[..., None, :, :], -jnp.inf))
    a = jnp.einsum('bhtk,bhsk,bhtsk->bhts', q, k, dec)
    return jnp.einsum('bhts,bhsv->bhtv', a, v) + jnp.einsum('bhtk,bhkv->bhtv', q * jnp.exp(b), s_mat)

def _hgrn_update(s_mat, chunk):
    _, k, v, log_f = chunk
    b = jnp.cumsum(log_f, axis=-2)
    b_end = b[..., -1:, :]
    return jnp.exp(b_end[..., 0, :])[..., None] * s_mat + jnp.einsum('bhsk,bhsv->bhkv', k * jnp.exp(b_end - b), v)

def _flip_time(inputs):
    return tuple(jnp.flip(a, axis=2) for a in inputs)

def _bidir_recurrence(out_fn, update_fn, ctx_dirs, lat_dirs, state0, need_ctx):
    y_ctx, y_lat = None, None
    for d in range(2):
        c_in, l_in = ctx_dirs[d], lat_dirs[d]
        if d == 1:
            c_in, l_in = _flip_time(c_in), _flip_time(l_in)
        if need_ctx:
            yc, state = _chunked_scan(out_fn, update_fn, c_in, state0)
            yc = jnp.flip(yc, axis=2) if d == 1 else yc
            y_ctx = yc if y_ctx is None else y_ctx + yc
        else:
            state = update_fn(state0, c_in)
        yl, _ = _chunked_scan(out_fn, update_fn, l_in, state)
        yl = jnp.flip(yl, axis=2) if d == 1 else yl
        y_lat = yl if y_lat is None else y_lat + yl
    return y_ctx, y_lat

def _mlstm_dirs(qk, v, gates):
    f32 = jnp.float32
    q, k = jnp.split(qk, 2, axis=-1)
    q = _heads(q, ML_HEADS).astype(f32)
    k = _heads(k, ML_HEADS).astype(f32) * (ML_DH ** -0.5)
    v = _heads(v, ML_HEADS).astype(f32)
    b, n, _ = gates.shape
    g = jnp.moveaxis(gates.astype(f32).reshape(b, n, 2, 2, ML_HEADS), 1, -1)
    return tuple((q, k, v, jax.nn.log_sigmoid(g[:, d, 1]), g[:, d, 0]) for d in range(2))

def _hgrn_dirs(q, i, f, lb):
    f32 = jnp.float32
    q = _heads(jax.nn.silu(q), HG_HEADS).astype(f32)
    v = _heads(i, HG_HEADS).astype(f32)
    b, n, _ = f.shape
    f = f.astype(f32).reshape(b, n, 2, HG_WK)
    dirs = []
    for d in range(2):
        pre, low = f[:, :, d], lb[d]
        log_f = jnp.logaddexp(jnp.log(low), jnp.log1p(-low) + jax.nn.log_sigmoid(pre))
        k = (1.0 - low) * jax.nn.sigmoid(-pre)
        dirs.append((q, _heads(k, HG_HEADS), v, _heads(log_f, HG_HEADS)))
    return tuple(dirs)

def _mla_q(cq, p, rope):
    b, n, _ = cq.shape
    q = (_rms(cq, p['mla_q_norm_g']) @ p['mla_w_uq']).reshape(b, n, MLA_HEADS, MLA_DQK)
    q = _rms(q, p['mla_q_qk_g']).transpose(0, 2, 1, 3)
    return q if rope is None else _axial_rope(q, rope)

def _mla_kv(ckv, kr, p, rope):
    b, n, _ = ckv.shape
    kv = (_rms(ckv, p['mla_kv_norm_g']) @ p['mla_w_ukv']).reshape(b, n, MLA_HEADS, MLA_NOPE + MLA_DV)
    k_nope, v = jnp.split(kv, [MLA_NOPE], axis=-1)
    k_rope = jnp.broadcast_to(kr[:, :, None, :], (b, n, MLA_HEADS, MLA_ROPE))
    k = _rms(jnp.concatenate([k_nope, k_rope], axis=-1), p['mla_k_qk_g']).transpose(0, 2, 1, 3)
    k = k if rope is None else _axial_rope(k, rope)
    return k, v.transpose(0, 2, 1, 3)

def _attend(q, k, v):
    s = jnp.einsum('bhqd,bhkd->bhqk', q, k).astype(jnp.float32) * (MLA_DQK ** -0.5)
    pr = jax.nn.softmax(s, axis=-1).astype(v.dtype)
    return jnp.einsum('bhqk,bhkd->bhqd', pr, v)

def _block_attend(q, k, v):
    b, h, n, d = q.shape
    qb = jnp.moveaxis(q.reshape(b, h, n // Q_BLOCK, Q_BLOCK, d), 2, 0)
    o = lax.map(lambda qq: _attend(qq, k, v), qb)
    return jnp.moveaxis(o, 0, 2).reshape(b, h, n, -1)

def _token_mixers(hc, hl, rope, lb, p, need_ctx):
    f32 = jnp.float32
    pc = _split_proj(hc, p['w_in'], p['b_in'])
    pl = _split_proj(hl, p['w_in'], p['b_in'])
    bsz = hl.shape[0]

    def ml_dirs(parts):
        qk = jax.nn.silu(_dwconv(parts[0], p['ml_conv_w'], p['ml_conv_b']))
        return _mlstm_dirs(qk, parts[1], parts[3])
    ml_state0 = (jnp.zeros((bsz, ML_HEADS, ML_DH, ML_DH), f32),
                 jnp.zeros((bsz, ML_HEADS, ML_DH), f32),
                 jnp.zeros((bsz, ML_HEADS), f32))
    ml_c, ml_l = _bidir_recurrence(_mlstm_out, _mlstm_update, ml_dirs(pc), ml_dirs(pl), ml_state0, need_ctx)

    hg_state0 = jnp.zeros((bsz, HG_HEADS, HG_DK, HG_DV), f32)
    hg_c, hg_l = _bidir_recurrence(_hgrn_out, _hgrn_update, _hgrn_dirs(pc[4], pc[5], pc[7], lb),
                                   _hgrn_dirs(pl[4], pl[5], pl[7], lb), hg_state0, need_ctx)

    k_c, v_c = _mla_kv(pc[9], pc[10], p, None)
    k_l, v_l = _mla_kv(pl[9], pl[10], p, rope)
    q_l = _mla_q(pl[8], p, rope)
    at_l = _block_attend(q_l, jnp.concatenate([k_c, k_l], axis=2), jnp.concatenate([v_c, v_l], axis=2))

    def merge(parts, ml, hg, at, dtype):
        y = jnp.concatenate([
            _head_norm_merge(ml, p['ml_norm_g']) * jax.nn.sigmoid(parts[2].astype(f32)),
            _head_norm_merge(hg, p['hg_norm_g']) * jax.nn.silu(parts[6].astype(f32)),
            _merge_heads(at).astype(f32)], axis=-1).astype(dtype)
        return y @ p['w_out']

    y_lat = merge(pl, ml_l, hg_l, at_l, hl.dtype)
    if not need_ctx:
        return None, y_lat
    at_c = _attend(_mla_q(pc[8], p, None), k_c, v_c)
    return merge(pc, ml_c, hg_c, at_c, hc.dtype), y_lat

def _expert_choice_ffn(h, router_w, w_gate, w_up, w_down):
    b, n, _ = h.shape
    cap = EC_CAPACITY * n // N_EXPERTS
    aff = jax.nn.softmax((h @ router_w).astype(jnp.float32), axis=-1)
    gate, idx = lax.top_k(jnp.swapaxes(aff, 1, 2), cap)
    bidx = jnp.arange(b)[:, None, None]
    xs = h[bidx, idx]
    hid = jax.nn.silu(jnp.einsum('becd,edf->becf', xs, w_gate)) * jnp.einsum('becd,edf->becf', xs, w_up)
    out = jnp.einsum('becf,efd->becd', hid, w_down) * gate[..., None].astype(h.dtype)
    return jnp.zeros_like(h).at[bidx, idx].add(out)

def setup_inputs(seed: int = 0) -> dict:
    key = jax.random.key(seed)
    ks = jax.random.split(key, 26)
    nrm = jax.random.normal
    f32 = jnp.float32
    D, L = D_MODEL, DEPTH
    fb = np.zeros((D_IN,), np.float32)
    off = 4 * ML_W
    fb[off + ML_HEADS: off + 2 * ML_HEADS] = np.linspace(3.0, 6.0, ML_HEADS)
    fb[off + 3 * ML_HEADS: off + 4 * ML_HEADS] = np.linspace(3.0, 6.0, ML_HEADS)
    return {
        'x': nrm(ks[0], (BATCH, SEQ, D), f32),
        'c': nrm(ks[1], (BATCH, D), f32),
        'ctx': nrm(ks[2], (BATCH, CTX_LEN, D), f32),
        'c_ctx': nrm(ks[3], (D,), f32),
        'ada_w': nrm(ks[4], (L, D, 6 * D), f32) * (0.5 * D ** -0.5),
        'ada_b': nrm(ks[5], (L, 6 * D), f32) * 0.02,
        'norm1_g': 1.0 + 0.05 * nrm(ks[6], (L, D), f32),
        'norm2_g': 1.0 + 0.05 * nrm(ks[7], (L, D), f32),
        'w_in': nrm(ks[8], (L, D, D_IN), f32) * D ** -0.5,
        'b_in': nrm(ks[9], (L, D_IN), f32) * 0.02 + jnp.asarray(fb),
        'ml_conv_w': nrm(ks[10], (L, ML_CONV, 2 * ML_W), f32) * ML_CONV ** -0.5,
        'ml_conv_b': nrm(ks[11], (L, 2 * ML_W), f32) * 0.02,
        'ml_norm_g': 1.0 + 0.05 * nrm(ks[12], (L, ML_W), f32),
        'hg_lb_logits': nrm(ks[13], (L, 2, HG_WK), f32) * 0.1,
        'hg_norm_g': 1.0 + 0.05 * nrm(ks[14], (L, HG_W), f32),
        'mla_q_norm_g': 1.0 + 0.05 * nrm(ks[15], (L, MLA_Q_RANK), f32),
        'mla_w_uq': nrm(ks[16], (L, MLA_Q_RANK, MLA_HEADS * MLA_DQK), f32) * MLA_Q_RANK ** -0.5,
        'mla_kv_norm_g': 1.0 + 0.05 * nrm(ks[17], (L, MLA_KV_RANK), f32),
        'mla_w_ukv': nrm(ks[18], (L, MLA_KV_RANK, MLA_HEADS * (MLA_NOPE + MLA_DV)), f32) * MLA_KV_RANK ** -0.5,
        'mla_q_qk_g': 1.0 + 0.05 * nrm(ks[19], (L, MLA_DQK), f32),
        'mla_k_qk_g': 1.0 + 0.05 * nrm(ks[20], (L, MLA_DQK), f32),
        'w_out': nrm(ks[21], (L, MIX_W, D), f32) * MIX_W ** -0.5,
        'router_w': nrm(ks[22], (L, D, N_EXPERTS), f32) * D ** -0.5,
        'ex_w_gate': nrm(ks[23], (L, N_EXPERTS, D, D_EXPERT), f32) * D ** -0.5,
        'ex_w_up': nrm(ks[24], (L, N_EXPERTS, D, D_EXPERT), f32) * D ** -0.5,
        'ex_w_down': nrm(ks[25], (L, N_EXPERTS, D_EXPERT, D), f32) * D_EXPERT ** -0.5,
    }

def reference(x, c, ctx, c_ctx, ada_w, ada_b, norm1_g, norm2_g, w_in, b_in, ml_conv_w, ml_conv_b,
              ml_norm_g, hg_lb_logits, hg_norm_g, mla_q_norm_g, mla_w_uq, mla_kv_norm_g, mla_w_ukv,
              mla_q_qk_g, mla_k_qk_g, w_out, router_w, ex_w_gate, ex_w_up, ex_w_down):
    n_lat = x.shape[1]
    rows = n_lat // GRID_W
    row_pos = jnp.repeat(jnp.arange(rows), GRID_W)
    col_pos = jnp.broadcast_to(jnp.arange(GRID_W), (rows, GRID_W)).reshape(-1)
    cos_r, sin_r = _rope_tables(row_pos)
    cos_c, sin_c = _rope_tables(col_pos)
    rope = (cos_r, sin_r, cos_c, sin_c)

    lb_all = jnp.cumsum(jax.nn.softmax(hg_lb_logits.astype(jnp.float32), axis=0), axis=0)
    lb_all = lb_all - lb_all[:1]

    for layer in range(DEPTH):
        need_ctx = layer < DEPTH - 1
        p = {'w_in': w_in[layer], 'b_in': b_in[layer], 'ml_conv_w': ml_conv_w[layer],
             'ml_conv_b': ml_conv_b[layer], 'ml_norm_g': ml_norm_g[layer], 'hg_norm_g': hg_norm_g[layer],
             'mla_q_norm_g': mla_q_norm_g[layer], 'mla_w_uq': mla_w_uq[layer],
             'mla_kv_norm_g': mla_kv_norm_g[layer], 'mla_w_ukv': mla_w_ukv[layer],
             'mla_q_qk_g': mla_q_qk_g[layer], 'mla_k_qk_g': mla_k_qk_g[layer], 'w_out': w_out[layer]}
        mod = jnp.split(jax.nn.silu(c) @ ada_w[layer] + ada_b[layer], 6, axis=-1)
        sh1, sc1, g1, sh2, sc2, g2 = [m[:, None, :] for m in mod]
        csh1, csc1, cg1, csh2, csc2, cg2 = jnp.split(jax.nn.silu(c_ctx) @ ada_w[layer] + ada_b[layer], 6, axis=-1)

        hl = _rms(x, norm1_g[layer]) * (1.0 + sc1) + sh1
        hc = _rms(ctx, norm1_g[layer]) * (1.0 + csc1) + csh1
        y_ctx, y_lat = _token_mixers(hc, hl, rope, lb_all[layer], p, need_ctx)
        x = x + g1 * y_lat
        x = x + g2 * _expert_choice_ffn(_rms(x, norm2_g[layer]) * (1.0 + sc2) + sh2, router_w[layer],
                                        ex_w_gate[layer], ex_w_up[layer], ex_w_down[layer])
        if need_ctx:
            ctx = ctx + cg1 * y_ctx
            ctx = ctx + cg2 * _expert_choice_ffn(_rms(ctx, norm2_g[layer]) * (1.0 + csc2) + csh2, router_w[layer],
                                                 ex_w_gate[layer], ex_w_up[layer], ex_w_down[layer])
    return x


_drawn_inputs = setup_inputs


def setup_inputs(seed=0):
    import zlib

    import numpy as np

    out = dict(_drawn_inputs(seed))
    spreads = {}
    factors = {'ctx': 3.066,
     'ada_b': 2.672,
     'norm1_g': 4.01,
     'norm2_g': 3.616,
     'ml_conv_b': 8.0,
     'ml_norm_g': 7.973,
     'hg_lb_logits': 8.0,
     'hg_norm_g': 6.775,
     'mla_q_norm_g': 8.0,
     'mla_kv_norm_g': 8.0,
     'mla_q_qk_g': 8.0,
     'mla_k_qk_g': 8.0}
    for name, (base, spread) in spreads.items():
        noise = np.random.default_rng([zlib.crc32(name.encode()), seed]).standard_normal(out[name].shape)
        drawn = base * np.exp(spread * noise) if base else spread * noise
        out[name] = jnp.asarray(drawn.astype(out[name].dtype))
    for name, factor in factors.items():
        out[name] = (out[name] * factor).astype(out[name].dtype)
    return out
```

```python
from contextlib import ExitStack

import numpy as np
import concourse.bass as bass
from concourse import mybir

ALU = mybir.AluOpType
ACT = mybir.ActivationFunctionType
AX = mybir.AxisListType
F32 = mybir.dt.float32
U32 = mybir.dt.uint32

P = 128
D = 1024
KD = D // P
NCTX, NLAT = 256, 1024
JC, JL = NCTX // P, NLAT // P
NJ = JC + JL
T = NJ * P
DEPTH = 2
H = 4
DH = 64
MH, DQK, DN, DV, DR = 8, 96, 64, 64, 32
NE, CAPL, CAPC = 16, NLAT // 8, NCTX // 8
CAP = CAPL + CAPC
EPS = 1e-6
D_IN = 2736
NEG = -1e30
LEVELS = [64, 32, 16, 8, 4, 2, 1]

FM_COLS = [0, 128, 256, 384, 1040, 1168, 1808, 1936, 2064, 2192]
TM_COLS = [(512, 776), (776, 1040), (1296, 1552), (1552, 1808), (2320, 2576), (2576, 2736)]
TMW = sum(b - a for a, b in TM_COLS)
TM_V, TM_OG, TM_GATE, TM_HI, TM_HG, TM_CQ, TM_CKV, TM_KR = 0, 256, 512, 528, 784, 1040, 1296, 1424

ORDER = [list(range(NJ)), list(range(JC - 1, -1, -1)) + list(range(NJ - 1, JC - 1, -1))]
GROUPS = [(0, JC), (JC, 4), (JC + 4, 4)]


def consts():
    i = np.arange(P)
    s, t = i[:, None], i[None, :]
    parts = {
        "ident": s == t, "flip": s + t == P - 1, "le": s <= t, "ge": s >= t, "ones": s + t >= 0,
        "mhalf": np.full((P, 80), -0.5),
        "mask0": np.where(s <= t, 0.0, NEG), "mask1": np.where(s >= t, 0.0, NEG),
    }
    for m in LEVELS:
        fwd = (s // (2 * m) == t // (2 * m)) & (s % (2 * m) < m) & (t % (2 * m) >= m)
        parts[f"lvl{m}"] = np.concatenate([fwd, fwd.T], 1)
    col, at = {}, 0
    for n, a in parts.items():
        col[n] = (at, a.shape[1])
        at += a.shape[1]
    return np.concatenate([np.asarray(a, np.float32) for a in parts.values()], 1), col


def rope_table():
    half = DR // 2
    inv = np.float32(10000.0) ** (-np.arange(0, half, 2, dtype=np.float32) / np.float32(half))
    pos = np.arange(NLAT)
    out = []
    for p in (pos // 64, pos % 64):
        ang = p.astype(np.float32)[:, None] * inv[None].astype(np.float32)
        out.append((np.cos(ang), np.sin(ang)))
    (cr, sr), (cc, sc) = out
    return np.concatenate([cr, cr, cc, cc, -sr, sr, -sc, sc], 1).astype(np.float32)


class Chain:

    def __init__(self, sem):
        self.sem, self.n, self.more = sem, 0, 0

    def did(self, ins):
        ins.then_inc(self.sem, 1)
        self.n += 1

    def settle(self, eng):
        if self.n or not isinstance(self.more, int):
            eng.wait_ge(self.sem, self.n + self.more)

    def step(self, eng, ins):
        self.did(ins)
        self.settle(eng)


def build(nc, a, out):
    _, CC = consts()
    c = ExitStack()
    with c, nc.allow_non_contiguous_dma(reason="short parameter vectors onto partitions"):
        def sb(name, shape, dt=F32):
            return c.enter_context(nc.sbuf_tensor(name, shape, dt))

        def sem(name):
            return c.enter_context(nc.semaphore(name))

        xres = nc.dram_tensor("xres", (T, D), F32, kind="Internal").ap()
        xnd = nc.dram_tensor("xnd", (T, D), F32, kind="Internal").ap()
        modd = nc.dram_tensor("modd", (DEPTH * 2, 6 * D), F32, kind="Internal").ap()

        ar = sb("arena", [P, 48608])
        cst = sb("cst", [P, sum(w for _, w in CC.values())])
        modT = sb("modT", [P, 2, 48])
        AB = sb("AB", [P, 2, 2, 2, KD])
        gcol = sb("gcol", [P, 2, KD])
        ss = sb("ss", [P, 4 * NJ])
        rs = sb("rs", [P, 4 * NJ])
        ropes = sb("ropes", [P, JL, 2 * DR])
        small = sb("small", [P, 160])
        gainr = sb("gainr", [P, H * DH])
        ps = c.enter_context(nc.psum_tensor("ps", [P, 8, 512], F32))

        def K(name):
            return cst[:, CC[name][0]:CC[name][0] + CC[name][1]]

        ident, ones = K("ident"), K("ones")

        ended = sem("stage_ended")
        const_in = sem("const_in")
        dve = Chain(sem("vector_own"))
        pool = Chain(sem("gpsimd_own"))
        act = Chain(sem("scalar_own"))
        sems = {}

        def S(name):
            if name not in sems:
                sems[name] = sem(name)
            return sems[name]

        def V(lo, shape):
            n = int(np.prod(shape))
            v = ar[:, lo:lo + n]
            if len(shape) == 2:
                v = v.rearrange("p (a b) -> p a b", b=shape[1])
            if len(shape) == 3:
                v = v.rearrange("p (a b c) -> p a b c", b=shape[1], c=shape[2])
            if len(shape) == 4:
                v = v.rearrange("p (a b c d) -> p a b c d", b=shape[1], c=shape[2], d=shape[3])
            return v

        def rsqrt(e, o, x, eps):
            pool.step(e, e.tensor_scalar(o, x, eps, None, ALU.add))
            return e.tensor_tensor(o, o, K("mhalf")[:, 0:o.shape[1]], ALU.pow)

        stages = []

        def stage(**parts):
            stages.append(parts)

        def ada(l):
            panel = [V(n * 4096, (KD, 512)) for n in range(2)]
            row = V(8192, (6 * D,))
            bias = V(8192 + 6 * D, (6 * D,))
            cT = V(8192 + 12 * D, (KD, 2))
            base = l * 12

            def sp(e):
                for s, src in enumerate((a["c_ctx"], a["c"].rearrange("a d -> (a d)"))):
                    e.dma_start(cT[:, :, s:s + 1], src.rearrange("(k p o) -> p k o", p=P, o=1)).then_inc(S("c_in"), 16)
                for s in range(2):
                    e.dma_start(bias[s:s + 1, :], a["ada_b"][l:l + 1, :]).then_inc(S("c_in"), 16)
                for n, g in enumerate(("norm1_g", "norm2_g")):
                    e.dma_start(gcol[:, n, :], a[g][l].rearrange("(k p) -> p k", p=P)).then_inc(S("c_in"), 16)
                w = a["ada_w"][l].rearrange("(k p) n -> p k n", p=P)
                for n in range(12):
                    if n >= 2:
                        e.wait_ge(S("ada_mm"), base + n - 1)
                    e.dma_start(panel[n % 2], w[:, :, n * 512:(n + 1) * 512]).then_inc(S(f"ada_w{n % 2}"), 16)
                e.wait_ge(S("ada_row"), base + 12)
                e.dma_start(modd[2 * l:2 * l + 2, :], row[0:2, :]).then_inc(S("mod_out"), 16)
                e.wait_ge(S("mod_out"), 16 * (l + 1))

            def sc(e):
                e.wait_ge(S("c_in"), 96 * (l + 1))
                e.activation(cT, cT, ACT.Silu).then_inc(S("c_silu"), 1)

            def pe(e):
                e.wait_ge(S("c_silu"), l + 1)
                for n in range(12):
                    e.wait_ge(S(f"ada_w{n % 2}"), 16 * (6 * l + n // 2 + 1))
                    if n >= 4:
                        e.wait_ge(S("ada_row"), base + n - 3)
                    for k in range(KD):
                        mm = e.matmul(ps[0:2, n % 4, :], cT[:, k, :], panel[n % 2][:, k, :], start=k == 0, stop=k == KD - 1)
                    mm.then_inc(S("ada_mm"), 1)
                e.wait_ge(S("ada_row"), base + 12)
                for m in range(48):
                    mm = e.transpose(ps[:, 4, 2 * m:2 * m + 2], row[0:2, m * P:(m + 1) * P], ident[0:2, 0:2])
                mm.then_inc(S("ada_t"), 1)

            def ve(e):
                for n in range(12):
                    e.wait_ge(S("ada_mm"), base + n + 1)
                    if n == 0:
                        e.wait_ge(S("c_in"), 96 * (l + 1))
                    e.tensor_tensor(row[0:2, n * 512:(n + 1) * 512], ps[0:2, n % 4, :], bias[0:2, n * 512:(n + 1) * 512],
                                    ALU.add).then_inc(S("ada_row"), 1)
                e.wait_ge(S("ada_t"), l + 1)
                dve.step(e, e.tensor_copy(modT[:, :, :], ps[:, 4, 0:96].rearrange("p (m s) -> p s m", s=2)))
                for n in range(2):
                    for s in range(2):
                        o = 3 * n * KD
                        dve.did(e.scalar_tensor_tensor(AB[:, n, s, 0, :], modT[:, s, o + KD:o + 2 * KD], 1.0,
                                                       gcol[:, n, :], ALU.add, ALU.mult))
                        dve.did(e.tensor_copy(AB[:, n, s, 1, :], modT[:, s, o:o + KD]))

            stage(sync=sp, scalar=sc, tensor=pe, vector=ve)

        norm_groups = [0]
        xn_stores, xn_all = [0, 0], [{}, {}]

        def norm(l, n):
            groups = GROUPS if not (l == 1 and n == 1) else GROUPS[1:]
            xg = [V(40000 - 4096 * (2 - i), (4, D)) for i in range(2)]
            junk = V(40000, (D,))
            hT = V(0, (KD, T))
            g0 = norm_groups[0]
            norm_groups[0] += len(groups)

            def source(j):
                if n == 0 and l == 0:
                    return (a["ctx"] if j < JC else a["x"])[0].rearrange("(j p) d -> p j d", p=P), (j if j < JC else j - JC)
                if l == 1 and n == 1:
                    return out[0].rearrange("(j p) d -> p j d", p=P), j - JC
                return xres.rearrange("(j p) d -> p j d", p=P), j

            def sp(e):
                for i, (j0, nj) in enumerate(groups):
                    g = g0 + i
                    if i >= 2:
                        e.wait_ge(S("norm_t"), KD * (g - 1))
                        if n == 1:
                            e.wait_ge(S(f"xn_out{g % 2}"), 16 * (xn_count[g % 2][g] - 1))
                    src, j = source(j0)
                    e.dma_start(xg[g % 2][:, 0:nj, :], src[:, j:j + nj, :]).then_inc(S(f"x_in{g % 2}"), 16)
                    if i == 0:
                        continue
                    if n == 1:
                        store(e, i - 1)
                if n == 1:
                    store(e, len(groups) - 1)
                    for i in range(2):
                        e.wait_ge(S(f"xn_out{i}"), 16 * max(xn_count[i].values()))

            def store(e, i):
                j0, nj = groups[i]
                g = g0 + i
                e.wait_ge(S("xn_done"), g + 1)
                e.dma_start(xnd.rearrange("(j p) d -> p j d", p=P)[:, j0:j0 + nj, :], xg[g % 2][:, 0:nj, :])\
                 .then_inc(S(f"xn_out{g % 2}"), 16)

            for g in range(g0, g0 + len(groups)) if n == 1 else ():
                xn_stores[g % 2] += 1
                xn_all[g % 2][g] = xn_stores[g % 2]
            xn_count = [dict(x) for x in xn_all]

            def sc(e):
                for i, (j0, nj) in enumerate(groups):
                    g = g0 + i
                    e.wait_ge(S(f"x_in{g % 2}"), 16 * (g // 2 + 1))
                    for j in range(nj):
                        act.step(e, e.activation(junk, xg[g % 2][:, j, :], ACT.Square, accum_out=ss[:, j0 + j:j0 + j + 1]))
                    e.activation(small[:, 0:1], ss[:, j0:j0 + 1], ACT.Copy).then_inc(S("norm_ss"), 1)
                    evac(e, i, 0)

            def evac(e, i, odd):
                j0, nj = groups[i]
                g = g0 + i
                s = 0 if j0 < JC else 1
                for k in range(odd, KD, 2):
                    e.wait_ge(S("norm_t"), KD * g + k + 1)
                    o, q = hT[:, k, j0 * P:(j0 + nj) * P], ps[:, k % 4, 0:nj * P]
                    sa, sh = AB[:, n, s, 0, k:k + 1], AB[:, n, s, 1, k:k + 1]
                    if odd:
                        e.tensor_scalar(o, q, sa, sh, ALU.mult, ALU.add).then_inc(S("norm_h1"), 1)
                    else:
                        e.activation(o, q, ACT.Identity, bias=sh, scale=sa).then_inc(S("norm_h0"), 1)

            def po(e):
                for i, (j0, nj) in enumerate(groups):
                    e.wait_ge(S("norm_ss"), g0 + i + 1)
                    rsqrt(e, rs[:, j0:j0 + nj], ss[:, j0:j0 + nj], EPS * D).then_inc(S("norm_rs"), 1)

            def ve(e):
                for i, (j0, nj) in enumerate(groups):
                    g = g0 + i
                    e.wait_ge(S("norm_rs"), g + 1)
                    for j in range(nj):
                        ins = e.tensor_scalar(xg[g % 2][:, j, :], xg[g % 2][:, j, :], rs[:, j0 + j:j0 + j + 1], float(D) ** 0.5,
                                              ALU.mult, ALU.mult)
                    ins.then_inc(S("xn_done"), 1)
                    evac(e, i, 1)

            def pe(e):
                for i, (j0, nj) in enumerate(groups):
                    g = g0 + i
                    e.wait_ge(S("xn_done"), g + 1)
                    for k in range(KD):
                        if i or k >= 4:
                            e.wait_ge(S(f"norm_h{k % 2}"), (KD * g + k - 4) // 2 + 1)
                        for j in range(nj):
                            mm = e.transpose(ps[:, k % 4, j * P:(j + 1) * P], xg[g % 2][:, j, k * P:(k + 1) * P], ident)
                        mm.then_inc(S("norm_t"), 1)

            stage(sync=sp, scalar=sc, gpsimd=po, vector=ve, tensor=pe)

        TM = V(10240, (NJ, TMW))
        QKR = V(24800, (4, T))
        HQ = V(29920, (2, T))
        ZF = V(32480, (4, T))

        def proj(l):
            hT = V(0, (KD, T))
            fpan = [V(37600 + n * 1024, (KD, P)) for n in range(2)]
            tpan = [ar[:, 39648 + n * 2112:39648 + (n + 1) * 2112] for n in range(2)]
            brow = V(43872, (TMW,))
            bcol = small[:, 0:len(FM_COLS)]
            toks = [(0, 512), (512, 512), (1024, 256)]
            nf, nt = len(FM_COLS), len(TM_COLS)
            tm_off = np.cumsum([0] + [b - x for x, b in TM_COLS]).tolist()

            def tview(n):
                w = TM_COLS[n][1] - TM_COLS[n][0]
                return tpan[n % 2][:, 0:KD * w].rearrange("p (k n) -> p k n", n=w)

            def sp(e):
                w = a["w_in"][l].rearrange("(k p) n -> p k n", p=P)
                for n, (x, y) in enumerate(TM_COLS):
                    e.dma_start(brow[0:1, tm_off[n]:tm_off[n + 1]], a["b_in"][l:l + 1, x:y]).then_inc(S("b_in"), 16)
                for n, x in enumerate(FM_COLS):
                    e.dma_start(bcol[:, n:n + 1], a["b_in"][l, x:x + P].rearrange("(p o) -> p o", o=1)).then_inc(S("b_in"), 16)
                for n in range(nf):
                    if n >= 2:
                        e.wait_ge(S("fm_mm"), 3 * (l * nf + n - 1))
                    e.dma_start(fpan[n % 2], w[:, :, FM_COLS[n]:FM_COLS[n] + P]).then_inc(S(f"fm_w{n % 2}"), 16)
                for n in range(nt):
                    if n >= 2:
                        e.wait_ge(S("tm_mm"), NJ * (l * nt + n - 1))
                    e.dma_start(tview(n), w[:, :, TM_COLS[n][0]:TM_COLS[n][1]]).then_inc(S(f"tm_w{n % 2}"), 16)

            def pe(e):
                q = 3 * nf * l
                for n in range(nf):
                    e.wait_ge(S(f"fm_w{n % 2}"), 16 * (l * nf // 2 + n // 2 + 1))
                    for i, (t0, tn) in enumerate(toks):
                        m = 3 * n + i
                        if m >= 4:
                            e.wait_ge(S("fm_out"), q + m - 3)
                        for k in range(KD):
                            mm = e.matmul(ps[:, m % 4, 0:tn], fpan[n % 2][:, k, :], hT[:, k, t0:t0 + tn], start=k == 0, stop=k == KD - 1)
                        mm.then_inc(S("fm_mm"), 1)
                e.wait_ge(S("b_in"), 16 * (nf + nt) * (l + 1))
                for n in range(nt):
                    e.wait_ge(S(f"tm_w{n % 2}"), 16 * (l * nt // 2 + n // 2 + 1))
                    w = TM_COLS[n][1] - TM_COLS[n][0]
                    for j in range(NJ):
                        m = NJ * n + j
                        if m >= 4:
                            e.wait_ge(S("tm_out"), NJ * nt * l + m - 3)
                        for k in range(KD):
                            e.matmul(ps[:, 4 + m % 4, 0:w], hT[:, k, j * P:(j + 1) * P], tview(n)[:, k, :], start=k == 0, stop=False)
                        mm = e.matmul(ps[:, 4 + m % 4, 0:w], ones[0:1, :], brow[0:1, tm_off[n]:tm_off[n] + w], start=False, stop=True)
                        mm.then_inc(S("tm_mm"), 1)

            def sc(e):
                e.wait_ge(S("b_in"), 16 * (nf + nt) * (l + 1))
                for n in range(nf):
                    dst = QKR[:, n, :] if n < 4 else HQ[:, n - 4, :] if n < 6 else ZF[:, n - 6, :]
                    for i, (t0, tn) in enumerate(toks):
                        m = 3 * n + i
                        e.wait_ge(S("fm_mm"), 3 * nf * l + m + 1)
                        e.activation(dst[:, t0:t0 + tn], ps[:, m % 4, 0:tn], ACT.Silu if n in (4, 5) else ACT.Identity,
                                     bias=bcol[:, n:n + 1]).then_inc(S("fm_out"), 1)

            def ve(e):
                for n in range(nt):
                    w = TM_COLS[n][1] - TM_COLS[n][0]
                    for j in range(NJ):
                        m = NJ * n + j
                        e.wait_ge(S("tm_mm"), NJ * nt * l + m + 1)
                        e.tensor_copy(TM[:, j, tm_off[n]:tm_off[n] + w], ps[:, 4 + m % 4, 0:w]).then_inc(S("tm_out"), 1)

            stage(sync=sp, tensor=pe, scalar=sc, vector=ve)

        def head_norm(l, name, Y, gate, func, gain):
            j0 = 0 if l == 0 else JC
            nj = NJ - j0
            G = gainr[:, :]
            SQ = V(0, (NJ, H * DH))
            y, sq, g = Y[:, j0:, :], SQ[:, 0:nj, :], gate[:, j0:, :]
            sums = ss[:, 0:nj * H]

            def sp(e):
                e.dma_start(G, gain[l].partition_broadcast(P)).then_inc(S("gain_in"), 16)

            def sc(e):
                e.activation(g, g, func).then_inc(S("gate_on"), 1)

            def ve(e, n):
                dve.step(e, e.tensor_tensor(sq, y, y, ALU.mult))
                e.tensor_reduce(sums.rearrange("p (j h) -> p j h", h=H), sq.rearrange("p j (h k) -> p j h k", h=H),
                                AX.X, ALU.add).then_inc(S("head_ss"), 1)
                e.wait_ge(S("head_rs"), n)
                r = rs[:, 0:nj * H].rearrange("p (j h o) -> p j h o", h=H, o=1).broadcast_to([P, nj, H, DH])
                yh = y.rearrange("p j (h k) -> p j h k", h=H)
                dve.step(e, e.tensor_tensor(yh, yh, r, ALU.mult))
                e.wait_ge(S("gain_in"), 16 * n)
                dve.step(e, e.scalar_tensor_tensor(y, y, float(DH) ** 0.5, G.unsqueeze(1).broadcast_to([P, nj, H * DH]),
                                                   ALU.mult, ALU.mult))
                e.wait_ge(S("gate_on"), n)
                dve.step(e, e.tensor_tensor(y, y, g, ALU.mult))

            def po(e, n):
                e.wait_ge(S("head_ss"), n)
                rsqrt(e, rs[:, 0:nj * H], sums, EPS * DH).then_inc(S("head_rs"), 1)

            return sp, sc, ve, po

        YM = TM[:, :, TM_V:TM_V + 256]

        def mlstm(l):
            QC = V(0, (4, T))
            KT = V(5120, (NJ, 256))
            VA = V(37600, (NJ, H, DH + 1))
            CS = V(40200, (NJ + 1, 4, 2 * (DH + 1)))
            W = V(7680, (2, H, P))
            PM = V(8704, (2, H, P))
            E2 = V(9728, (2, 2, P))
            gm = V(45920, (2, H, P))
            QP = V(46944, (2, 2, P))
            VW = [V(24800 + n * 520, (2, H, DH + 1)) for n in range(2)]
            Y1 = V(25840, (H, DH))
            sm = V(26112, (3600,))
            cw, cb = small[:, 16:28].rearrange("p (x w) -> p x w", w=3), small[:, 28:32]
            n_ = [0]

            def take(k, parts=P):
                v = sm[0:parts, n_[0]:n_[0] + k]
                n_[0] += k
                return v

            def four(v):
                return v.rearrange("p (d i h) -> p d i h", d=2, h=H)

            GI, GF, AX_, LF, BS, GG = (take(80) for _ in range(6))
            GR, CM, NM = (take(256, 40).rearrange("p (d t) -> p d t", d=2) for _ in range(3))
            BR, GX = take(80, 1), take(80, 1)
            MM = take(88, 1).rearrange("p (d i h) -> p d i h", d=2, h=H)
            RR = take(160, 1)
            MC = take(2, 40)
            MB = take(160)
            CR = take(40)
            NC = take(80)
            EM, WK, WC = take(80), take(80), take(80)
            WH = take(40).rearrange("p (d i a) -> p d i a", d=2, a=2)
            DN_, RD = take(8), take(8)
            assert n_[0] <= 3600
            jo = 0 if l == 0 else JC
            nout = NJ - jo
            steps = NJ - 1
            ob = (0, NJ)[l]
            hn = head_norm(l, "ml", YM, TM[:, :, TM_OG:TM_OG + 256], ACT.Sigmoid, a["ml_norm_g"])

            def sp(e):
                for w in range(3):
                    e.dma_start(cw[:, :, w:w + 1], a["ml_conv_w"][l, w].rearrange("(x p o) -> p x o", p=P, o=1)).then_inc(S("conv_in"), 16)
                e.dma_start(cb, a["ml_conv_b"][l].rearrange("(x p) -> p x", p=P)).then_inc(S("conv_in"), 16)
                hn[0](e)

            def po(e):
                e.wait_ge(S("ml_conv"), 4 * (l + 1))
                for d in range(2):
                    for i, j in enumerate(ORDER[d]):
                        for G, o in ((GI, 0), (GF, 4)):
                            at = TM_GATE + 8 * d + o
                            pool.did(e.tensor_copy(four(G)[:, d, i, :], TM[:, j, at:at + 4]))
                e.tensor_copy(VA[:, :, :, 0:DH], TM[:, :, TM_V:TM_V + 256].rearrange("p j (h k) -> p j h k", h=H)).then_inc(S("ml_gates"), 1)
                pool.step(e, e.memset(VA[:, :, :, DH:DH + 1], 1.0))
                pool.step(e, e.memset(CS[:, :, :, :], 0.0))
                for x in (2, 3):
                    e.wait_ge(S("ml_silu"), 4 * l + x + 1)
                    e.tensor_scalar(QC[:, x, :], QC[:, x, :], DH ** -0.5, None, ALU.mult).then_inc(S("ml_k"), 1)
                e.wait_ge(S("ml_wk"), l + 1)
                for i in range(steps):
                    if i >= 2:
                        e.wait_ge(S("ml_u"), l * steps + i - 1)
                    for d in range(2):
                        w = four(WK)[:, d, i, :].unsqueeze(2).broadcast_to([P, H, DH + 1])
                        e.tensor_tensor(VW[i % 2][:, d], VA[:, ORDER[d][i]], w, ALU.mult).then_inc(S("ml_vw"), 1)
                for m, j in enumerate(range(jo, NJ)):
                    if m:
                        e.wait_ge(S("ml_e"), ob + m)
                    for d in range(2):
                        i = ORDER[d].index(j)
                        g = four(GG)[:, d, i, :].unsqueeze(2).broadcast_to([P, H, P])
                        mk = K(f"mask{d}").unsqueeze(1).broadcast_to([P, H, P])
                        e.tensor_tensor(gm[:, d], g, mk, ALU.add).then_inc(S("ml_gm"), 1)
                hn[3](e, 2 * l + 1)

            def sc(e):
                for x in range(4):
                    e.wait_ge(S("ml_conv"), 4 * l + x + 1)
                    e.activation(QC[:, x, :], QC[:, x, :], ACT.Silu).then_inc(S("ml_silu"), 1)
                e.wait_ge(S("ml_ax"), l + 1)
                act.step(e, e.activation(AX_, AX_, ACT.Exp, scale=-1.0))
                e.activation(AX_, AX_, ACT.Ln, bias=1.0).then_inc(S("ml_ln"), 1)
                for j in range(NJ):
                    e.wait_ge(S("ml_kt"), NJ * l + j + 1)
                    e.activation(KT[:, j, :], ps[:, 6 + j % 2, 0:256], ACT.Copy).then_inc(S("ml_kto"), 1)
                e.wait_ge(S("ml_small"), l + 1)
                act.did(e.activation(EM, EM, ACT.Exp))
                act.did(e.activation(WC, WC, ACT.Exp))
                e.activation(WK, WK, ACT.Exp).then_inc(S("ml_wk"), 1)
                for m in range(nout):
                    e.wait_ge(S("ml_e"), ob + m + 1)
                    e.activation(W[:, :, :, :], W[:, :, :, :], ACT.Exp).then_inc(S("ml_w"), 1)
                    e.activation(E2[:, :, :, :], E2[:, :, :, :], ACT.Exp).then_inc(S("ml_w"), 1)
                hn[1](e)

            def ve(e):
                e.wait_ge(S("conv_in"), 64 * (l + 1))
                for x in range(4):
                    raw, y = QKR[:, x, :], QC[:, x, :]
                    dve.step(e, e.tensor_scalar(y, raw, cw[:, x, 1:2], cb[:, x:x + 1], ALU.mult, ALU.add))
                    for s0, s1 in ((0, NCTX), (NCTX, T)):
                        dve.did(e.scalar_tensor_tensor(y[:, s0 + 1:s1], raw[:, s0:s1 - 1], cw[:, x, 0:1], y[:, s0 + 1:s1], ALU.mult, ALU.add))
                    dve.settle(e)
                    for s0, s1 in ((0, NCTX), (NCTX, T)):
                        ins = e.scalar_tensor_tensor(y[:, s0:s1 - 1], raw[:, s0 + 1:s1], cw[:, x, 2:3], y[:, s0:s1 - 1], ALU.mult, ALU.add)
                        if s0:
                            ins.then_inc(S("ml_conv"), 1)
                        else:
                            dve.did(ins)
                e.wait_ge(S("ml_gates"), l + 1)
                e.wait_ge(S("ml_conv"), 4 * (l + 1))
                e.scalar_tensor_tensor(AX_, GF, -1.0, GF, ALU.mult, ALU.max).then_inc(S("ml_ax"), 1)
                e.wait_ge(S("ml_ln"), l + 1)
                e.scalar_tensor_tensor(LF, GF, 0.0, AX_, ALU.min, ALU.subtract).then_inc(S("ml_lf"), 1)
                e.wait_ge(S("ml_p"), 5 * l + 1)
                dve.did(e.tensor_copy(BS, ps[:, 0, 0:80]))
                dve.did(e.tensor_copy(BR, ps[0:1, 0, 128:208]))
                e.tensor_tensor(GG, GI, ps[:, 0, 0:80], ALU.subtract).then_inc(S("ml_g"), 1)
                e.wait_ge(S("ml_p"), 5 * l + 2)
                dve.step(e, e.tensor_copy(GR, ps[0:40, 1, 0:256].rearrange("p (d t) -> p d t", d=2)))
                for d in range(2):
                    ins = e.tensor_tensor_scan(CM[:, d, :], GR[:, d, :], GR[:, d, :], NEG, ALU.max, ALU.max)
                    ins.then_inc(S("ml_cm"), 1)
                dve.step(e, e.memset(MM[:, :, 0, :], 0.0))
                e.wait_ge(S("ml_p"), 5 * l + 3)
                dve.step(e, e.tensor_copy(GX, ps[0:1, 2, 0:80]))
                for d in range(2):
                    for h in range(H):
                        dve.did(e.tensor_tensor_scan(MM[:, d, 1:NJ + 1, h], four(GX)[:, d, :, h], four(BR)[:, d, :, h], 0.0, ALU.max, ALU.add))
                dve.settle(e)
                dve.step(e, e.tensor_copy(four(RR[:, 0:80]), MM[:, :, 0:NJ, :]))
                e.tensor_tensor(RR[:, 80:160], RR[:, 0:80], GX, ALU.max).then_inc(S("ml_rr"), 1)
                e.wait_ge(S("ml_p"), 5 * l + 4)
                dve.did(e.tensor_copy(MB, ps[:, 3, 0:160]))
                dve.did(e.tensor_copy(MC, ps[0:40, 3, 256:258]))
                dve.settle(e)
                for d in range(2):
                    e.tensor_scalar(NM[:, d, :], CM[:, d, :], MC[:, d:d + 1], -1.0, ALU.max, ALU.mult).then_inc(S("ml_nm"), 1)
                dve.did(e.tensor_tensor(WK, GG, MB[:, 80:160], ALU.subtract))
                dve.did(e.tensor_tensor(WC, MB[:, 0:80], MB[:, 80:160], ALU.subtract))
                e.wait_ge(S("ml_p"), 5 * l + 5)
                dve.did(e.tensor_copy(NC[:, 0:40], ps[:, 4, 0:40]))
                e.tensor_copy(CR, ps[:, 4, 64:104]).then_inc(S("ml_cr"), 1)
                e.wait_ge(S("ml_p2"), l + 1)
                dve.did(e.tensor_copy(NM[:, 1, :], ps[0:40, 5, 0:P]))
                dve.did(e.tensor_copy(NC[:, 40:80], ps[:, 5, 128:168]))
                dve.settle(e)
                e.tensor_tensor(EM, NC, BS, ALU.subtract).then_inc(S("ml_small"), 1)
                e.wait_ge(S("ml_wk"), l + 1)
                for b in range(2):
                    r = slice(64 * b, 64 * b + 64)
                    dve.did(e.tensor_copy(WH[r], WC.rearrange("p (d i a b) -> p d i a b", d=2, a=2, b=2)[r, :, :, :, b]))
                dve.settle(e)
                for i in range(steps):
                    w = WH[:, :, i, :].unsqueeze(3).broadcast_to([P, 2, 2, 2 * (DH + 1)])
                    dve.step(e, e.tensor_tensor(*(CS[:, k, :, :].rearrange("p (d a) q -> p d a q", d=2) for k in (i + 1, i)), w, ALU.mult))
                    e.wait_ge(S("ml_u"), l * steps + i + 1)
                    for d in range(2):
                        for b in range(2):
                            r = slice(64 * b, 64 * b + 64)
                            o = CS[r, i + 1, 2 * d:2 * d + 2, 65 * b:65 * b + 65]
                            u = ps[r, 2 * (i % 2) + d, 0:260].rearrange("p (a q) -> p a q", a=2)[:, :, 65 * b:65 * b + 65]
                            e.tensor_tensor(o, o, u, ALU.add).then_inc(S("ml_cs"), 1)
                    e.wait_ge(S("ml_cs"), 4 * (l * steps + i + 1))
                def finish(m, j):
                    for d in range(2):
                        e.wait_ge(S("ml_o"), 2 * (ob + m) + d + 1)
                        o = ps[:, 4 + d, 0:260].rearrange("p (h q) -> p h q", h=H)
                        dn = DN_[:, 4 * d:4 * d + 4]
                        dve.step(e, e.scalar_tensor_tensor(dn, o[:, :, DH], -1.0, four(EM)[:, d, ORDER[d].index(j), :], ALU.mult, ALU.max))
                        dve.did(e.tensor_tensor(dn, o[:, :, DH], dn, ALU.max))
                    dve.settle(e)
                    dve.step(e, e.reciprocal(RD, DN_))
                    for d in range(2):
                        o = ps[:, 4 + d, 0:260].rearrange("p (h q) -> p h q", h=H)
                        y = YM[:, j, :].rearrange("p (h k) -> p h k", h=H) if d == 0 else Y1
                        r = RD[:, 4 * d:4 * d + 4].unsqueeze(2).broadcast_to([P, H, DH])
                        ins = e.tensor_tensor(y, o[:, :, 0:DH], r, ALU.mult)
                        ins.then_inc(S("ml_od"), 1)
                    e.wait_ge(S("ml_od"), 2 * (ob + m + 1))
                    y = YM[:, j, :].rearrange("p (h k) -> p h k", h=H)
                    dve.step(e, e.tensor_tensor(y, y, Y1, ALU.add))

                for m, j in enumerate(range(jo, NJ)):
                    e.wait_ge(S("ml_gm"), 2 * (ob + m + 1))
                    e.wait_ge(S("ml_nmb"), ob + m + 1)
                    if m:
                        e.wait_ge(S("ml_pm"), 4 * (ob + m))
                    for d in range(2):
                        n4 = ps[:, 2 + d, :].rearrange("p (h t) -> p h t", h=H)
                        dve.did(e.tensor_tensor(W[:, d], gm[:, d], n4, ALU.add))
                        for b in range(2):
                            r = slice(64 * b, 64 * b + 64)
                            mp = MB[:, 0:80].rearrange("p (d i a b) -> p d i a b", d=2, a=2, b=2)[r, d, ORDER[d].index(j), :, b]
                            ins = e.tensor_tensor(E2[r, d], n4.rearrange("p (a b) t -> p a b t", b=2)[r, :, b, :],
                                                  mp.unsqueeze(2).broadcast_to([64, 2, P]), ALU.add)
                            if (d, b) == (1, 1):
                                ins.then_inc(S("ml_e"), 1)
                            else:
                                dve.did(ins)
                    if m:
                        finish(m - 1, j - 1)
                    e.wait_ge(S("ml_sco"), ob + m + 1)
                    e.wait_ge(S("ml_w"), 2 * (ob + m + 1))
                    for d in range(2):
                        pm, w = (X[:, d].rearrange("p (a b) t -> p b a t", b=2) for X in (PM, W))
                        sco = ps[:, 6 * (m % 2):6 * (m % 2) + 2, 0:256].rearrange("p b (a t) -> p b a t", a=2)
                        e.tensor_tensor(pm, w, sco, ALU.mult).then_inc(S("ml_pm"), 1)
                    for d in range(2):
                        e.tensor_tensor(QP[:, d], E2[:, d], QC[:, 0:2, j * P:(j + 1) * P], ALU.mult).then_inc(S("ml_pm"), 1)
                finish(nout - 1, NJ - 1)
                hn[2](e, 2 * l + 1)

            def pe(e):
                for j in range(NJ):
                    for x in range(2):
                        if j == 0:
                            e.wait_ge(S("ml_k"), 2 * l + x + 1)
                        elif j >= 2:
                            e.wait_ge(S("ml_kto"), NJ * l + j - 1)
                        mm = e.transpose(ps[:, 6 + j % 2, x * P:(x + 1) * P], QC[:, 2 + x, j * P:(j + 1) * P], ident)
                    mm.then_inc(S("ml_kt"), 1)
                e.wait_ge(S("ml_lf"), l + 1)
                for d in range(2):
                    e.matmul(ps[:, 0, 40 * d:40 * d + 40], K("ge" if d else "le"), LF[:, 40 * d:40 * d + 40], start=True, stop=True)
                e.matmul(ps[0:1, 0, 128:208], ones[:, 0:1], LF, start=True, stop=True).then_inc(S("ml_p"), 1)
                e.wait_ge(S("ml_g"), l + 1)
                for d in range(2):
                    mm = e.matmul(ps[0:40, 1, P * d:P * d + P], GG[:, 40 * d:40 * d + 40], K("flip") if d else ident, start=True, stop=True)
                mm.then_inc(S("ml_p"), 1)
                e.wait_ge(S("ml_cm"), 2 * l + 2)
                for d in range(2):
                    mm = e.matmul(ps[0:1, 2, 40 * d:40 * d + 40], CM[:, d, P - 1:P], ident[0:40, 0:40], start=True, stop=True)
                mm.then_inc(S("ml_p"), 1)
                e.wait_ge(S("ml_rr"), l + 1)
                e.matmul(ps[:, 3, 0:160], ones[0:1, :], RR, start=True, stop=True)
                for d in range(2):
                    mm = e.matmul(ps[0:40, 3, 256 + d:257 + d], RR[:, 40 * d:40 * d + 40], ones[0:1, 0:1], start=True, stop=True)
                mm.then_inc(S("ml_p"), 1)
                e.wait_ge(S("ml_nm"), 2 * l + 2)
                for d in range(2):
                    mm = e.transpose(ps[:, 4, 64 * d:64 * d + 40], NM[:, d, :], ident[0:40, 0:40])
                mm.then_inc(S("ml_p"), 1)
                e.wait_ge(S("ml_cr"), l + 1)
                e.matmul(ps[0:40, 5, 0:P], CR, K("flip"), start=True, stop=True)
                e.matmul(ps[:, 5, 128:168], K("flip"), CR, start=True, stop=True).then_inc(S("ml_p2"), 1)
                e.wait_ge(S("ml_kto"), NJ * (l + 1))
                for i in range(steps):
                    e.wait_ge(S("ml_vw"), 2 * (l * steps + i + 1))
                    if i >= 2:
                        e.wait_ge(S("ml_cs"), 4 * (l * steps + i - 1))
                    elif i == 0:
                        e.wait_ge(S("ml_small"), l + 1)
                    for d in range(2):
                        for x in range(2):
                            mm = e.matmul(ps[:, 2 * (i % 2) + d, 130 * x:130 * x + 130], KT[:, ORDER[d][i], x * P:(x + 1) * P],
                                          VW[i % 2][:, d, 2 * x:2 * x + 2, :], start=True, stop=True)
                    mm.then_inc(S("ml_u"), 1)
                e.wait_ge(S("ml_cs"), 4 * steps * (l + 1))

                def values(m, j):
                    for d in range(2):
                        i = ORDER[d].index(j)
                        if m:
                            e.wait_ge(S("ml_od"), 2 * (ob + m))
                        e.wait_ge(S("ml_pm"), 4 * (ob + m + 1))
                        for h in range(H):
                            o = ps[:, 4 + d, 65 * h:65 * h + 65]
                            e.matmul(o, PM[:, d, h, :], VA[:, j, h, :], start=h == 0, stop=False, skip_group_check=True)
                        for x in range(2):
                            mm = e.matmul(ps[:, 4 + d, 130 * x:130 * x + 130], QP[:, d, x, :], CS[:, i, 2 * d + x, :],
                                          start=False, stop=x == 1, skip_group_check=True)
                        mm.then_inc(S("ml_o"), 1)

                for m, j in enumerate(range(jo, NJ)):
                    if m:
                        e.wait_ge(S("ml_e"), ob + m)
                    for d in range(2):
                        i = ORDER[d].index(j)
                        for h in range(H):
                            q = 4 * i + h
                            mm = e.matmul(ps[:, 2 + d, h * P:(h + 1) * P], ident[0:40, q:q + 1].broadcast_to([40, P]), NM[:, d, :],
                                          start=True, stop=True)
                    mm.then_inc(S("ml_nmb"), 1)
                    if m >= 2:
                        e.wait_ge(S("ml_pm"), 4 * (ob + m - 1))
                    for h in range(H):
                        r = slice(64 * (h % 2), 64 * (h % 2) + 64)
                        mm = e.matmul(ps[:, 6 * (m % 2) + h % 2, (h // 2) * P:(h // 2 + 1) * P], QC[r, 2 + h // 2, j * P:(j + 1) * P], QC[r, h // 2, j * P:(j + 1) * P],
                                      start=True, stop=True)
                    mm.then_inc(S("ml_sco"), 1)
                    if m:
                        values(m - 1, j - 1)
                values(nout - 1, NJ - 1)

            stage(sync=sp, gpsimd=po, scalar=sc, vector=ve, tensor=pe)

        YH = V(32480, (NJ, 256))

        def hgrn(l):
            FH = V(0, (4, T))
            SH = V(5120, (4, T))
            Z = V(37600, (4, NJ, P + 1))
            SS = V(42760, (NJ, 4, P))
            L = [V(24800 + n * 1280, (T,)) for n in range(2)]
            LF = [V(27360 + n * 1280, (T,)) for n in range(2)]
            A = [V(24800 + n * 1024, (2, 4, P)) for n in range(2)]
            E = [V(26848 + n * 512, (4, P)) for n in range(2)]
            X = [V(27872 + n * 512, (4, P)) for n in range(2)]
            KP, KPT = X, [V(24800 + n * 1024, (4, P)) for n in range(2)]
            QP = [V(35040 + n * 512, (4, P)) for n in range(2)]
            AR = [V(36064 + n * 512, (4, P)) for n in range(2)]
            LG = small[:, 64:72].rearrange("p (l x) -> p l x", l=2)
            la, lc, lx, lm = (small[:, 72 + 4 * n:76 + 4 * n] for n in range(4))
            eT = small[:, 96:96 + 40].rearrange("p (x j) -> p x j", x=4)
            jo = 0 if l == 0 else JC
            nout, steps, NL = NJ - jo, NJ - 1, len(LEVELS)
            ob = (0, NJ)[l]
            hn = head_norm(l, "hg", YH, TM[:, :, TM_HG:TM_HG + 256], ACT.Silu, a["hg_norm_g"])

            def sp(e):
                for n in range(2):
                    for d in range(2):
                        e.dma_start(LG[:, n, 2 * d:2 * d + 2], a["hg_lb_logits"][n, d].rearrange("(a p) -> p a", p=P)).then_inc(S("lb_in"), 16)
                hn[0](e)

            def halves(v, m):
                w = v.rearrange("p x (b s m) -> p x b s m", s=2, m=m)
                return w[:, :, :, 0, :], w[:, :, :, 1, :]

            def po(e):
                pool.did(e.tensor_copy(FH[:, 2:4, :], HQ[:, :, :]))
                pool.did(e.tensor_copy(SH[:, 0:2, :], HQ[:, :, :]))
                pool.did(e.memset(SS[:, :, :, :], 0.0))
                e.memset(Z[:, :, :, 0:1], 0.0).then_inc(S("hg_zero"), 1)
                pool.settle(e)
                e.wait_ge(S("hg_z"), l + 1)
                for i in range(steps):
                    if i >= 2:
                        e.wait_ge(S("hg_kp"), 2 * (steps * l + i - 1))
                    j = ORDER[0][i]
                    z = Z[:, 0:2, j, :]
                    e.tensor_tensor(E[i % 2][:, 0:2, :], z[:, :, P:P + 1].broadcast_to([P, 2, P]), z[:, :, 1:P + 1], ALU.subtract).then_inc(S("hg_se"), 1)
                e.wait_ge(S("hg_ss"), 2 * steps * (l + 1))
                for m, j in enumerate(range(jo, NJ)):
                    b = m % 2
                    if m >= 2:
                        e.wait_ge(S("hg_o"), ob + m - 1)
                        pool.settle(e)
                    pool.did(e.tensor_copy(AR[b][:, 0:2, :], Z[:, 0:2, j, 1:P + 1]))
                    pool.did(e.tensor_copy(AR[b][:, 2:4, :], Z[:, 2:4, j, 0:P]))
                    z = Z[:, 2:4, j, :]
                    e.tensor_tensor(QP[b][:, 2:4, :], z[:, :, P:P + 1].broadcast_to([P, 2, P]), z[:, :, 0:P], ALU.subtract).then_inc(S("hg_qe"), 1)
                    pool.settle(e)
                    ar = AR[b]
                    for n, w in enumerate(LEVELS):
                        g = NL * (ob + m) + n
                        if NL * m + n >= 2:
                            e.wait_ge(S("hg_x"), g - 1)
                        r = Z[:, :, j, w:P:2 * w].unsqueeze(3).broadcast_to([P, 4, P // (2 * w), w])
                        (e0, e1), (a0, a1) = halves(E[g % 2], w), halves(ar, w)
                        pool.did(e.tensor_tensor(e0, r, a0, ALU.subtract))
                        e.tensor_tensor(e1, a1, r, ALU.subtract).then_inc(S("hg_e"), 1)
                hn[3](e, 2 * l + 2)

            def sc(e):
                if l:
                    e.wait_ge(S("lb_ax"), 1)
                    act.step(e, e.activation(lx, lx, ACT.Exp, scale=-1.0))
                    e.activation(lx, lx, ACT.Ln, bias=1.0).then_inc(S("lb_ln"), 1)
                for x in range(4):
                    for half in range(l + 1):
                        e.wait_ge(S("hg_ax"), (0, 4)[l] + (l + 1) * x + half + 1)
                        act.step(e, e.activation(L[x % 2], L[x % 2], ACT.Exp, scale=-1.0))
                        e.activation(L[x % 2], L[x % 2], ACT.Ln, bias=1.0).then_inc(S("hg_ln"), 1)
                    e.wait_ge(S("hg_nk"), 4 * l + x + 1)
                    k = (FH if x < 2 else SH)[:, x, :]
                    if l:
                        e.wait_ge(S("lb_on"), 1)
                    e.activation(k, ZF[:, x, :], ACT.Exp, scale=-1.0, bias=lc[:, x:x + 1] if l else 0.0).then_inc(S("hg_k"), 1)
                e.wait_ge(S("hg_z"), l + 1)
                act.step(e, e.activation(eT, Z[:, :, :, P], ACT.Exp))
                for i in range(steps):
                    if i >= 2:
                        e.wait_ge(S("hg_kp"), 2 * (steps * l + i - 1))
                    e.wait_ge(S("hg_se"), steps * l + i + 1)
                    en = E[i % 2]
                    act.did(e.activation(en[:, 0:2, :], en[:, 0:2, :], ACT.Exp))
                    e.activation(en[:, 2:4, :], Z[:, 2:4, ORDER[1][i], 0:P], ACT.Exp).then_inc(S("hg_sx"), 1)
                    e.wait_ge(S("hg_kt"), steps * l + i + 1)
                    if i >= 2:
                        e.wait_ge(S("hg_u"), steps * l + i - 1)
                    e.activation(KPT[i % 2][:, :, :], ps[:, i % 2, :].rearrange("p (x t) -> p x t", x=4), ACT.Copy).then_inc(S("hg_kto"), 1)
                e.wait_ge(S("hg_ss"), 2 * steps * (l + 1))
                for m, j in enumerate(range(jo, NJ)):
                    b = m % 2
                    e.wait_ge(S("hg_qe"), ob + m + 1)
                    act.did(e.activation(QP[b][:, 2:4, :], QP[b][:, 2:4, :], ACT.Exp))
                    e.activation(QP[b][:, 0:2, :], AR[b][:, 0:2, :], ACT.Exp).then_inc(S("hg_qx"), 1)
                    for n in range(NL):
                        g = NL * (ob + m) + n
                        e.wait_ge(S("hg_e"), g + 1)
                        if NL * m + n >= 2:
                            gg = (NL + 1) * (ob + (NL * m + n - 2) // NL) + (n - 2) % NL + 1
                            e.wait_ge(S("hg_g"), gg + 1)
                        e.activation(X[g % 2][:, :, :], E[g % 2][:, :, :], ACT.Exp).then_inc(S("hg_x"), 1)
                    if m:
                        out_copy(e, m - 1, j - 1)
                out_copy(e, nout - 1, NJ - 1)
                hn[1](e)

            def out_copy(e, m, j):
                e.wait_ge(S("hg_o"), ob + m + 1)
                e.activation(YH[:, j, :], ps[:, 4 + m % 2, 0:256], ACT.Copy).then_inc(S("hg_y"), 1)

            def ve(e):
                if l:
                    e.wait_ge(S("lb_in"), 64 * 2)
                    dve.step(e, e.tensor_tensor(lm, LG[:, 1, :], LG[:, 0, :], ALU.subtract))
                    e.scalar_tensor_tensor(lx, lm, -1.0, lm, ALU.mult, ALU.max).then_inc(S("lb_ax"), 1)
                    e.wait_ge(S("lb_ln"), 1)
                    dve.did(e.scalar_tensor_tensor(la, lm, 0.0, lx, ALU.min, ALU.subtract))
                    dve.step(e, e.tensor_scalar(lc, lm, -1.0, 0.0, ALU.mult, ALU.min))
                    dve.step(e, e.tensor_tensor(lc, lc, lx, ALU.subtract))
                    e.tensor_tensor(lm, lc, la, ALU.subtract).then_inc(S("lb_on"), 1)
                    e.wait_ge(S("lb_on"), 1)
                for x in range(4):
                    z, ln, lf = ZF[:, x, :], L[x % 2], LF[x % 2]
                    nln = (0, 4)[l] + (l + 1) * x
                    e.scalar_tensor_tensor(ln, z, -1.0, z, ALU.mult, ALU.max).then_inc(S("hg_ax"), 1)
                    e.wait_ge(S("hg_ln"), nln + 1)
                    dve.step(e, e.scalar_tensor_tensor(lf, z, 0.0, ln, ALU.min, ALU.subtract))
                    e.scalar_tensor_tensor(z, z, 0.0, ln, ALU.max, ALU.add).then_inc(S("hg_nk"), 1)
                    if l:
                        e.wait_ge(S("hg_nk"), 4 * l + x + 1)
                        dve.step(e, e.tensor_scalar(ln, lf, lm[:, x:x + 1], None, ALU.add))
                        e.scalar_tensor_tensor(ln, ln, -1.0, ln, ALU.mult, ALU.max).then_inc(S("hg_ax"), 1)
                        dve.step(e, e.tensor_scalar(lf, lf, lc[:, x:x + 1], la[:, x:x + 1], ALU.add, ALU.max))
                        e.wait_ge(S("hg_ln"), nln + 2)
                        dve.step(e, e.tensor_tensor(lf, lf, ln, ALU.add))
                    if x == 0:
                        e.wait_ge(S("hg_zero"), l + 1)
                    for j in range(NJ):
                        dve.did(e.tensor_tensor_scan(Z[:, x, j, 1:P + 1], ones, lf[:, j * P:(j + 1) * P], 0.0, ALU.mult, ALU.add))
                    dve.settle(e)
                e.engine_nop().then_inc(S("hg_z"), 1)
                e.wait_ge(S("hg_k"), 4 * (l + 1))
                for i in range(steps):
                    e.wait_ge(S("hg_sx"), steps * l + i + 1)
                    if i >= 2:
                        e.wait_ge(S("hg_kt"), steps * l + i - 1)
                    for d, F_ in enumerate((FH, SH)):
                        j = ORDER[d][i]
                        r = slice(2 * d, 2 * d + 2)
                        e.tensor_tensor(KP[i % 2][:, r, :], E[i % 2][:, r, :], F_[:, r, j * P:(j + 1) * P], ALU.mult).then_inc(S("hg_kp"), 1)
                    for d in range(2):
                        r = slice(2 * d, 2 * d + 2)
                        w = eT[:, r, ORDER[d][i]].unsqueeze(2).broadcast_to([P, 2, P])
                        dve.did(e.tensor_tensor(SS[:, i + 1, r, :], SS[:, i, r, :], w, ALU.mult))
                    dve.settle(e)
                    e.wait_ge(S("hg_u"), steps * l + i + 1)
                    for b in range(2):
                        r, q = slice(64 * b, 64 * b + 64), slice(64 * b, 64 * b + 64)
                        o = SS[r, i + 1, :, q]
                        e.tensor_tensor(o, o, ps[r, 2 + i % 2, :].rearrange("p (x v) -> p x v", x=4)[:, :, q], ALU.add).then_inc(S("hg_ss"), 1)
                    e.wait_ge(S("hg_ss"), 2 * (steps * l + i + 1))

                def take(m, n):
                    g = (NL + 1) * (ob + m) + n
                    e.wait_ge(S("hg_g"), g + 1)
                    Am, bank = A[m % 2], 2 * (g % 2)
                    if n == 0:
                        if m >= 2:
                            e.wait_ge(S("hg_o"), ob + m - 1)
                        src = ps[:, bank:bank + 2, :].rearrange("p b (x t) -> p b x t", x=4)
                        for b in range(2):
                            ins = e.tensor_tensor(Am[:, b], src[:, b], ident.unsqueeze(1).broadcast_to([P, 4, P]), ALU.mult)
                            ins.then_inc(S("hg_c"), 1)
                    else:
                        mask = K(f"lvl{LEVELS[n - 1]}").bitcast(U32).rearrange("p (d t) -> p d t", d=2).unsqueeze(2).broadcast_to([P, 2, 2, P])
                        e.wait_ge(S("hg_c"), 2 * g)
                        for b in range(2):
                            e.copy_predicated(Am[:, b].rearrange("p (d a) t -> p d a t", d=2), mask,
                                              ps[:, bank + b, :].rearrange("p (d a t) -> p d a t", d=2, a=2)).then_inc(S("hg_c"), 1)

                for m, j in enumerate(range(jo, NJ)):
                    tok = slice(j * P, (j + 1) * P)
                    e.wait_ge(S("hg_qx"), ob + m + 1)
                    qp = QP[m % 2].rearrange("p (d a) t -> p d a t", d=2)
                    e.tensor_tensor(qp, qp, FH[:, 2:4, tok].unsqueeze(1).broadcast_to([P, 2, 2, P]), ALU.mult).then_inc(S("hg_qp"), 1)
                    for n, w in enumerate(LEVELS):
                        g = NL * (ob + m) + n
                        e.wait_ge(S("hg_x"), g + 1)
                        (x0, x1), (f0, _), (_, s1) = halves(X[g % 2], w), halves(FH[:, :, tok], w), halves(SH[:, :, tok], w)
                        dve.did(e.tensor_tensor(x0, x0, f0, ALU.mult))
                        e.tensor_tensor(x1, x1, s1, ALU.mult).then_inc(S("hg_xm"), 1)
                        take(m, n)
                    take(m, NL)
                e.wait_ge(S("hg_y"), ob + nout)
                hn[2](e, 2 * l + 2)

            def pe(e):
                for i in range(steps):
                    e.wait_ge(S("hg_kp"), 2 * (steps * l + i + 1))
                    if i >= 2:
                        e.wait_ge(S("hg_kto"), steps * l + i - 1)
                    for x in range(4):
                        mm = e.transpose(ps[:, i % 2, x * P:(x + 1) * P], KP[i % 2][:, x, :], ident)
                    mm.then_inc(S("hg_kt"), 1)
                    e.wait_ge(S("hg_kto"), steps * l + i + 1)
                    if i >= 2:
                        e.wait_ge(S("hg_ss"), 2 * (steps * l + i - 1))
                    for x in range(4):
                        v = TM[:, ORDER[x // 2][i], TM_HI + P * (x % 2):TM_HI + P * (x % 2) + P]
                        mm = e.matmul(ps[:, 2 + i % 2, x * P:(x + 1) * P], KPT[i % 2][:, x, :], v, start=True, stop=True)
                    mm.then_inc(S("hg_u"), 1)
                e.wait_ge(S("hg_ss"), 2 * steps * (l + 1))

                def gram(m, n, lhs, rhs):
                    g = (NL + 1) * (ob + m) + n
                    if (NL + 1) * m + n >= 2:
                        e.wait_ge(S("hg_c"), 2 * (g - 1))
                    for x in range(4):
                        for b in range(2):
                            r = slice(64 * b, 64 * b + 64)
                            mm = e.matmul(ps[:, 2 * (g % 2) + b, x * P:(x + 1) * P], lhs(x)[r], rhs(x)[r], start=True, stop=True)
                    mm.then_inc(S("hg_g"), 1)

                def values(m, j):
                    if m >= 2:
                        e.wait_ge(S("hg_y"), ob + m - 1)
                    e.wait_ge(S("hg_qp"), ob + m + 1)
                    e.wait_ge(S("hg_c"), 2 * (NL + 1) * (ob + m + 1))
                    o = ps[:, 4 + m % 2, :]
                    for h in range(H):
                        for d in range(2):
                            v = TM[:, j, TM_HI + 64 * h:TM_HI + 64 * h + 64]
                            e.matmul(o[:, 64 * h:64 * h + 64], A[m % 2][:, h % 2, 2 * d + h // 2, :], v, start=h == 0 and d == 0, stop=False,
                                     skip_group_check=True)
                    for x in range(4):
                        i = ORDER[x // 2].index(j)
                        mm = e.matmul(o[:, P * (x % 2):P * (x % 2) + P], QP[m % 2][:, x, :], SS[:, i, x, :], start=False, stop=x == 3,
                                      skip_group_check=True)
                    mm.then_inc(S("hg_o"), 1)

                for m, j in enumerate(range(jo, NJ)):
                    tok = slice(j * P, (j + 1) * P)
                    gram(m, 0, lambda x: (FH if x < 2 else SH)[:, x, tok], lambda x: FH[:, 2 + x % 2, tok])
                    if m:
                        values(m - 1, j - 1)
                    for n in range(NL):
                        g = NL * (ob + m) + n
                        e.wait_ge(S("hg_xm"), g + 1)
                        gram(m, n + 1, lambda x: X[g % 2][:, x, :], lambda x: X[g % 2][:, x, :])
                values(nout - 1, NJ - 1)

            stage(sync=sp, gpsimd=po, scalar=sc, vector=ve, tensor=pe)

        def mla(l):
            QT = V(0, (MH, T))
            KT = V(37600, (MH, T))
            VV = V(24800, (NJ, MH, DV))
            wq = V(35040, (2, MH * DQK))
            wkv = V(36576, (MH * (DN + DV),))
            CT = V(29920, (3, P))
            XS = {"q": V(30304, (MH, DQK)), "k": V(31072, (MH, DQK))}
            SQ = V(47840, (MH, DQK))
            PB = [V(29920 + n * 1280, (T,)) for n in range(2)]
            PT = [V(35040 + n * 1280, (NJ, P)) for n in range(2)]
            gq, gkv = small[:, 0:2], small[:, 2:3]
            gains = {"q": gainr[:, 0:DQK], "k": gainr[:, DQK:2 * DQK]}
            sx, rx = small[:, 8:16], small[:, 16:24]
            mx, nm, sm, rc = (small[:, 24 + 2 * n:26 + 2 * n] for n in range(4))
            cs, cr = ss[:, 0:2 * NJ].rearrange("p (c j) -> p c j", c=2), rs[:, 0:2 * NJ].rearrange("p (c j) -> p c j", c=2)
            parts = ((TM_CQ, 256), (TM_CKV, 128))
            jo = 0 if l == 0 else JC
            items = [(j, w) for j in range(NJ) for w in "qk" if w == "k" or j >= jo]
            ib = (0, 2 * NJ)[l]
            at = [(j, h) for j in range(jo, NJ) for h in range(MH)]
            ab = (0, NJ * MH)[l]

            def sp(e):
                e.dma_start(wq, a["mla_w_uq"][l].rearrange("(k p) n -> p k n", p=P)).then_inc(S("la_in"), 16)
                e.dma_start(wkv, a["mla_w_ukv"][l]).then_inc(S("la_in"), 16)
                e.dma_start(gq, a["mla_q_norm_g"][l].rearrange("(k p) -> p k", p=P)).then_inc(S("la_in"), 16)
                e.dma_start(gkv, a["mla_kv_norm_g"][l].rearrange("(p o) -> p o", o=1)).then_inc(S("la_in"), 16)
                for w, g in (("q", "mla_q_qk_g"), ("k", "mla_k_qk_g")):
                    e.dma_start(gains[w], a[g][l].partition_broadcast(P)).then_inc(S("la_in"), 16)

            def sc(e):
                for c_, (o, w) in enumerate(parts):
                    for j in range(NJ):
                        act.step(e, e.activation(SQ.rearrange("p a b -> p (a b)")[:, 0:w], TM[:, j, o:o + w], ACT.Square,
                                                 accum_out=cs[:, c_, j:j + 1]))
                e.activation(small[:, 3:4], cs[:, 0, 0:1], ACT.Copy).then_inc(S("la_ss"), 1)
                for j in range(NJ):
                    n = NJ * l + j
                    e.wait_ge(S("la_t"), n + 1)
                    if j:
                        e.wait_ge(S("la_mm"), n)
                    e.activation(CT, ps[:, 0, 0:384].rearrange("p (k t) -> p k t", k=3), ACT.Copy).then_inc(S("la_ct"), 1)
                    if j:
                        evac(e, [x for x in items if x[0] == j - 1])
                    e.wait_ge(S("la_mm"), n + 1)
                    if j:
                        e.wait_ge(S("la_xt"), ib + items.index((j - 1, "k")) + 1)
                    for b in range(2):
                        if j >= jo:
                            act.did(e.activation(XS["q"][:, 4 * b:4 * b + 4, :], ps[:, 1 + b, 0:384].rearrange("p (h q) -> p h q", h=4), ACT.Copy))
                        ins = e.activation(XS["k"][:, 4 * b:4 * b + 4, 0:DN], ps[:, 3 + b, :].rearrange("p (h q) -> p h q", h=4)[:, :, 0:DN], ACT.Copy)
                        ins.then_inc(S("la_cp"), 1)
                evac(e, [x for x in items if x[0] == NJ - 1])
                for n, (j, h) in enumerate(at):
                    nk = NCTX if j < JC else T
                    e.wait_ge(S("at_m"), ab + n + 1)
                    if n >= 2:
                        e.wait_ge(S("at_t"), ab + n - 1)
                    e.activation(PB[n % 2][:, 0:nk], flat(0, nk), ACT.Exp, bias=nm[:, n % 2:n % 2 + 1], scale=DQK ** 0.5,
                                 accum_out=sm[:, n % 2:n % 2 + 1]).then_inc(S("at_e"), 1)
                    if n:
                        turn(e, n - 1)
                turn(e, len(at) - 1)

            def turn(e, n):
                nk = NCTX if at[n][0] < JC else T
                e.wait_ge(S("at_t"), ab + n + 1)
                if n >= 2:
                    e.wait_ge(S("at_o"), ab + n - 1)
                e.activation(PT[n % 2][:, 0:nk // P, :].rearrange("p k t -> p (k t)"), flat(3, nk), ACT.Copy).then_inc(S("at_pt"), 1)

            def evac(e, its):
                for it in its:
                    n = ib + items.index(it)
                    e.wait_ge(S("la_xt"), n + 1)
                    dst = (QT if it[1] == "q" else KT)[0:DQK, :, it[0] * P:(it[0] + 1) * P]
                    e.activation(dst, ps[0:DQK, 5:7, :].rearrange("p b (h t) -> p (b h) t", h=4), ACT.Copy).then_inc(S("la_xo"), 1)

            def flat(b, n):
                return ps[:, b:b + 3, :].rearrange("p b c -> p (b c)")[:, 0:n]

            def po(e):
                e.wait_ge(S("la_ss"), l + 1)
                for c_, (o, w) in enumerate(parts):
                    ins = rsqrt(e, cr[:, c_, :], cs[:, c_, :], EPS * w)
                    ins.then_inc(S("la_rs"), 1)
                for n, (j, w) in enumerate(items):
                    if w == "k":
                        if j:
                            e.wait_ge(S("la_xt"), ib + items.index((j - 1, "k")) + 1)
                        kr = TM[:, j, TM_KR:TM_KR + DR].unsqueeze(1).broadcast_to([P, MH, DR])
                        e.tensor_copy(XS["k"][:, :, DN:DQK], kr).then_inc(S("la_kr"), 1)
                    e.wait_ge(S("la_s"), ib + n + 1)
                    if n:
                        e.wait_ge(S("la_x"), ib + n)
                    rsqrt(e, rx, sx, EPS * DQK).then_inc(S("la_r"), 1)

            def ve(e):
                e.wait_ge(S("la_in"), 96 * (l + 1))
                for k in range(2):
                    e.tensor_scalar(wq[:, k, :], wq[:, k, :], gq[:, k:k + 1], None, ALU.mult).then_inc(S("la_w"), 1)
                e.tensor_scalar(wkv, wkv, gkv, None, ALU.mult).then_inc(S("la_w"), 1)
                e.wait_ge(S("la_rs"), 2 * (l + 1))
                for c_, (o, w) in enumerate(parts):
                    for j in range(NJ):
                        v = TM[:, j, o:o + w]
                        e.tensor_scalar(v, v, cr[:, c_, j:j + 1], float(w) ** 0.5, ALU.mult, ALU.mult).then_inc(S("la_c"), 1)
                for n, (j, w) in enumerate(items):
                    X = XS[w]
                    e.wait_ge(S("la_cp"), 2 * (NJ * l + j + 1))
                    if w == "k":
                        for b in range(2):
                            e.tensor_copy(VV[:, j, 4 * b:4 * b + 4, :], ps[:, 3 + b, :].rearrange("p (h q) -> p h q", h=4)[:, :, DN:DN + DV])\
                             .then_inc(S("la_v"), 1)
                        e.wait_ge(S("la_kr"), NJ * l + j + 1)
                    dve.step(e, e.tensor_tensor(SQ, X, X, ALU.mult))
                    e.tensor_reduce(sx, SQ, AX.X, ALU.add).then_inc(S("la_s"), 1)
                    e.wait_ge(S("la_r"), ib + n + 1)
                    dve.step(e, e.tensor_tensor(X, X, rx.unsqueeze(2).broadcast_to([P, MH, DQK]), ALU.mult))
                    ins = e.tensor_tensor(X, X, gains[w].unsqueeze(1).broadcast_to([P, MH, DQK]), ALU.mult)
                    if j >= JC:
                        dve.step(e, ins)
                        cos, sin = ropes[:, j - JC, 0:DR], ropes[:, j - JC, DR:2 * DR]
                        xr = X[:, :, DN:DQK]
                        x4, t4 = (v.rearrange("p h (g s q) -> p h g s q", g=2, s=2) for v in (xr, SQ[:, :, 0:DR]))
                        s4 = sin.rearrange("p (g s q) -> p g s q", g=2, s=2)
                        for s in range(2):
                            dve.did(e.tensor_tensor(t4[:, :, :, s, :], x4[:, :, :, 1 - s, :],
                                                    s4[:, :, s, :].unsqueeze(1).broadcast_to([P, MH, 2, 8]), ALU.mult))
                        dve.settle(e)
                        dve.step(e, e.tensor_tensor(xr, xr, cos.unsqueeze(1).broadcast_to([P, MH, DR]), ALU.mult))
                        ins = e.tensor_tensor(xr, xr, SQ[:, :, 0:DR], ALU.add)
                    ins.then_inc(S("la_x"), 1)
                    e.wait_ge(S("la_x"), ib + n + 1)

                def scale(n):
                    nk = NCTX if at[n][0] < JC else T
                    b = n % 2
                    e.wait_ge(S("at_e"), ab + n + 1)
                    dve.step(e, e.reciprocal(rc[:, b:b + 1], sm[:, b:b + 1]))
                    e.tensor_scalar(PB[b][:, 0:nk], PB[b][:, 0:nk], rc[:, b:b + 1], None, ALU.mult).then_inc(S("at_p"), 1)

                def head_out(n):
                    j, h = at[n]
                    if h % 2:
                        e.wait_ge(S("at_o"), ab + n + 1)
                        y = TM[:, j, 256 + P * (h // 2):256 + P * (h // 2) + P]
                        e.tensor_copy(y, ps[:, 6 + (n // 2) % 2, 0:P]).then_inc(S("at_y"), 1)

                for n, (j, h) in enumerate(at):
                    nk = NCTX if j < JC else T
                    b = n % 2
                    e.wait_ge(S("at_s"), ab + n + 1)
                    if n >= 2:
                        e.wait_ge(S("at_e"), ab + n - 1)
                    dve.step(e, e.tensor_reduce(mx[:, b:b + 1], flat(0, nk), AX.X, ALU.max))
                    e.tensor_scalar(nm[:, b:b + 1], mx[:, b:b + 1], -(DQK ** 0.5), None, ALU.mult).then_inc(S("at_m"), 1)
                    scale(n)
                    if n >= 2:
                        head_out(n - 2)
                head_out(len(at) - 1)

            def pe(e):
                e.wait_ge(S("la_c"), 2 * NJ * (l + 1))
                e.wait_ge(S("la_w"), 3 * (l + 1))

                def front(j):
                    n = NJ * l + j
                    if j:
                        e.wait_ge(S("la_ct"), n)
                    for k in range(3):
                        mm = e.transpose(ps[:, 0, k * P:(k + 1) * P], TM[:, j, TM_CQ + k * P:TM_CQ + (k + 1) * P], ident)
                    mm.then_inc(S("la_t"), 1)
                    e.wait_ge(S("la_ct"), n + 1)
                    if j:
                        e.wait_ge(S("la_cp"), 2 * n)
                        e.wait_ge(S("la_v"), 2 * n)
                    for b in range(2):
                        if j >= jo:
                            for k in range(2):
                                e.matmul(ps[:, 1 + b, 0:384], CT[:, k, :], wq[:, k, 384 * b:384 * b + 384], start=k == 0, stop=k == 1)
                        mm = e.matmul(ps[:, 3 + b, :], CT[:, 2, :], wkv[:, 512 * b:512 * b + 512], start=True, stop=True)
                    mm.then_inc(S("la_mm"), 1)

                def back(j):
                    for it in [x for x in items if x[0] == j]:
                        n = ib + items.index(it)
                        e.wait_ge(S("la_x"), n + 1)
                        if n > ib:
                            e.wait_ge(S("la_xo"), n)
                        for h in range(MH):
                            mm = e.transpose(ps[0:DQK, 5 + h // 4, P * (h % 4):P * (h % 4) + P], XS[it[1]][:, h, :], ident)
                        mm.then_inc(S("la_xt"), 1)

                front(0)
                for j in range(1, NJ):
                    front(j)
                    back(j - 1)
                back(NJ - 1)
                e.wait_ge(S("la_xo"), ib + len(items))

                def scores(n):
                    j, h = at[n]
                    nk = NCTX if j < JC else T
                    if n:
                        e.wait_ge(S("at_e"), ab + n)
                    for k0 in range(0, nk, 512):
                        w = min(512, nk - k0)
                        mm = e.matmul(ps[:, k0 // 512, 0:w], QT[0:DQK, h, j * P:(j + 1) * P], KT[0:DQK, h, k0:k0 + w], start=True, stop=True)
                    mm.then_inc(S("at_s"), 1)

                def outs(n):
                    j, h = at[n]
                    nk = (NCTX if j < JC else T) // P
                    e.wait_ge(S("at_pt"), ab + n + 1)
                    pair = (ab + n) // 2
                    if h % 2 == 0 and pair - ab // 2 >= 2:
                        e.wait_ge(S("at_y"), pair - 1)
                    r = slice(64 * (h % 2), 64 * (h % 2) + 64)
                    if h % 2:
                        e.wait_ge(S("at_o"), ab + n)
                    for k in range(nk):
                        mm = e.matmul(ps[r, 6 + (n // 2) % 2, 0:P], VV[:, k, h, :], PT[n % 2][:, k, :], start=k == 0, stop=k == nk - 1)
                    mm.then_inc(S("at_o"), 1)

                scores(0)
                for n, (j, h) in enumerate(at):
                    nk = (NCTX if j < JC else T) // P
                    if n + 1 < len(at):
                        scores(n + 1)
                    e.wait_ge(S("at_p"), ab + n + 1)
                    if n:
                        e.wait_ge(S("at_pt"), ab + n)
                    for k in range(nk):
                        mm = e.transpose(ps[:, 3 + k // 4, P * (k % 4):P * (k % 4) + P], PB[n % 2][:, k * P:(k + 1) * P], ident)
                    mm.then_inc(S("at_t"), 1)
                    if n:
                        outs(n - 1)
                outs(len(at) - 1)

            stage(sync=sp, gpsimd=po, scalar=sc, vector=ve, tensor=pe)

        def wout(l):
            wo = V(0, (KD, D))
            G1 = V(8192, (2, D))
            yt = [V(37600 + n * 512, (4, P)) for n in range(2)]
            xt = [V(38624 + n * 1024, (D,)) for n in range(2)]
            pt = [V(40672 + n * 1024, (D,)) for n in range(2)]
            jo = 0 if l == 0 else JC
            nout = NJ - jo
            ob = (0, NJ)[l]

            def tile_of(j, src):
                if src and l == 0:
                    t, q = (a["ctx"][0], j) if j < JC else (a["x"][0], j - JC)
                elif not src and l == 1:
                    t, q = out[0], j - JC
                else:
                    t, q = xres, j
                return t[q * P:(q + 1) * P, :]

            def sp(e):
                e.dma_start(wo, a["w_out"][l].rearrange("(k p) n -> p k n", p=P)).then_inc(S("wo_in"), 16)
                for s in range(2):
                    e.dma_start(G1[:, s, :], modd[2 * l + s, 2 * D:3 * D].partition_broadcast(P)).then_inc(S("wo_in"), 16)
                def store(m, j):
                    e.wait_ge(S("wo_x"), ob + m + 1)
                    e.dma_start(tile_of(j, False), xt[m % 2]).then_inc(S(f"wo_st{m % 2}"), 16)
                for m, j in enumerate(range(jo, NJ)):
                    if m >= 2:
                        e.wait_ge(S(f"wo_st{m % 2}"), 16 * (ob // 2 + m // 2))
                    e.dma_start(xt[m % 2], tile_of(j, True)).then_inc(S(f"wo_ld{m % 2}"), 16)
                    if m:
                        store(m - 1, j - 1)
                store(nout - 1, NJ - 1)
                for b in range(2):
                    e.wait_ge(S(f"wo_st{b}"), 16 * (ob + nout) // 2)

            def pe(e):
                def prod(m, j):
                    e.wait_ge(S("wo_y"), ob + m + 1)
                    if m == 0:
                        e.wait_ge(S("wo_in"), 48 * (l + 1))
                    if m >= 2:
                        e.wait_ge(S("wo_p"), ob + m - 1)
                    for n in range(2):
                        for k in range(KD):
                            y = yt[m % 2][:, k, :] if k < 4 else TM[:, j, 256 + P * (k - 4):256 + P * (k - 3)]
                            mm = e.matmul(ps[:, 2 + 2 * (m % 2) + n, :], y, wo[:, k, n * 512:(n + 1) * 512], start=k == 0, stop=k == KD - 1)
                    mm.then_inc(S("wo_mm"), 1)
                for m, j in enumerate(range(jo, NJ)):
                    if m >= 2:
                        e.wait_ge(S("wo_y"), ob + m - 1)
                    for k in range(4):
                        y = (YM if k < 2 else YH)[:, j, P * (k % 2):P * (k % 2) + P]
                        mm = e.transpose(ps[:, m % 2, k * P:(k + 1) * P], y, ident)
                    mm.then_inc(S("wo_t"), 1)
                    if m:
                        prod(m - 1, j - 1)
                prod(nout - 1, NJ - 1)

            def sc(e):
                for m in range(nout):
                    e.wait_ge(S("wo_t"), ob + m + 1)
                    if m >= 2:
                        e.wait_ge(S("wo_mm"), ob + m - 1)
                    e.activation(yt[m % 2], ps[:, m % 2, :].rearrange("p (k t) -> p k t", k=4), ACT.Copy).then_inc(S("wo_y"), 1)

            def ve(e):
                for m, j in enumerate(range(jo, NJ)):
                    e.wait_ge(S("wo_mm"), ob + m + 1)
                    if m >= 2:
                        e.wait_ge(S("wo_x"), ob + m - 1)
                    b = 2 + 2 * (m % 2)
                    e.tensor_tensor(pt[m % 2], ps[:, b:b + 2, :].rearrange("p b c -> p (b c)"), G1[:, 0 if j < JC else 1, :], ALU.mult)\
                     .then_inc(S("wo_p"), 1)
                    e.wait_ge(S("wo_p"), ob + m + 1)
                    e.wait_ge(S(f"wo_ld{m % 2}"), 16 * (ob // 2 + m // 2 + 1))
                    e.tensor_tensor(xt[m % 2], xt[m % 2], pt[m % 2], ALU.add).then_inc(S("wo_x"), 1)

            stage(sync=sp, tensor=pe, scalar=sc, vector=ve)

        GL, GC = small[:, 0:16], small[:, 16:32]
        IG, IS, CG = (small[:, 32 + 16 * n:48 + 16 * n].bitcast(U32) for n in range(3))

        def route(l):
            hT = V(0, (KD, T))
            rw = V(10240, (KD, NE))
            LR = V(10400, (T,))[0:NE]
            AT = V(11700, (NJ, NE))
            EX = V(11900, (NJ, NE))
            AF = V(12400, (T,))[0:NE]
            VL = V(15000, (CAP,))[0:NE]
            IX = V(15200, (CAP,))[0:NE].bitcast(U32)
            IF = V(15400, (CAP,))[0:NE]
            col = V(15600, (80,))
            r1, r2 = small[:, 100:100 + NJ], small[:, 112:112 + NJ]
            j0 = 0 if l == 0 else JC
            nj = NJ - j0
            t0 = j0 * P
            toks = [(x, min(512, T - x)) for x in range(t0, T, 512)]
            nb = (0, len([x for x in range(0, T, 512)]))[l]

            def sp(e):
                e.dma_start(rw, a["router_w"][l].rearrange("(k p) n -> p k n", p=P)).then_inc(S("rw_in"), 16)

            def pe(e):
                e.wait_ge(S("rw_in"), 16 * (l + 1))
                for n, (x, w) in enumerate(toks):
                    for k in range(KD):
                        mm = e.matmul(ps[0:NE, n, 0:w], rw[:, k, :], hT[:, k, x:x + w], start=k == 0, stop=k == KD - 1)
                    mm.then_inc(S("rt_l"), 1)
                e.wait_ge(S("rt_lr"), nb + len(toks))
                for j in range(j0, NJ):
                    mm = e.transpose(ps[:, 3, NE * j:NE * j + NE], LR[:, j * P:(j + 1) * P], ident[0:NE, 0:NE])
                mm.then_inc(S("rt_t"), 1)
                e.wait_ge(S("rt_a"), l + 1)
                for j in range(j0, NJ):
                    mm = e.transpose(ps[0:NE, 4 + j // 4, P * (j % 4):P * (j % 4) + P], AT[:, j, :], ident)
                mm.then_inc(S("rt_t"), 1)
                e.wait_ge(S("rt_if"), l + 1)
                for n, v in enumerate((VL, IF)):
                    e.transpose(ps[:, 0, 16 * n:16 * n + 16], v[:, 0:CAPL], ident[0:NE, 0:NE])
                    if l == 0:
                        e.transpose(ps[0:CAPC, 0, 32 + 16 * n:48 + 16 * n], v[:, CAPL:CAP], ident[0:NE, 0:NE])
                e.transpose(ps[:, 0, 64:80], IF[:, 0:CAPL], ident[0:NE, 0:NE]).then_inc(S("rt_t"), 1)

            def sc(e):
                for n, (x, w) in enumerate(toks):
                    e.wait_ge(S("rt_l"), nb + n + 1)
                    e.activation(LR[:, x:x + w], ps[0:NE, n, 0:w], ACT.Copy).then_inc(S("rt_lr"), 1)
                e.wait_ge(S("rt_s"), l + 1)
                e.activation(EX[:, j0:, :], EX[:, j0:, :], ACT.Exp).then_inc(S("rt_e"), 1)

            def ve(e):
                e.wait_ge(S("rt_t"), 3 * l + 1)
                lg = ps[:, 3, 0:NJ * NE].rearrange("p (j n) -> p j n", n=NE)[:, j0:, :]
                a_, x_ = AT[:, j0:, :], EX[:, j0:, :]
                m_, s_ = r1[:, 0:nj], r2[:, 0:nj]
                dve.step(e, e.tensor_reduce(m_, lg, AX.X, ALU.max))
                e.tensor_tensor(x_, lg, m_.unsqueeze(2).broadcast_to([P, nj, NE]), ALU.subtract).then_inc(S("rt_s"), 1)
                e.wait_ge(S("rt_e"), l + 1)
                dve.step(e, e.tensor_reduce(s_, x_, AX.X, ALU.add))
                dve.step(e, e.reciprocal(m_, s_))
                e.tensor_tensor(a_, x_, m_.unsqueeze(2).broadcast_to([P, nj, NE]), ALU.mult).then_inc(S("rt_a"), 1)
                e.wait_ge(S("rt_t"), 3 * l + 2)
                src = ps[0:NE, 4:7, :].rearrange("p b c -> p (b c)")
                dve.step(e, e.tensor_copy(AF[:, t0:T], src[:, t0:T]))
                for x0, x1, o, n in ((NCTX, T, 0, CAPL), (0, NCTX, CAPL, CAPC))[:2 - l]:
                    w = AF[:, x0:x1]
                    for q in range(o, o + n, 8):
                        dve.step(e, e.max(VL[:, q:q + 8], w))
                        dve.did(e.max_index(IX[:, q:q + 8], VL[:, q:q + 8], w))
                        dve.settle(e)
                        dve.step(e, e.match_replace(w, VL[:, q:q + 8], w, -1.0))
                nn = CAP if l == 0 else CAPL
                e.tensor_copy(IF[:, 0:nn], IX[:, 0:nn]).then_inc(S("rt_if"), 1)
                e.wait_ge(S("rt_t"), 3 * l + 3)
                dve.step(e, e.tensor_copy(col[:, 0:32], ps[:, 0, 0:32]))
                dve.did(e.tensor_copy(GL, col[:, 0:16]))
                dve.did(e.tensor_scalar(IG, col[:, 16:32], float(NCTX), None, ALU.add))
                dve.did(e.tensor_scalar(IS, col[:, 16:32], float(0 if l else NCTX), None, ALU.add))
                if l == 0:
                    dve.did(e.tensor_copy(GC[0:CAPC, :], ps[0:CAPC, 0, 32:48]))
                    dve.did(e.tensor_copy(CG[0:CAPC, :], ps[0:CAPC, 0, 48:64]))
                dve.settle(e)

            stage(sync=sp, tensor=pe, scalar=sc, vector=ve)

        def ffn(l):
            wg, wu, wd = (V(8192 * n, (KD, D)) for n in range(3))
            G2 = V(24576, (2, D))
            XL, XC = V(26624, (D,)), V(27648, (D,))
            tw = CAP if l == 0 else CAPL
            XT, HD, OT = (V(28672 + 1280 * n, (KD, CAP)) for n in range(3))
            OL, OC = V(32512, (D,)), V(33536, (D,))
            SG = [V(34560 + CAP * n, (CAP,)) for n in range(2)]
            slots = small[:, 96:104]
            ig, is_, cg, cs_ = (slots[:, n:n + 1].bitcast(U32) for n in range(4))
            gl, gc = slots[:, 4:5], slots[:, 5:6]
            dst = xres if l == 0 else out[0]
            E0 = NE * l
            per = 4 if l == 0 else 2

            def halves(e, i, f):
                for h in range(2):
                    if f:
                        e.wait_ge(S("ff_gu"), i * 8 + (8 * E0 - 8 + 4 * (h + 1)))
                    for w, src in ((wg, "ex_w_gate"), (wu, "ex_w_up")):
                        v = a[src][l].rearrange("e (k p) n -> e p k n", p=P)
                        e.dma_start(w[:, :, 512 * h:512 * h + 512], v[i, :, :, 512 * h:512 * h + 512]).then_inc(S(f"ff_wg{h}"), 16)
                for h in range(2):
                    if f:
                        e.wait_ge(S("ff_dn"), i * 8 + (8 * E0 - 8 + 4 * (h + 1)))
                    v = a["ex_w_down"][l].rearrange("e (k p) n -> e p k n", p=P)
                    e.dma_start(wd[:, :, 512 * h:512 * h + 512], v[i, :, :, 512 * h:512 * h + 512]).then_inc(S(f"ff_wd{h}"), 16)

            def sp(e):
                for s in range(2):
                    e.dma_start(G2[:, s, :], modd[2 * l + s, 5 * D:6 * D].partition_broadcast(P)).then_inc(S("ff_g2"), 16)
                halves(e, 0, False)
                with e.Fori(1, NE) as i:
                    halves(e, i, True)

            def gather(e, i):
                c1 = lambda v, k=P: v[0:k, i:i + 1] if isinstance(i, int) else v[0:k, bass.ds(i, 1)]
                e.tensor_copy(ig, c1(IG)).then_inc(S("ff_ix"), 1)
                if l == 0:
                    e.tensor_copy(cg[0:CAPC], c1(CG, CAPC)).then_inc(S("ff_ix"), 1)
                e.wait_ge(S("ff_ix"), (i + 1) * ixn + ix0)
                e.sem_inc(S("ff_go"), 1)
                e.indirect_dma_start(out=XL, out_offset=None, in_=xnd, in_offset=bass.IndirectOffsetOnAxis(ap=ig, axis=0)).then_inc(S("ff_xl"), 16)
                if l == 0:
                    e.indirect_dma_start(out=XC[0:CAPC], out_offset=None, in_=xnd,
                                         in_offset=bass.IndirectOffsetOnAxis(ap=cg[0:CAPC], axis=0)).then_inc(S("ff_xc"), 16)

            ixn, ix0 = (2, 0) if l == 0 else (1, 2 * NE)

            def scatter(e, i):
                c1 = lambda v, k=P: v[0:k, i:i + 1] if isinstance(i, int) else v[0:k, bass.ds(i, 1)]
                e.wait_ge(S("ff_sl"), i * 16 + 16 * E0)
                if l == 0:
                    e.wait_ge(S("ff_sc"), i * 16)
                e.tensor_copy(is_, c1(IS)).then_inc(S("ff_iy"), 1)
                if l == 0:
                    e.tensor_copy(cs_[0:CAPC], c1(CG, CAPC)).then_inc(S("ff_iy"), 1)
                e.wait_ge(S("ff_iy"), (i + 1) * ixn + ix0)
                e.wait_ge(S("ff_ol"), (i + 1) * ixn + ix0)
                e.sem_inc(S("ff_go"), 1)
                e.indirect_dma_start(out=dst, out_offset=bass.IndirectOffsetOnAxis(ap=is_, axis=0), in_=OL, in_offset=None,
                                     compute_op=ALU.add).then_inc(S("ff_sl"), 16)
                if l == 0:
                    e.indirect_dma_start(out=dst, out_offset=bass.IndirectOffsetOnAxis(ap=cs_[0:CAPC], axis=0), in_=OC[0:CAPC], in_offset=None,
                                         compute_op=ALU.add).then_inc(S("ff_sc"), 16)

            def po(e):
                gather(e, 0)
                with e.Fori(0, NE - 1) as i:
                    e.wait_ge(S("ff_xtt"), i + (E0 + 1))
                    gather(e, i + 1)
                    scatter(e, i)
                scatter(e, NE - 1)
                e.wait_ge(S("ff_sl"), 16 * (E0 + NE))
                if l == 0:
                    e.wait_ge(S("ff_sc"), 16 * NE)

            def turn(e, i):
                e.wait_ge(S("ff_xl"), (i + 1) * 16 + 16 * E0)
                if l == 0:
                    e.wait_ge(S("ff_xc"), (i + 1) * 16)
                for k in range(KD):
                    mm = e.transpose(ps[:, k // 4, P * (k % 4):P * (k % 4) + P], XL[:, k * P:(k + 1) * P], ident)
                    if l == 0:
                        mm = e.transpose(ps[:, 2, CAPC * k:CAPC * (k + 1)], XC[0:CAPC, k * P:(k + 1) * P], ident[0:CAPC, 0:CAPC])
                mm.then_inc(S("ff_xtt"), 1)

            def pe(e):
                def expert(i, last):
                    b8 = i * 8 + 8 * E0
                    e.wait_ge(S("ff_xt"), (i + 1) * ixn + ix0)
                    e.wait_ge(S("ff_hd"), b8)
                    for f in range(8):
                        if f % 4 == 0:
                            e.wait_ge(S(f"ff_wg{f // 4}"), (i + 1) * 32 + 32 * E0)
                        if f >= 3:
                            e.wait_ge(S("ff_hd"), b8 + (f - 2))
                        for n, w in enumerate((wg, wu)):
                            for k in range(KD):
                                mm = e.matmul(ps[:, 3 + f % 3, 256 * n:256 * n + tw], w[:, k, f * P:(f + 1) * P], XT[:, k, 0:tw],
                                              start=k == 0, stop=k == KD - 1)
                        mm.then_inc(S("ff_gu"), 1)
                    if not last:
                        e.wait_ge(S("ff_ol"), i * ixn + ix0)
                        turn(e, i + 1)
                    e.wait_ge(S("ff_ot"), b8)
                    e.wait_ge(S("ff_hd"), b8 + 8)
                    e.wait_ge(S("ff_ol"), i * ixn + ix0)
                    for d in range(8):
                        if d % 4 == 0:
                            e.wait_ge(S(f"ff_wd{d // 4}"), (i + 1) * 16 + 16 * E0)
                        if d >= 2:
                            e.wait_ge(S("ff_ot"), b8 + (d - 1))
                        for k in range(KD):
                            mm = e.matmul(ps[:, 6 + d % 2, 0:tw], wd[:, k, d * P:(d + 1) * P], HD[:, k, 0:tw], start=k == 0, stop=k == KD - 1)
                        mm.then_inc(S("ff_dn"), 1)
                    e.wait_ge(S("ff_ot"), b8 + 8)
                    if not last:
                        e.wait_ge(S("ff_xt"), (i + 2) * ixn + ix0)
                    for d in range(8):
                        mm = e.transpose(ps[:, d // 4, P * (d % 4):P * (d % 4) + P], OT[:, d, 0:CAPL], ident)
                        if l == 0:
                            mm = e.transpose(ps[0:CAPC, 6 + d // 4, P * (d % 4):P * (d % 4) + P], OT[:, d, CAPL:CAP], ident)
                    mm.then_inc(S("ff_bt"), 1)

                turn(e, 0)
                with e.Fori(0, NE - 1) as i:
                    expert(i, False)
                expert(NE - 1, True)

            def sc(e):
                with e.Fori(0, NE) as i:
                    b8 = i * 8 + 8 * E0
                    for f in range(8):
                        e.wait_ge(S("ff_gu"), b8 + (f + 1))
                        e.wait_ge(S("ff_hd"), b8 + max(f - 1, 0))
                        e.activation(SG[f % 2][:, 0:tw], ps[:, 3 + f % 3, 0:tw], ACT.Silu).then_inc(S("ff_sg"), 1)
                    e.wait_ge(S("ff_bt"), i + E0)
                    for d in range(8):
                        e.wait_ge(S("ff_dn"), b8 + (d + 1))
                        e.activation(OT[:, d, 0:tw], ps[:, 6 + d % 2, 0:tw], ACT.Copy).then_inc(S("ff_ot"), 1)

            def modulate(e, i):
                e.wait_ge(S("ff_xtt"), i + (E0 + 1))
                for s, k0, w, src in ((1, 0, CAPL, ps[:, 0:2, :].rearrange("p b (k t) -> p (b k) t", k=4)),
                                      (0, CAPL, CAPC, ps[:, 2, 0:256].rearrange("p (k t) -> p k t", k=KD)))[:2 - l]:
                    o = XT[:, :, k0:k0 + w]
                    sc_, sh = (AB[:, 1, s, q, :].unsqueeze(2).broadcast_to([P, KD, w]) for q in range(2))
                    dve.step(e, e.tensor_tensor(o, src, sc_, ALU.mult))
                    e.tensor_tensor(o, o, sh, ALU.add).then_inc(S("ff_xt"), 1)

            def ve(e):
                def expert(i, last):
                    b8 = i * 8 + 8 * E0
                    e.wait_ge(S("ff_dn"), b8)
                    for f in range(8):
                        e.wait_ge(S("ff_sg"), b8 + (f + 1))
                        e.tensor_tensor(HD[:, f, 0:tw], SG[f % 2][:, 0:tw], ps[:, 3 + f % 3, 256:256 + tw], ALU.mult).then_inc(S("ff_hd"), 1)
                    if not last:
                        modulate(e, i + 1)
                    c1 = lambda v, k=P: v[0:k, i:i + 1] if isinstance(i, int) else v[0:k, bass.ds(i, 1)]
                    e.wait_ge(S("ff_ol"), i * ixn + ix0)
                    dve.did(e.tensor_copy(gl, c1(GL)))
                    if l == 0:
                        dve.did(e.tensor_copy(gc[0:CAPC], c1(GC, CAPC)))
                    dve.settle(e)
                    e.wait_ge(S("ff_bt"), i + (E0 + 1))
                    e.wait_ge(S("ff_sl"), i * 16 + 16 * E0)
                    e.scalar_tensor_tensor(OL, ps[:, 0:2, :].rearrange("p b c -> p (b c)"), gl, G2[:, 1, :], ALU.mult, ALU.mult)\
                     .then_inc(S("ff_ol"), 1)
                    if l == 0:
                        e.wait_ge(S("ff_sc"), i * 16)
                        e.scalar_tensor_tensor(OC[0:CAPC], ps[0:CAPC, 6:8, :].rearrange("p b c -> p (b c)"), gc[0:CAPC], G2[0:CAPC, 0, :],
                                               ALU.mult, ALU.mult).then_inc(S("ff_ol"), 1)

                e.wait_ge(S("ff_g2"), 32 * (l + 1))
                modulate(e, 0)
                n0 = dve.n
                with e.Fori(0, NE - 1) as i:
                    dve.more = i * per
                    expert(i, False)
                assert dve.n == n0 + per
                dve.more, dve.n = 0, n0 + per * (NE - 1)
                expert(NE - 1, True)

            stage(sync=sp, gpsimd=po, tensor=pe, scalar=sc, vector=ve)

        def run(e, name):
            for n, st in enumerate(stages):
                if n:
                    e.wait_ge(ended, 5 * n)
                if name in st:
                    st[name](e)
                e.drain().then_inc(ended, 1)

        for l in range(DEPTH):
            ada(l)
            norm(l, 0)
            proj(l)
            mlstm(l)
            hgrn(l)
            mla(l)
            wout(l)
            norm(l, 1)
            route(l)
            ffn(l)

        block = c.enter_context(nc.Block())

        @block.sync
        def _(e):
            e.dma_start(cst[:, :], a["const"]).then_inc(const_in, 16)
            e.dma_start(ropes[:, :, :], a["rope"].rearrange("(j p) c -> p j c", p=P)).then_inc(const_in, 16)
            e.wait_ge(const_in, 32)
            run(e, "sync")

        @block.scalar
        def _(e):
            e.wait_ge(const_in, 32)
            run(e, "scalar")

        @block.gpsimd
        def _(e):
            e.wait_ge(const_in, 32)
            run(e, "gpsimd")

        @block.vector
        def _(e):
            e.wait_ge(const_in, 32)
            run(e, "vector")

        @block.tensor
        def _(e):
            e.wait_ge(const_in, 32)
            run(e, "tensor")


_INS = ["x", "c", "ctx", "c_ctx", "ada_w", "ada_b", "norm1_g", "norm2_g", "w_in", "b_in", "ml_conv_w", "ml_conv_b",
        "ml_norm_g", "hg_lb_logits", "hg_norm_g", "mla_q_norm_g", "mla_w_uq", "mla_kv_norm_g", "mla_w_ukv",
        "mla_q_qk_g", "mla_k_qk_g", "w_out", "router_w", "ex_w_gate", "ex_w_up", "ex_w_down"]


def kernel(**inputs):
    import concourse.bacc as _bacc
    from concourse.bass_utils import run_bass_kernel_spmd as _run

    nc = _bacc.Bacc("TRN2", target_bir_lowering=False, num_devices=1)
    given = {n: np.ascontiguousarray(inputs[n]) for n in _INS}
    given |= {"const": consts()[0], "rope": rope_table()}
    arrays, aps = {}, {}
    for name, v in given.items():
        arrays[f"in_{name}"] = v
        aps[name] = nc.dram_tensor(f"in_{name}", v.shape, mybir.dt.from_np(v.dtype), kind="ExternalInput").ap()
    out = nc.dram_tensor("out_0", (1, NLAT, D), F32, kind="ExternalOutput").ap()
    build(nc, aps, out)
    r = _run(nc, [arrays], core_ids=[0])
    return r.results[0]["out_0"]
```

```python
from contextlib import ExitStack

import numpy as np
import concourse.bass as bass
from concourse import mybir

ALU = mybir.AluOpType
ACT = mybir.ActivationFunctionType
AX = mybir.AxisListType
F32 = mybir.dt.float32
U32 = mybir.dt.uint32

P = 128
D = 1024
KD = D // P
NCTX, NLAT = 256, 1024
JC, JL = NCTX // P, NLAT // P
NJ = JC + JL
T = NJ * P
DEPTH = 2
H = 4
DH = 64
MH, DQK, DN, DV, DR = 8, 96, 64, 64, 32
NE, CAPL, CAPC = 16, NLAT // 8, NCTX // 8
CAP = CAPL + CAPC
EPS = 1e-6
D_IN = 2736
NEG = -1e30
LEVELS = [64, 32, 16, 8, 4, 2, 1]

FM_COLS = [0, 128, 256, 384, 1040, 1168, 1808, 1936, 2064, 2192]
TM_COLS = [(512, 776), (776, 1040), (1296, 1552), (1552, 1808), (2320, 2576), (2576, 2736)]
TMW = sum(b - a for a, b in TM_COLS)
TM_V, TM_OG, TM_GATE, TM_HI, TM_HG, TM_CQ, TM_CKV, TM_KR = 0, 256, 512, 528, 784, 1040, 1296, 1424

ORDER = [list(range(NJ)), list(range(JC - 1, -1, -1)) + list(range(NJ - 1, JC - 1, -1))]
GROUPS = [(0, JC), (JC, 4), (JC + 4, 4)]


def consts():
    i = np.arange(P)
    s, t = i[:, None], i[None, :]
    parts = {
        "ident": s == t, "flip": s + t == P - 1, "le": s <= t, "ge": s >= t, "ones": s + t >= 0,
        "mhalf": np.full((P, 80), -0.5),
        "mask0": np.where(s <= t, 0.0, NEG), "mask1": np.where(s >= t, 0.0, NEG),
    }
    for m in LEVELS:
        fwd = (s // (2 * m) == t // (2 * m)) & (s % (2 * m) < m) & (t % (2 * m) >= m)
        parts[f"lvl{m}"] = np.concatenate([fwd, fwd.T], 1)
    col, at = {}, 0
    for n, a in parts.items():
        col[n] = (at, a.shape[1])
        at += a.shape[1]
    return np.concatenate([np.asarray(a, np.float32) for a in parts.values()], 1), col


def rope_table():
    half = DR // 2
    inv = np.float32(10000.0) ** (-np.arange(0, half, 2, dtype=np.float32) / np.float32(half))
    pos = np.arange(NLAT)
    out = []
    for p in (pos // 64, pos % 64):
        ang = p.astype(np.float32)[:, None] * inv[None].astype(np.float32)
        out.append((np.cos(ang), np.sin(ang)))
    (cr, sr), (cc, sc) = out
    return np.concatenate([cr, cr, cc, cc, -sr, sr, -sc, sc], 1).astype(np.float32)


class Chain:

    def __init__(self, sem):
        self.sem, self.n, self.more = sem, 0, 0

    def did(self, ins):
        ins.then_inc(self.sem, 1)
        self.n += 1

    def settle(self, eng):
        if self.n or not isinstance(self.more, int):
            eng.wait_ge(self.sem, self.n + self.more)

    def step(self, eng, ins):
        self.did(ins)
        self.settle(eng)


def build(nc, a, out):
    _, CC = consts()
    c = ExitStack()
    with c, nc.allow_non_contiguous_dma(reason="short parameter vectors onto partitions"):
        def sb(name, shape, dt=F32):
            return c.enter_context(nc.sbuf_tensor(name, shape, dt))

        def sem(name):
            return c.enter_context(nc.semaphore(name))

        xres = nc.dram_tensor("xres", (T, D), F32, kind="Internal").ap()
        xnd = nc.dram_tensor("xnd", (T, D), F32, kind="Internal").ap()
        modd = nc.dram_tensor("modd", (DEPTH * 2, 6 * D), F32, kind="Internal").ap()

        ar = sb("arena", [P, 48608])
        cst = sb("cst", [P, sum(w for _, w in CC.values())])
        modT = sb("modT", [P, 2, 48])
        AB = sb("AB", [P, 2, 2, 2, KD])
        gcol = sb("gcol", [P, 2, KD])
        ss = sb("ss", [P, 4 * NJ])
        rs = sb("rs", [P, 4 * NJ])
        ropes = sb("ropes", [P, JL, 2 * DR])
        small = sb("small", [P, 160])
        gainr = sb("gainr", [P, H * DH])
        ps = c.enter_context(nc.psum_tensor("ps", [P, 8, 512], F32))

        def K(name):
            return cst[:, CC[name][0]:CC[name][0] + CC[name][1]]

        ident, ones = K("ident"), K("ones")

        ended = sem("stage_ended")
        const_in = sem("const_in")
        dve = Chain(sem("vector_own"))
        pool = Chain(sem("gpsimd_own"))
        act = Chain(sem("scalar_own"))
        sems = {}

        def S(name):
            if name not in sems:
                sems[name] = sem(name)
            return sems[name]

        def V(lo, shape):
            n = int(np.prod(shape))
            v = ar[:, lo:lo + n]
            if len(shape) == 2:
                v = v.rearrange("p (a b) -> p a b", b=shape[1])
            if len(shape) == 3:
                v = v.rearrange("p (a b c) -> p a b c", b=shape[1], c=shape[2])
            if len(shape) == 4:
                v = v.rearrange("p (a b c d) -> p a b c d", b=shape[1], c=shape[2], d=shape[3])
            return v

        def rsqrt(e, o, x, eps):
            pool.step(e, e.tensor_scalar(o, x, eps, None, ALU.add))
            return e.tensor_tensor(o, o, K("mhalf")[:, 0:o.shape[1]], ALU.pow)

        stages = []

        def stage(**parts):
            stages.append(parts)

        def ada_parts(l, panel, row, bias, cT, banks, last_bank, room=None, between=None):
            base = l * 12

            def sp(e):
                for s, src in enumerate((a["c_ctx"], a["c"].rearrange("a d -> (a d)"))):
                    e.dma_start(cT[:, :, s:s + 1], src.rearrange("(k p o) -> p k o", p=P, o=1)).then_inc(S("c_in"), 16)
                w = a["ada_w"][l].rearrange("(k p) n -> p k n", p=P)
                for n in range(12):
                    if n == 2:
                        if room:
                            room(e)
                        for s in range(2):
                            e.dma_start(bias[s:s + 1, :], a["ada_b"][l:l + 1, :]).then_inc(S("ada_b"), 16)
                        for i, g in enumerate(("norm1_g", "norm2_g")):
                            e.dma_start(gcol[:, i, :], a[g][l].rearrange("(k p) -> p k", p=P)).then_inc(S("ada_b"), 16)
                    if n >= 2:
                        e.wait_ge(S("ada_mm"), base + n - 1)
                    e.dma_start(panel[n % 2], w[:, :, n * 512:(n + 1) * 512]).then_inc(S(f"ada_w{n % 2}"), 16)
                    if between:
                        between(e, n)
                e.wait_ge(S("ada_sum"), base + 12)
                e.dma_start(modd[2 * l:2 * l + 2, :], row[0:2, :]).then_inc(S("mod_out"), 16)
                e.wait_ge(S("mod_out"), 16 * (l + 1))

            def silu(e):
                e.wait_ge(S("c_in"), 32 * (l + 1))
                e.activation(cT, cT, ACT.Silu).then_inc(S("c_silu"), 1)

            def sc(e):
                for n in range(12):
                    e.wait_ge(S("ada_mm"), base + n + 1)
                    e.activation(row[0:2, n * 512:(n + 1) * 512], ps[0:2, banks[n % len(banks)], :], ACT.Copy).then_inc(S("ada_row"), 1)

            def pe(e):
                e.wait_ge(S("c_silu"), l + 1)
                nb = len(banks)
                for n in range(12):
                    e.wait_ge(S(f"ada_w{n % 2}"), 16 * (6 * l + n // 2 + 1))
                    if n >= nb:
                        e.wait_ge(S("ada_row"), base + n - nb + 1)
                    for k in range(KD):
                        mm = e.matmul(ps[0:2, banks[n % nb], :], cT[:, k, :], panel[n % 2][:, k, :], start=k == 0, stop=k == KD - 1)
                    mm.then_inc(S("ada_mm"), 1)
                e.wait_ge(S("ada_sum"), base + 12)
                for m in range(48):
                    mm = e.transpose(ps[:, last_bank, 2 * m:2 * m + 2], row[0:2, m * P:(m + 1) * P], ident[0:2, 0:2])
                mm.then_inc(S("ada_t"), 1)

            def po(e):
                e.wait_ge(S("ada_b"), 64 * (l + 1))
                for n in range(12):
                    e.wait_ge(S("ada_row"), base + n + 1)
                    r = slice(n * 512, (n + 1) * 512)
                    e.tensor_tensor(row[0:2, r], row[0:2, r], bias[0:2, r], ALU.add).then_inc(S("ada_sum"), 1)

            def ve(e):
                e.wait_ge(S("ada_t"), l + 1)
                dve.step(e, e.tensor_copy(modT[:, :, :], ps[:, last_bank, 0:96].rearrange("p (m s) -> p s m", s=2)))

            return sp, silu, sc, pe, po, ve

        def scales(e):
            for n in range(2):
                for s in range(2):
                    o = 3 * n * KD
                    dve.did(e.scalar_tensor_tensor(AB[:, n, s, 0, :], modT[:, s, o + KD:o + 2 * KD], 1.0,
                                                   gcol[:, n, :], ALU.add, ALU.mult))
                    dve.did(e.tensor_copy(AB[:, n, s, 1, :], modT[:, s, o:o + KD]))

        def ada(l):
            if l:
                stage(vector=scales)
                return
            sp, silu, copies, pe, po, turned = ada_parts(
                l, [V(n * 4096, (KD, 512)) for n in range(2)], V(8192, (6 * D,)), V(8192 + 6 * D, (6 * D,)),
                V(8192 + 12 * D, (KD, 2)), (0, 1, 2, 3), 4)

            def sc(e):
                silu(e)
                copies(e)

            def ve(e):
                turned(e)
                scales(e)

            stage(sync=sp, scalar=sc, gpsimd=po, tensor=pe, vector=ve)

        norm_groups = [0]
        xn_stores, xn_all = [0, 0], [{}, {}]

        def norm(l, n):
            groups = GROUPS if not (l == 1 and n == 1) else GROUPS[1:]
            xg = [V(10240 + 4096 * i, (4, D)) for i in range(2)]
            junk = V(18432, (D,))
            hT = V(0, (KD, T))
            g0 = norm_groups[0]
            norm_groups[0] += len(groups)

            def source(j):
                if n == 0 and l == 0:
                    return (a["ctx"] if j < JC else a["x"])[0].rearrange("(j p) d -> p j d", p=P), (j if j < JC else j - JC)
                if l == 1 and n == 1:
                    return out[0].rearrange("(j p) d -> p j d", p=P), j - JC
                return xres.rearrange("(j p) d -> p j d", p=P), j

            def sp(e):
                for i, (j0, nj) in enumerate(groups):
                    g = g0 + i
                    if i >= 2:
                        e.wait_ge(S("norm_t"), KD * (g - 1))
                        if n == 1:
                            e.wait_ge(S(f"xn_out{g % 2}"), 16 * (xn_count[g % 2][g] - 1))
                    src, j = source(j0)
                    e.dma_start(xg[g % 2][:, 0:nj, :], src[:, j:j + nj, :]).then_inc(S(f"x_in{g % 2}"), 16)
                    if i == 0:
                        continue
                    if n == 1:
                        store(e, i - 1)
                if n == 1:
                    store(e, len(groups) - 1)
                    for i in range(2):
                        e.wait_ge(S(f"xn_out{i}"), 16 * max(xn_count[i].values()))

            def store(e, i):
                j0, nj = groups[i]
                g = g0 + i
                e.wait_ge(S("xn_done"), g + 1)
                e.dma_start(xnd.rearrange("(j p) d -> p j d", p=P)[:, j0:j0 + nj, :], xg[g % 2][:, 0:nj, :])\
                 .then_inc(S(f"xn_out{g % 2}"), 16)

            for g in range(g0, g0 + len(groups)) if n == 1 else ():
                xn_stores[g % 2] += 1
                xn_all[g % 2][g] = xn_stores[g % 2]
            xn_count = [dict(x) for x in xn_all]

            def sc(e):
                for i, (j0, nj) in enumerate(groups):
                    g = g0 + i
                    e.wait_ge(S(f"x_in{g % 2}"), 16 * (g // 2 + 1))
                    for j in range(nj):
                        act.step(e, e.activation(junk, xg[g % 2][:, j, :], ACT.Square, accum_out=ss[:, j0 + j:j0 + j + 1]))
                    e.activation(small[:, 0:1], ss[:, j0:j0 + 1], ACT.Copy).then_inc(S("norm_ss"), 1)
                    evac(e, i, 0)

            def evac(e, i, odd):
                j0, nj = groups[i]
                g = g0 + i
                s = 0 if j0 < JC else 1
                for k in range(odd, KD, 2):
                    e.wait_ge(S("norm_t"), KD * g + k + 1)
                    o, q = hT[:, k, j0 * P:(j0 + nj) * P], ps[:, k % 4, 0:nj * P]
                    sa, sh = AB[:, n, s, 0, k:k + 1], AB[:, n, s, 1, k:k + 1]
                    if odd:
                        e.tensor_scalar(o, q, sa, sh, ALU.mult, ALU.add).then_inc(S("norm_h1"), 1)
                    else:
                        e.activation(o, q, ACT.Identity, bias=sh, scale=sa).then_inc(S("norm_h0"), 1)

            def po(e):
                for i, (j0, nj) in enumerate(groups):
                    e.wait_ge(S("norm_ss"), g0 + i + 1)
                    rsqrt(e, rs[:, j0:j0 + nj], ss[:, j0:j0 + nj], EPS * D).then_inc(S("norm_rs"), 1)

            def ve(e):
                for i, (j0, nj) in enumerate(groups):
                    g = g0 + i
                    e.wait_ge(S("norm_rs"), g + 1)
                    for j in range(nj):
                        ins = e.tensor_scalar(xg[g % 2][:, j, :], xg[g % 2][:, j, :], rs[:, j0 + j:j0 + j + 1], float(D) ** 0.5,
                                              ALU.mult, ALU.mult)
                    ins.then_inc(S("xn_done"), 1)
                    evac(e, i, 1)

            def pe(e):
                for i, (j0, nj) in enumerate(groups):
                    g = g0 + i
                    e.wait_ge(S("xn_done"), g + 1)
                    for k in range(KD):
                        if i or k >= 4:
                            e.wait_ge(S(f"norm_h{k % 2}"), (KD * g + k - 4) // 2 + 1)
                        for j in range(nj):
                            mm = e.transpose(ps[:, k % 4, j * P:(j + 1) * P], xg[g % 2][:, j, k * P:(k + 1) * P], ident)
                        mm.then_inc(S("norm_t"), 1)

            stage(sync=sp, scalar=sc, gpsimd=po, vector=ve, tensor=pe)

        TM = V(10240, (NJ, TMW))
        QKR = V(24800, (4, T))
        HQ = V(29920, (2, T))
        ZF = V(32480, (4, T))

        def proj(l):
            hT = V(0, (KD, T))
            fpan = [V(37600 + n * 1024, (KD, P)) for n in range(2)]
            tpan = [ar[:, 39648 + n * 2112:39648 + (n + 1) * 2112] for n in range(2)]
            brow = V(43872, (TMW,))
            bcol = small[:, 0:len(FM_COLS)]
            toks = [(0, 512), (512, 512), (1024, 256)]
            nf, nt = len(FM_COLS), len(TM_COLS)
            tm_off = np.cumsum([0] + [b - x for x, b in TM_COLS]).tolist()

            def tview(n):
                w = TM_COLS[n][1] - TM_COLS[n][0]
                return tpan[n % 2][:, 0:KD * w].rearrange("p (k n) -> p k n", n=w)

            def sp(e):
                w = a["w_in"][l].rearrange("(k p) n -> p k n", p=P)
                for n, (x, y) in enumerate(TM_COLS):
                    e.dma_start(brow[:, tm_off[n]:tm_off[n + 1]], a["b_in"][l, x:y].partition_broadcast(P)).then_inc(S("b_in"), 16)
                for n, x in enumerate(FM_COLS):
                    e.dma_start(bcol[:, n:n + 1], a["b_in"][l, x:x + P].rearrange("(p o) -> p o", o=1)).then_inc(S("b_in"), 16)
                for n in range(nf):
                    if n >= 2:
                        e.wait_ge(S("fm_mm"), 3 * (l * nf + n - 1))
                    e.dma_start(fpan[n % 2], w[:, :, FM_COLS[n]:FM_COLS[n] + P]).then_inc(S(f"fm_w{n % 2}"), 16)
                for n in range(nt):
                    if n >= 2:
                        e.wait_ge(S("tm_mm"), NJ * (l * nt + n - 1))
                    e.dma_start(tview(n), w[:, :, TM_COLS[n][0]:TM_COLS[n][1]]).then_inc(S(f"tm_w{n % 2}"), 16)

            def pe(e):
                q = 3 * nf * l
                for n in range(nf):
                    e.wait_ge(S(f"fm_w{n % 2}"), 16 * (l * nf // 2 + n // 2 + 1))
                    for i, (t0, tn) in enumerate(toks):
                        m = 3 * n + i
                        if m >= 4:
                            e.wait_ge(S("fm_out"), q + m - 3)
                        for k in range(KD):
                            mm = e.matmul(ps[:, m % 4, 0:tn], fpan[n % 2][:, k, :], hT[:, k, t0:t0 + tn], start=k == 0, stop=k == KD - 1)
                        mm.then_inc(S("fm_mm"), 1)
                for n in range(nt):
                    e.wait_ge(S(f"tm_w{n % 2}"), 16 * (l * nt // 2 + n // 2 + 1))
                    w = TM_COLS[n][1] - TM_COLS[n][0]
                    for j in range(NJ):
                        m = NJ * n + j
                        if m >= 4:
                            e.wait_ge(S("tm_out"), NJ * nt * l + m - 3)
                        for k in range(KD):
                            mm = e.matmul(ps[:, 4 + m % 4, 0:w], hT[:, k, j * P:(j + 1) * P], tview(n)[:, k, :], start=k == 0, stop=k == KD - 1)
                        mm.then_inc(S("tm_mm"), 1)

            def sc(e):
                e.wait_ge(S("b_in"), 16 * (nf + nt) * (l + 1))
                for n in range(nf):
                    dst = QKR[:, n, :] if n < 4 else HQ[:, n - 4, :] if n < 6 else ZF[:, n - 6, :]
                    for i, (t0, tn) in enumerate(toks):
                        m = 3 * n + i
                        e.wait_ge(S("fm_mm"), 3 * nf * l + m + 1)
                        e.activation(dst[:, t0:t0 + tn], ps[:, m % 4, 0:tn], ACT.Silu if n in (4, 5) else ACT.Identity,
                                     bias=bcol[:, n:n + 1]).then_inc(S("fm_out"), 1)

            def ve(e):
                e.wait_ge(S("b_in"), 16 * (nf + nt) * (l + 1))
                for n in range(nt):
                    w = TM_COLS[n][1] - TM_COLS[n][0]
                    for j in range(NJ):
                        m = NJ * n + j
                        e.wait_ge(S("tm_mm"), NJ * nt * l + m + 1)
                        e.tensor_tensor(TM[:, j, tm_off[n]:tm_off[n] + w], ps[:, 4 + m % 4, 0:w], brow[:, tm_off[n]:tm_off[n] + w], ALU.add).then_inc(S("tm_out"), 1)

            stage(sync=sp, tensor=pe, scalar=sc, vector=ve)

        def head_norm(l, name, Y, gate, func, gain):
            j0 = 0 if l == 0 else JC
            nj = NJ - j0
            G = gainr[:, :]
            SQ = V(0, (NJ, H * DH))
            y, sq, g = Y[:, j0:, :], SQ[:, 0:nj, :], gate[:, j0:, :]
            sums = ss[:, 0:nj * H]

            def sp(e):
                e.dma_start(G, gain[l].partition_broadcast(P)).then_inc(S("gain_in"), 16)

            def sc(e):
                e.activation(g, g, func).then_inc(S("gate_on"), 1)

            def ve(e, n):
                dve.step(e, e.tensor_tensor(sq, y, y, ALU.mult))
                e.tensor_reduce(sums.rearrange("p (j h) -> p j h", h=H), sq.rearrange("p j (h k) -> p j h k", h=H),
                                AX.X, ALU.add).then_inc(S("head_ss"), 1)
                e.wait_ge(S("gain_in"), 16 * n)
                dve.step(e, e.scalar_tensor_tensor(y, y, float(DH) ** 0.5, G.unsqueeze(1).broadcast_to([P, nj, H * DH]),
                                                   ALU.mult, ALU.mult))
                e.wait_ge(S("gate_on"), n)
                dve.step(e, e.tensor_tensor(y, y, g, ALU.mult))
                e.wait_ge(S("head_rs"), n)
                r = rs[:, 0:nj * H].rearrange("p (j h o) -> p j h o", h=H, o=1).broadcast_to([P, nj, H, DH])
                yh = y.rearrange("p j (h k) -> p j h k", h=H)
                dve.step(e, e.tensor_tensor(yh, yh, r, ALU.mult))

            def po(e, n):
                e.wait_ge(S("head_ss"), n)
                rsqrt(e, rs[:, 0:nj * H], sums, EPS * DH).then_inc(S("head_rs"), 1)

            return sp, sc, ve, po

        YM = TM[:, :, TM_V:TM_V + 256]

        def mlstm(l):
            QC = V(0, (4, T))
            KT = V(5120, (NJ, 256))
            VA = V(37600, (NJ, H, DH + 1))
            CS = V(40200, (NJ + 1, 4, 2 * (DH + 1)))
            W = V(7680, (2, H, P))
            PM = V(8704, (2, H, P))
            E2 = V(9728, (2, 2, P))
            gm = V(45920, (2, H, P))
            QP = V(46944, (2, 2, P))
            VW = [V(24800 + n * 520, (2, H, DH + 1)) for n in range(2)]
            Y1 = V(25840, (H, DH))
            sm = V(26112, (3600,))
            cw, cb = small[:, 16:28].rearrange("p (x w) -> p x w", w=3), small[:, 28:32]
            taken = [0]

            def take(k, parts=P):
                v = sm[0:parts, taken[0]:taken[0] + k]
                taken[0] += k
                return v

            def four(v):
                return v.rearrange("p (d i h) -> p d i h", d=2, h=H)

            GI, GF, AX_, LF, BS, GG = (V(47968 + 80 * n, (80,)) for n in range(6))
            GR, CM, NM = (take(256, 40).rearrange("p (d t) -> p d t", d=2) for _ in range(3))
            BR, GX = take(80, 1), take(80, 1)
            MM = take(88, 1).rearrange("p (d i h) -> p d i h", d=2, h=H)
            RR = take(160, 1)
            MC = take(2, 40)
            MB = take(160)
            CR = take(40)
            NC = take(80)
            EM, WK, WC = take(80), take(80), take(80)
            WH = take(40).rearrange("p (d i a) -> p d i a", d=2, a=2)
            DN_, RD = take(8), take(8)
            assert taken[0] <= 3600
            jo = 0 if l == 0 else JC
            nout = NJ - jo
            steps = NJ - 1
            ob = (0, NJ)[l]
            hn = head_norm(l, "ml", YM, TM[:, :, TM_OG:TM_OG + 256], ACT.Sigmoid, a["ml_norm_g"])

            def sp(e):
                for w in range(3):
                    e.dma_start(cw[:, :, w:w + 1], a["ml_conv_w"][l, w].rearrange("(x p o) -> p x o", p=P, o=1)).then_inc(S("conv_in"), 16)
                e.dma_start(cb, a["ml_conv_b"][l].rearrange("(x p) -> p x", p=P)).then_inc(S("conv_in"), 16)
                hn[0](e)

            def po(e):
                for G, o in ((GI, 0), (GF, 4)):
                    pool.did(e.tensor_copy(four(G)[:, 0], TM[:, :, TM_GATE + o:TM_GATE + o + 4]))
                for i, j in enumerate(ORDER[1]):
                    for G, o in ((GI, 0), (GF, 4)):
                        at = TM_GATE + 8 + o
                        ins = e.tensor_copy(four(G)[:, 1, i, :], TM[:, j, at:at + 4])
                        if (i, o) == (NJ - 1, 4):
                            ins.then_inc(S("ml_gates"), 1)
                        else:
                            pool.did(ins)
                pool.did(e.tensor_copy(VA[:, :, :, 0:DH], TM[:, :, TM_V:TM_V + 256].rearrange("p j (h k) -> p j h k", h=H)))
                pool.step(e, e.memset(VA[:, :, :, DH:DH + 1], 1.0))
                pool.step(e, e.memset(CS[:, :, :, :], 0.0))
                for x in (2, 3):
                    e.wait_ge(S("ml_silu"), 4 * l + x + 1)
                    e.tensor_scalar(QC[:, x, :], QC[:, x, :], DH ** -0.5, None, ALU.mult).then_inc(S("ml_k"), 1)
                e.wait_ge(S("ml_wk"), l + 1)
                for i in range(steps):
                    if i >= 2:
                        e.wait_ge(S("ml_u"), l * steps + i - 1)
                    for d in range(2):
                        w = four(WK)[:, d, i, :].unsqueeze(2).broadcast_to([P, H, DH + 1])
                        e.tensor_tensor(VW[i % 2][:, d], VA[:, ORDER[d][i]], w, ALU.mult).then_inc(S("ml_vw"), 1)
                for m, j in enumerate(range(jo, NJ)):
                    if m:
                        e.wait_ge(S("ml_e"), ob + m)
                    for d in range(2):
                        i = ORDER[d].index(j)
                        g = four(GG)[:, d, i, :].unsqueeze(2).broadcast_to([P, H, P])
                        mk = K(f"mask{d}").unsqueeze(1).broadcast_to([P, H, P])
                        e.tensor_tensor(gm[:, d], g, mk, ALU.add).then_inc(S("ml_gm"), 1)
                hn[3](e, 2 * l + 1)

            def sc(e):
                e.wait_ge(S("ml_ax"), l + 1)
                act.step(e, e.activation(AX_, AX_, ACT.Exp, scale=-1.0))
                e.activation(AX_, AX_, ACT.Ln, bias=1.0).then_inc(S("ml_ln"), 1)
                for x in range(4):
                    e.wait_ge(S("ml_conv"), 4 * l + x + 1)
                    e.activation(QC[:, x, :], QC[:, x, :], ACT.Silu).then_inc(S("ml_silu"), 1)
                for j in range(NJ):
                    e.wait_ge(S("ml_kt"), NJ * l + j + 1)
                    e.activation(KT[:, j, :], ps[:, 6 + j % 2, 0:256], ACT.Copy).then_inc(S("ml_kto"), 1)
                e.wait_ge(S("ml_small"), l + 1)
                act.did(e.activation(EM, EM, ACT.Exp))
                act.did(e.activation(WC, WC, ACT.Exp))
                e.activation(WK, WK, ACT.Exp).then_inc(S("ml_wk"), 1)
                for m in range(nout):
                    e.wait_ge(S("ml_e"), ob + m + 1)
                    e.activation(W[:, :, :, :], W[:, :, :, :], ACT.Exp).then_inc(S("ml_w"), 1)
                    e.activation(E2[:, :, :, :], E2[:, :, :, :], ACT.Exp).then_inc(S("ml_w"), 1)
                hn[1](e)

            def ve(e):
                e.wait_ge(S("ml_gates"), l + 1)
                e.scalar_tensor_tensor(AX_, GF, -1.0, GF, ALU.mult, ALU.max).then_inc(S("ml_ax"), 1)
                e.wait_ge(S("conv_in"), 64 * (l + 1))
                for x in range(4):
                    if x == 1:
                        e.wait_ge(S("ml_ln"), l + 1)
                        e.scalar_tensor_tensor(LF, GF, 0.0, AX_, ALU.min, ALU.subtract).then_inc(S("ml_lf"), 1)
                    raw, y = QKR[:, x, :], QC[:, x, :]
                    dve.step(e, e.tensor_scalar(y, raw, cw[:, x, 1:2], cb[:, x:x + 1], ALU.mult, ALU.add))
                    for s0, s1 in ((0, NCTX), (NCTX, T)):
                        dve.did(e.scalar_tensor_tensor(y[:, s0 + 1:s1], raw[:, s0:s1 - 1], cw[:, x, 0:1], y[:, s0 + 1:s1], ALU.mult, ALU.add))
                    dve.settle(e)
                    for s0, s1 in ((0, NCTX), (NCTX, T)):
                        ins = e.scalar_tensor_tensor(y[:, s0:s1 - 1], raw[:, s0 + 1:s1], cw[:, x, 2:3], y[:, s0:s1 - 1], ALU.mult, ALU.add)
                        if s0:
                            ins.then_inc(S("ml_conv"), 1)
                        else:
                            dve.did(ins)
                e.wait_ge(S("ml_conv"), 4 * (l + 1))
                e.wait_ge(S("ml_p"), 5 * l + 1)
                dve.did(e.tensor_copy(BS, ps[:, 0, 0:80]))
                dve.did(e.tensor_copy(BR, ps[0:1, 0, 128:208]))
                e.tensor_tensor(GG, GI, ps[:, 0, 0:80], ALU.subtract).then_inc(S("ml_g"), 1)
                e.wait_ge(S("ml_p"), 5 * l + 2)
                dve.step(e, e.tensor_copy(GR, ps[0:40, 1, 0:256].rearrange("p (d t) -> p d t", d=2)))
                for d in range(2):
                    ins = e.tensor_tensor_scan(CM[:, d, :], GR[:, d, :], GR[:, d, :], NEG, ALU.max, ALU.max)
                    ins.then_inc(S("ml_cm"), 1)
                dve.step(e, e.memset(MM[:, :, 0, :], 0.0))
                e.wait_ge(S("ml_p"), 5 * l + 3)
                dve.step(e, e.tensor_copy(GX, ps[0:1, 2, 0:80]))
                for d in range(2):
                    for h in range(H):
                        dve.did(e.tensor_tensor_scan(MM[:, d, 1:NJ + 1, h], four(GX)[:, d, :, h], four(BR)[:, d, :, h], 0.0, ALU.max, ALU.add))
                dve.settle(e)
                dve.step(e, e.tensor_copy(four(RR[:, 0:80]), MM[:, :, 0:NJ, :]))
                e.tensor_tensor(RR[:, 80:160], RR[:, 0:80], GX, ALU.max).then_inc(S("ml_rr"), 1)
                e.wait_ge(S("ml_p"), 5 * l + 4)
                dve.did(e.tensor_copy(MB, ps[:, 3, 0:160]))
                dve.did(e.tensor_copy(MC, ps[0:40, 3, 256:258]))
                dve.settle(e)
                for d in range(2):
                    e.tensor_scalar(NM[:, d, :], CM[:, d, :], MC[:, d:d + 1], -1.0, ALU.max, ALU.mult).then_inc(S("ml_nm"), 1)
                dve.did(e.tensor_tensor(WK, GG, MB[:, 80:160], ALU.subtract))
                dve.did(e.tensor_tensor(WC, MB[:, 0:80], MB[:, 80:160], ALU.subtract))
                e.wait_ge(S("ml_p"), 5 * l + 5)
                dve.did(e.tensor_copy(NC[:, 0:40], ps[:, 4, 0:40]))
                e.tensor_copy(CR, ps[:, 4, 64:104]).then_inc(S("ml_cr"), 1)
                e.wait_ge(S("ml_p2"), l + 1)
                dve.did(e.tensor_copy(NM[:, 1, :], ps[0:40, 5, 0:P]))
                dve.did(e.tensor_copy(NC[:, 40:80], ps[:, 5, 128:168]))
                dve.settle(e)
                e.tensor_tensor(EM, NC, BS, ALU.subtract).then_inc(S("ml_small"), 1)
                e.wait_ge(S("ml_wk"), l + 1)
                for b in range(2):
                    r = slice(64 * b, 64 * b + 64)
                    dve.did(e.tensor_copy(WH[r], WC.rearrange("p (d i a b) -> p d i a b", d=2, a=2, b=2)[r, :, :, :, b]))
                dve.settle(e)
                for i in range(steps):
                    w = WH[:, :, i, :].unsqueeze(3).broadcast_to([P, 2, 2, 2 * (DH + 1)])
                    dve.step(e, e.tensor_tensor(*(CS[:, k, :, :].rearrange("p (d a) q -> p d a q", d=2) for k in (i + 1, i)), w, ALU.mult))
                    e.wait_ge(S("ml_u"), l * steps + i + 1)
                    for d in range(2):
                        for b in range(2):
                            r = slice(64 * b, 64 * b + 64)
                            o = CS[r, i + 1, 2 * d:2 * d + 2, 65 * b:65 * b + 65]
                            u = ps[r, 2 * (i % 2) + d, 0:260].rearrange("p (a q) -> p a q", a=2)[:, :, 65 * b:65 * b + 65]
                            e.tensor_tensor(o, o, u, ALU.add).then_inc(S("ml_cs"), 1)
                    e.wait_ge(S("ml_cs"), 4 * (l * steps + i + 1))
                def finish(m, j):
                    for d in range(2):
                        e.wait_ge(S("ml_o"), 2 * (ob + m) + d + 1)
                        o = ps[:, 4 + d, 0:260].rearrange("p (h q) -> p h q", h=H)
                        dn = DN_[:, 4 * d:4 * d + 4]
                        dve.step(e, e.scalar_tensor_tensor(dn, o[:, :, DH], -1.0, four(EM)[:, d, ORDER[d].index(j), :], ALU.mult, ALU.max))
                        dve.did(e.tensor_tensor(dn, o[:, :, DH], dn, ALU.max))
                    dve.settle(e)
                    dve.step(e, e.reciprocal(RD, DN_))
                    for d in range(2):
                        o = ps[:, 4 + d, 0:260].rearrange("p (h q) -> p h q", h=H)
                        y = YM[:, j, :].rearrange("p (h k) -> p h k", h=H) if d == 0 else Y1
                        r = RD[:, 4 * d:4 * d + 4].unsqueeze(2).broadcast_to([P, H, DH])
                        ins = e.tensor_tensor(y, o[:, :, 0:DH], r, ALU.mult)
                        ins.then_inc(S("ml_od"), 1)
                    e.wait_ge(S("ml_od"), 2 * (ob + m + 1))
                    y = YM[:, j, :].rearrange("p (h k) -> p h k", h=H)
                    dve.step(e, e.tensor_tensor(y, y, Y1, ALU.add))

                for m, j in enumerate(range(jo, NJ)):
                    e.wait_ge(S("ml_gm"), 2 * (ob + m + 1))
                    e.wait_ge(S("ml_nmb"), ob + m + 1)
                    if m:
                        e.wait_ge(S("ml_pm"), 4 * (ob + m))
                    for d in range(2):
                        n4 = ps[:, 2 + d, :].rearrange("p (h t) -> p h t", h=H)
                        dve.did(e.tensor_tensor(W[:, d], gm[:, d], n4, ALU.add))
                        for b in range(2):
                            r = slice(64 * b, 64 * b + 64)
                            mp = MB[:, 0:80].rearrange("p (d i a b) -> p d i a b", d=2, a=2, b=2)[r, d, ORDER[d].index(j), :, b]
                            ins = e.tensor_tensor(E2[r, d], n4.rearrange("p (a b) t -> p a b t", b=2)[r, :, b, :],
                                                  mp.unsqueeze(2).broadcast_to([64, 2, P]), ALU.add)
                            if (d, b) == (1, 1):
                                ins.then_inc(S("ml_e"), 1)
                            else:
                                dve.did(ins)
                    if m:
                        finish(m - 1, j - 1)
                    e.wait_ge(S("ml_sco"), ob + m + 1)
                    e.wait_ge(S("ml_w"), 2 * (ob + m + 1))
                    for d in range(2):
                        pm, w = (X[:, d].rearrange("p (a b) t -> p b a t", b=2) for X in (PM, W))
                        sco = ps[:, 6 * (m % 2):6 * (m % 2) + 2, 0:256].rearrange("p b (a t) -> p b a t", a=2)
                        e.tensor_tensor(pm, w, sco, ALU.mult).then_inc(S("ml_pm"), 1)
                    for d in range(2):
                        e.tensor_tensor(QP[:, d], E2[:, d], QC[:, 0:2, j * P:(j + 1) * P], ALU.mult).then_inc(S("ml_pm"), 1)
                finish(nout - 1, NJ - 1)
                hn[2](e, 2 * l + 1)

            def pe(e):
                e.wait_ge(S("ml_lf"), l + 1)
                for d in range(2):
                    e.matmul(ps[:, 0, 40 * d:40 * d + 40], K("ge" if d else "le"), LF[:, 40 * d:40 * d + 40], start=True, stop=True)
                e.matmul(ps[0:1, 0, 128:208], ones[:, 0:1], LF, start=True, stop=True).then_inc(S("ml_p"), 1)
                e.wait_ge(S("ml_g"), l + 1)
                for d in range(2):
                    mm = e.matmul(ps[0:40, 1, P * d:P * d + P], GG[:, 40 * d:40 * d + 40], K("flip") if d else ident, start=True, stop=True)
                mm.then_inc(S("ml_p"), 1)
                e.wait_ge(S("ml_cm"), 2 * l + 2)
                for d in range(2):
                    mm = e.matmul(ps[0:1, 2, 40 * d:40 * d + 40], CM[:, d, P - 1:P], ident[0:40, 0:40], start=True, stop=True)
                mm.then_inc(S("ml_p"), 1)
                for j in range(NJ):
                    for x in range(2):
                        if j == 0:
                            e.wait_ge(S("ml_k"), 2 * l + x + 1)
                        elif j >= 2:
                            e.wait_ge(S("ml_kto"), NJ * l + j - 1)
                        mm = e.transpose(ps[:, 6 + j % 2, x * P:(x + 1) * P], QC[:, 2 + x, j * P:(j + 1) * P], ident)
                    mm.then_inc(S("ml_kt"), 1)
                e.wait_ge(S("ml_rr"), l + 1)
                e.matmul(ps[:, 3, 0:160], ones[0:1, :], RR, start=True, stop=True)
                for d in range(2):
                    mm = e.matmul(ps[0:40, 3, 256 + d:257 + d], RR[:, 40 * d:40 * d + 40], ones[0:1, 0:1], start=True, stop=True)
                mm.then_inc(S("ml_p"), 1)
                e.wait_ge(S("ml_nm"), 2 * l + 2)
                for d in range(2):
                    mm = e.transpose(ps[:, 4, 64 * d:64 * d + 40], NM[:, d, :], ident[0:40, 0:40])
                mm.then_inc(S("ml_p"), 1)
                e.wait_ge(S("ml_cr"), l + 1)
                e.matmul(ps[0:40, 5, 0:P], CR, K("flip"), start=True, stop=True)
                e.matmul(ps[:, 5, 128:168], K("flip"), CR, start=True, stop=True).then_inc(S("ml_p2"), 1)
                e.wait_ge(S("ml_kto"), NJ * (l + 1))
                for i in range(steps):
                    e.wait_ge(S("ml_vw"), 2 * (l * steps + i + 1))
                    if i >= 2:
                        e.wait_ge(S("ml_cs"), 4 * (l * steps + i - 1))
                    elif i == 0:
                        e.wait_ge(S("ml_small"), l + 1)
                    for d in range(2):
                        for x in range(2):
                            mm = e.matmul(ps[:, 2 * (i % 2) + d, 130 * x:130 * x + 130], KT[:, ORDER[d][i], x * P:(x + 1) * P],
                                          VW[i % 2][:, d, 2 * x:2 * x + 2, :], start=True, stop=True)
                    mm.then_inc(S("ml_u"), 1)
                e.wait_ge(S("ml_cs"), 4 * steps * (l + 1))

                def values(m, j):
                    for d in range(2):
                        i = ORDER[d].index(j)
                        if m:
                            e.wait_ge(S("ml_od"), 2 * (ob + m))
                        e.wait_ge(S("ml_pm"), 4 * (ob + m + 1))
                        for h in range(H):
                            o = ps[:, 4 + d, 65 * h:65 * h + 65]
                            e.matmul(o, PM[:, d, h, :], VA[:, j, h, :], start=h == 0, stop=False, skip_group_check=True)
                        for x in range(2):
                            mm = e.matmul(ps[:, 4 + d, 130 * x:130 * x + 130], QP[:, d, x, :], CS[:, i, 2 * d + x, :],
                                          start=False, stop=x == 1, skip_group_check=True)
                        mm.then_inc(S("ml_o"), 1)

                for m, j in enumerate(range(jo, NJ)):
                    if m:
                        e.wait_ge(S("ml_e"), ob + m)
                    for d in range(2):
                        i = ORDER[d].index(j)
                        for h in range(H):
                            q = 4 * i + h
                            mm = e.matmul(ps[:, 2 + d, h * P:(h + 1) * P], ident[0:40, q:q + 1].broadcast_to([40, P]), NM[:, d, :],
                                          start=True, stop=True)
                    mm.then_inc(S("ml_nmb"), 1)
                    if m >= 2:
                        e.wait_ge(S("ml_pm"), 4 * (ob + m - 1))
                    for h in range(H):
                        r = slice(64 * (h % 2), 64 * (h % 2) + 64)
                        mm = e.matmul(ps[:, 6 * (m % 2) + h % 2, (h // 2) * P:(h // 2 + 1) * P], QC[r, 2 + h // 2, j * P:(j + 1) * P], QC[r, h // 2, j * P:(j + 1) * P],
                                      start=True, stop=True)
                    mm.then_inc(S("ml_sco"), 1)
                    if m:
                        values(m - 1, j - 1)
                values(nout - 1, NJ - 1)

            stage(sync=sp, gpsimd=po, scalar=sc, vector=ve, tensor=pe)

        YH = V(32480, (NJ, 256))

        def hgrn(l):
            FH = V(0, (4, T))
            SH = V(5120, (4, T))
            Z = V(37600, (4, NJ, P + 1))
            SS = V(42760, (NJ, 4, P))
            L = [V(24800 + n * 1280, (T,)) for n in range(2)]
            LF = [V(27360 + n * 1280, (T,)) for n in range(2)]
            A = [V(24800 + n * 1024, (2, 4, P)) for n in range(2)]
            E = [V(26848 + n * 512, (4, P)) for n in range(2)]
            X = [V(27872 + n * 512, (4, P)) for n in range(2)]
            KP, KPT = X, [V(24800 + n * 1024, (4, P)) for n in range(2)]
            QP = [V(35040 + n * 512, (4, P)) for n in range(2)]
            AR = [V(36064 + n * 512, (4, P)) for n in range(2)]
            LG = small[:, 64:72].rearrange("p (l x) -> p l x", l=2)
            la, lc, lx, lm = (small[:, 72 + 4 * n:76 + 4 * n] for n in range(4))
            eT = small[:, 96:96 + 40].rearrange("p (x j) -> p x j", x=4)
            jo = 0 if l == 0 else JC
            nout, steps, NL = NJ - jo, NJ - 1, len(LEVELS)
            ob = (0, NJ)[l]
            hn = head_norm(l, "hg", YH, TM[:, :, TM_HG:TM_HG + 256], ACT.Silu, a["hg_norm_g"])

            def sp(e):
                for n in range(2):
                    for d in range(2):
                        e.dma_start(LG[:, n, 2 * d:2 * d + 2], a["hg_lb_logits"][n, d].rearrange("(a p) -> p a", p=P)).then_inc(S("lb_in"), 16)
                hn[0](e)

            def halves(v, m):
                w = v.rearrange("p x (b s m) -> p x b s m", s=2, m=m)
                return w[:, :, :, 0, :], w[:, :, :, 1, :]

            def po(e):
                e.memset(Z[:, :, :, 0:1], 0.0).then_inc(S("hg_zero"), 1)
                pool.did(e.memset(SS[:, :, :, :], 0.0))
                pool.did(e.tensor_copy(FH[:, 2:4, :], HQ[:, :, :]))
                pool.did(e.tensor_copy(SH[:, 0:2, :], HQ[:, :, :]))
                pool.settle(e)
                e.wait_ge(S("hg_z"), l + 1)
                for i in range(steps):
                    if i >= 2:
                        e.wait_ge(S("hg_kp"), 2 * (steps * l + i - 1))
                    j = ORDER[0][i]
                    z = Z[:, 0:2, j, :]
                    e.tensor_tensor(E[i % 2][:, 0:2, :], z[:, :, P:P + 1].broadcast_to([P, 2, P]), z[:, :, 1:P + 1], ALU.subtract).then_inc(S("hg_se"), 1)
                e.wait_ge(S("hg_ss"), 2 * steps * (l + 1))
                for m, j in enumerate(range(jo, NJ)):
                    b = m % 2
                    if m >= 2:
                        e.wait_ge(S("hg_o"), ob + m - 1)
                        pool.settle(e)
                    pool.did(e.tensor_copy(AR[b][:, 0:2, :], Z[:, 0:2, j, 1:P + 1]))
                    pool.did(e.tensor_copy(AR[b][:, 2:4, :], Z[:, 2:4, j, 0:P]))
                    z = Z[:, 2:4, j, :]
                    e.tensor_tensor(QP[b][:, 2:4, :], z[:, :, P:P + 1].broadcast_to([P, 2, P]), z[:, :, 0:P], ALU.subtract).then_inc(S("hg_qe"), 1)
                    pool.settle(e)
                    ar = AR[b]
                    for n, w in enumerate(LEVELS):
                        g = NL * (ob + m) + n
                        if NL * m + n >= 2:
                            e.wait_ge(S("hg_x"), g - 1)
                        r = Z[:, :, j, w:P:2 * w].unsqueeze(3).broadcast_to([P, 4, P // (2 * w), w])
                        (e0, e1), (a0, a1) = halves(E[g % 2], w), halves(ar, w)
                        pool.did(e.tensor_tensor(e0, r, a0, ALU.subtract))
                        e.tensor_tensor(e1, a1, r, ALU.subtract).then_inc(S("hg_e"), 1)
                hn[3](e, 2 * l + 2)

            ax_order = [(0, 0)]
            for x in range(4):
                ax_order += ([(x + 1, 0)] if x < 3 else []) + ([(x, 1)] if l else [])

            def sc(e):
                if l:
                    e.wait_ge(S("lb_ax"), 1)
                    act.step(e, e.activation(lx, lx, ACT.Exp, scale=-1.0))
                    e.activation(lx, lx, ACT.Ln, bias=1.0).then_inc(S("lb_ln"), 1)
                for x in range(4):
                    for half in range(l + 1):
                        e.wait_ge(S("hg_ax"), (0, 4)[l] + ax_order.index((x, half)) + 1)
                        act.step(e, e.activation(L[x % 2], L[x % 2], ACT.Exp, scale=-1.0))
                        e.activation(L[x % 2], L[x % 2], ACT.Ln, bias=1.0).then_inc(S("hg_ln"), 1)
                    e.wait_ge(S("hg_nk"), 4 * l + x + 1)
                    k = (FH if x < 2 else SH)[:, x, :]
                    if l:
                        e.wait_ge(S("lb_on"), 1)
                    e.activation(k, ZF[:, x, :], ACT.Exp, scale=-1.0, bias=lc[:, x:x + 1] if l else 0.0).then_inc(S("hg_k"), 1)
                e.wait_ge(S("hg_z"), l + 1)
                act.step(e, e.activation(eT, Z[:, :, :, P], ACT.Exp))
                for i in range(steps):
                    if i >= 2:
                        e.wait_ge(S("hg_kp"), 2 * (steps * l + i - 1))
                    e.wait_ge(S("hg_se"), steps * l + i + 1)
                    en = E[i % 2]
                    act.did(e.activation(en[:, 0:2, :], en[:, 0:2, :], ACT.Exp))
                    e.activation(en[:, 2:4, :], Z[:, 2:4, ORDER[1][i], 0:P], ACT.Exp).then_inc(S("hg_sx"), 1)
                    e.wait_ge(S("hg_kt"), steps * l + i + 1)
                    if i >= 2:
                        e.wait_ge(S("hg_u"), steps * l + i - 1)
                    e.activation(KPT[i % 2][:, :, :], ps[:, i % 2, :].rearrange("p (x t) -> p x t", x=4), ACT.Copy).then_inc(S("hg_kto"), 1)
                e.wait_ge(S("hg_ss"), 2 * steps * (l + 1))
                for m, j in enumerate(range(jo, NJ)):
                    b = m % 2
                    e.wait_ge(S("hg_qe"), ob + m + 1)
                    act.did(e.activation(QP[b][:, 2:4, :], QP[b][:, 2:4, :], ACT.Exp))
                    e.activation(QP[b][:, 0:2, :], AR[b][:, 0:2, :], ACT.Exp).then_inc(S("hg_qx"), 1)
                    for n in range(NL):
                        g = NL * (ob + m) + n
                        e.wait_ge(S("hg_e"), g + 1)
                        if NL * m + n >= 2:
                            gg = (NL + 1) * (ob + (NL * m + n - 2) // NL) + (n - 2) % NL + 1
                            e.wait_ge(S("hg_g"), gg + 1)
                        e.activation(X[g % 2][:, :, :], E[g % 2][:, :, :], ACT.Exp).then_inc(S("hg_x"), 1)
                    if m:
                        out_copy(e, m - 1, j - 1)
                out_copy(e, nout - 1, NJ - 1)
                hn[1](e)

            def out_copy(e, m, j):
                e.wait_ge(S("hg_o"), ob + m + 1)
                e.activation(YH[:, j, :], ps[:, 4 + m % 2, 0:256], ACT.Copy).then_inc(S("hg_y"), 1)

            def ve(e):
                if l:
                    e.wait_ge(S("lb_in"), 64 * 2)
                    dve.step(e, e.tensor_tensor(lm, LG[:, 1, :], LG[:, 0, :], ALU.subtract))
                    e.scalar_tensor_tensor(lx, lm, -1.0, lm, ALU.mult, ALU.max).then_inc(S("lb_ax"), 1)
                    e.wait_ge(S("lb_ln"), 1)
                    dve.did(e.scalar_tensor_tensor(la, lm, 0.0, lx, ALU.min, ALU.subtract))
                    dve.step(e, e.tensor_scalar(lc, lm, -1.0, 0.0, ALU.mult, ALU.min))
                    dve.step(e, e.tensor_tensor(lc, lc, lx, ALU.subtract))
                    e.tensor_tensor(lm, lc, la, ALU.subtract).then_inc(S("lb_on"), 1)
                    e.wait_ge(S("lb_on"), 1)
                def gate_abs(x):
                    e.scalar_tensor_tensor(L[x % 2], ZF[:, x, :], -1.0, ZF[:, x, :], ALU.mult, ALU.max).then_inc(S("hg_ax"), 1)

                gate_abs(0)
                for x in range(4):
                    z, ln, lf = ZF[:, x, :], L[x % 2], LF[x % 2]
                    nln = (0, 4)[l] + (l + 1) * x
                    if x < 3:
                        if x:
                            e.wait_ge(S("hg_nk"), 4 * l + x)
                        gate_abs(x + 1)
                    e.wait_ge(S("hg_ln"), nln + 1)
                    dve.step(e, e.scalar_tensor_tensor(lf, z, 0.0, ln, ALU.min, ALU.subtract))
                    e.scalar_tensor_tensor(z, z, 0.0, ln, ALU.max, ALU.add).then_inc(S("hg_nk"), 1)
                    if l:
                        e.wait_ge(S("hg_nk"), 4 * l + x + 1)
                        dve.step(e, e.tensor_scalar(ln, lf, lm[:, x:x + 1], None, ALU.add))
                        e.scalar_tensor_tensor(ln, ln, -1.0, ln, ALU.mult, ALU.max).then_inc(S("hg_ax"), 1)
                        dve.step(e, e.tensor_scalar(lf, lf, lc[:, x:x + 1], la[:, x:x + 1], ALU.add, ALU.max))
                        e.wait_ge(S("hg_ln"), nln + 2)
                        dve.step(e, e.tensor_tensor(lf, lf, ln, ALU.add))
                    if x == 0:
                        e.wait_ge(S("hg_zero"), l + 1)
                    for j in range(NJ):
                        dve.did(e.tensor_tensor_scan(Z[:, x, j, 1:P + 1], ones, lf[:, j * P:(j + 1) * P], 0.0, ALU.mult, ALU.add))
                    dve.settle(e)
                e.engine_nop().then_inc(S("hg_z"), 1)
                e.wait_ge(S("hg_k"), 4 * (l + 1))
                for i in range(steps):
                    e.wait_ge(S("hg_sx"), steps * l + i + 1)
                    if i >= 2:
                        e.wait_ge(S("hg_kt"), steps * l + i - 1)
                    for d, F_ in enumerate((FH, SH)):
                        j = ORDER[d][i]
                        r = slice(2 * d, 2 * d + 2)
                        e.tensor_tensor(KP[i % 2][:, r, :], E[i % 2][:, r, :], F_[:, r, j * P:(j + 1) * P], ALU.mult).then_inc(S("hg_kp"), 1)
                    for d in range(2):
                        r = slice(2 * d, 2 * d + 2)
                        w = eT[:, r, ORDER[d][i]].unsqueeze(2).broadcast_to([P, 2, P])
                        dve.did(e.tensor_tensor(SS[:, i + 1, r, :], SS[:, i, r, :], w, ALU.mult))
                    dve.settle(e)
                    e.wait_ge(S("hg_u"), steps * l + i + 1)
                    for b in range(2):
                        r, q = slice(64 * b, 64 * b + 64), slice(64 * b, 64 * b + 64)
                        o = SS[r, i + 1, :, q]
                        e.tensor_tensor(o, o, ps[r, 2 + i % 2, :].rearrange("p (x v) -> p x v", x=4)[:, :, q], ALU.add).then_inc(S("hg_ss"), 1)
                    e.wait_ge(S("hg_ss"), 2 * (steps * l + i + 1))

                def take(m, n):
                    g = (NL + 1) * (ob + m) + n
                    e.wait_ge(S("hg_g"), g + 1)
                    Am, bank = A[m % 2], 2 * (g % 2)
                    if n == 0:
                        if m >= 2:
                            e.wait_ge(S("hg_o"), ob + m - 1)
                        src = ps[:, bank:bank + 2, :].rearrange("p b (x t) -> p b x t", x=4)
                        for b in range(2):
                            ins = e.tensor_tensor(Am[:, b], src[:, b], ident.unsqueeze(1).broadcast_to([P, 4, P]), ALU.mult)
                            ins.then_inc(S("hg_c"), 1)
                    else:
                        mask = K(f"lvl{LEVELS[n - 1]}").bitcast(U32).rearrange("p (d t) -> p d t", d=2).unsqueeze(2).broadcast_to([P, 2, 2, P])
                        e.wait_ge(S("hg_c"), 2 * g)
                        for b in range(2):
                            e.copy_predicated(Am[:, b].rearrange("p (d a) t -> p d a t", d=2), mask,
                                              ps[:, bank + b, :].rearrange("p (d a t) -> p d a t", d=2, a=2)).then_inc(S("hg_c"), 1)

                for m, j in enumerate(range(jo, NJ)):
                    tok = slice(j * P, (j + 1) * P)
                    e.wait_ge(S("hg_qx"), ob + m + 1)
                    qp = QP[m % 2].rearrange("p (d a) t -> p d a t", d=2)
                    e.tensor_tensor(qp, qp, FH[:, 2:4, tok].unsqueeze(1).broadcast_to([P, 2, 2, P]), ALU.mult).then_inc(S("hg_qp"), 1)
                    for n, w in enumerate(LEVELS):
                        g = NL * (ob + m) + n
                        e.wait_ge(S("hg_x"), g + 1)
                        (x0, x1), (f0, _), (_, s1) = halves(X[g % 2], w), halves(FH[:, :, tok], w), halves(SH[:, :, tok], w)
                        dve.did(e.tensor_tensor(x0, x0, f0, ALU.mult))
                        e.tensor_tensor(x1, x1, s1, ALU.mult).then_inc(S("hg_xm"), 1)
                        take(m, n)
                    take(m, NL)
                e.wait_ge(S("hg_y"), ob + nout)
                hn[2](e, 2 * l + 2)

            def pe(e):
                for i in range(steps):
                    e.wait_ge(S("hg_kp"), 2 * (steps * l + i + 1))
                    if i >= 2:
                        e.wait_ge(S("hg_kto"), steps * l + i - 1)
                    for x in range(4):
                        mm = e.transpose(ps[:, i % 2, x * P:(x + 1) * P], KP[i % 2][:, x, :], ident)
                    mm.then_inc(S("hg_kt"), 1)
                    e.wait_ge(S("hg_kto"), steps * l + i + 1)
                    if i >= 2:
                        e.wait_ge(S("hg_ss"), 2 * (steps * l + i - 1))
                    for x in range(4):
                        v = TM[:, ORDER[x // 2][i], TM_HI + P * (x % 2):TM_HI + P * (x % 2) + P]
                        mm = e.matmul(ps[:, 2 + i % 2, x * P:(x + 1) * P], KPT[i % 2][:, x, :], v, start=True, stop=True)
                    mm.then_inc(S("hg_u"), 1)
                e.wait_ge(S("hg_ss"), 2 * steps * (l + 1))

                def gram(m, n, lhs, rhs):
                    g = (NL + 1) * (ob + m) + n
                    if (NL + 1) * m + n >= 2:
                        e.wait_ge(S("hg_c"), 2 * (g - 1))
                    for x in range(4):
                        for b in range(2):
                            r = slice(64 * b, 64 * b + 64)
                            mm = e.matmul(ps[:, 2 * (g % 2) + b, x * P:(x + 1) * P], lhs(x)[r], rhs(x)[r], start=True, stop=True)
                    mm.then_inc(S("hg_g"), 1)

                def values(m, j):
                    if m >= 2:
                        e.wait_ge(S("hg_y"), ob + m - 1)
                    e.wait_ge(S("hg_qp"), ob + m + 1)
                    e.wait_ge(S("hg_c"), 2 * (NL + 1) * (ob + m + 1))
                    o = ps[:, 4 + m % 2, :]
                    for h in range(H):
                        for d in range(2):
                            v = TM[:, j, TM_HI + 64 * h:TM_HI + 64 * h + 64]
                            e.matmul(o[:, 64 * h:64 * h + 64], A[m % 2][:, h % 2, 2 * d + h // 2, :], v, start=h == 0 and d == 0, stop=False,
                                     skip_group_check=True)
                    for x in range(4):
                        i = ORDER[x // 2].index(j)
                        mm = e.matmul(o[:, P * (x % 2):P * (x % 2) + P], QP[m % 2][:, x, :], SS[:, i, x, :], start=False, stop=x == 3,
                                      skip_group_check=True)
                    mm.then_inc(S("hg_o"), 1)

                for m, j in enumerate(range(jo, NJ)):
                    tok = slice(j * P, (j + 1) * P)
                    gram(m, 0, lambda x: (FH if x < 2 else SH)[:, x, tok], lambda x: FH[:, 2 + x % 2, tok])
                    if m:
                        values(m - 1, j - 1)
                    for n in range(NL):
                        g = NL * (ob + m) + n
                        e.wait_ge(S("hg_xm"), g + 1)
                        gram(m, n + 1, lambda x: X[g % 2][:, x, :], lambda x: X[g % 2][:, x, :])
                values(nout - 1, NJ - 1)

            stage(sync=sp, gpsimd=po, scalar=sc, vector=ve, tensor=pe)

        def cum_all(l):
            return MH * sum(-(-(NCTX if j < JC else T) // 512) for j in range(0 if l == 0 else JC, NJ))

        def mla(l):
            QT = V(0, (MH, T))
            KT = V(37600, (MH, T))
            VV = V(24800, (NJ, MH, DV))
            wq = V(35040, (2, MH * DQK))
            wkv = V(36576, (MH * (DN + DV),))
            CT = V(29920, (3, P))
            XQ = [TM[:, j, 256:256 + MH * DQK].rearrange("p (h q) -> p h q", h=MH) for j in range(NJ)]
            XK = [V(30304 + 768 * n, (MH, DQK)) for n in range(2)]
            SQ = V(47840, (MH, DQK))
            RT = V(31840, (MH, DR))
            PB = [V(29920 + n * 1280, (T,)) for n in range(2)]
            PT = [V(35040 + n * 1280, (NJ, P)) for n in range(2)]
            gq, gkv = small[:, 0:2], small[:, 2:3]
            gains = {"q": gainr[:, 0:DQK], "k": gainr[:, DQK:2 * DQK]}
            sx, rx = small[:, 8:16], small[:, 16:24]
            mx, sm = (small[:, 32 + 8 * n:40 + 8 * n].rearrange("p (b k) -> p b k", k=4) for n in range(2))
            nm, rc = (small[:, 24 + 2 * n:26 + 2 * n] for n in range(2))
            cs, cr = ss[:, 0:2 * NJ].rearrange("p (c j) -> p c j", c=2), rs[:, 0:2 * NJ].rearrange("p (c j) -> p c j", c=2)
            parts = ((TM_CQ, 256), (TM_CKV, 128))
            jo = 0 if l == 0 else JC
            items = [(j, w) for j in range(NJ) for w in "qk" if w == "k" or j >= jo]
            ib = (0, 2 * NJ)[l]
            widths = [(NCTX if j < JC else T) for j in range(jo, NJ) for h in range(MH)]
            banks = [[(k, min(512, w - 512 * k)) for k in range(-(-w // 512))] for w in widths]
            cum = [sum(len(x) for x in banks[:n]) for n in range(len(banks) + 1)]
            bb = (0, cum_all(0))[l]
            at = [(j, h) for j in range(jo, NJ) for h in range(MH)]
            ab = (0, NJ * MH)[l]

            def sp(e):
                e.dma_start(wq, a["mla_w_uq"][l].rearrange("(k p) n -> p k n", p=P)).then_inc(S("la_in"), 16)
                e.dma_start(wkv, a["mla_w_ukv"][l]).then_inc(S("la_in"), 16)
                e.dma_start(gq, a["mla_q_norm_g"][l].rearrange("(k p) -> p k", p=P)).then_inc(S("la_in"), 16)
                e.dma_start(gkv, a["mla_kv_norm_g"][l].rearrange("(p o) -> p o", o=1)).then_inc(S("la_in"), 16)
                for w, g in (("q", "mla_q_qk_g"), ("k", "mla_k_qk_g")):
                    e.dma_start(gains[w], a[g][l].partition_broadcast(P)).then_inc(S("la_in"), 16)

            def sc(e):
                for c_, (o, w) in enumerate(parts):
                    for j in range(NJ):
                        act.step(e, e.activation(SQ.rearrange("p a b -> p (a b)")[:, 0:w], TM[:, j, o:o + w], ACT.Square,
                                                 accum_out=cs[:, c_, j:j + 1]))
                e.activation(small[:, 3:4], cs[:, 0, 0:1], ACT.Copy).then_inc(S("la_ss"), 1)
                columns(e, 0)
                for j in range(NJ):
                    n = NJ * l + j
                    e.wait_ge(S("la_mm"), n + 1)
                    if j >= 2:
                        e.wait_ge(S("la_xt"), ib + items.index((j - 2, "k")) + 1)
                    for b in range(2):
                        kv = ps[:, 3 + b, :].rearrange("p (h q) -> p h q", h=4)
                        if j >= jo:
                            act.did(e.activation(XQ[j][:, 4 * b:4 * b + 4, :], ps[:, 1 + b, 0:384].rearrange("p (h q) -> p h q", h=4), ACT.Copy))
                        e.activation(VV[:, j, 4 * b:4 * b + 4, :], kv[:, :, DN:DN + DV], ACT.Copy).then_inc(S("la_cp"), 1)
                        e.activation(XK[j % 2][:, 4 * b:4 * b + 4, 0:DN], kv[:, :, 0:DN], ACT.Copy).then_inc(S("la_cp"), 1)
                    if j + 1 < NJ:
                        columns(e, j + 1)
                    for it in [x for x in items if x[0] == j]:
                        m = ib + items.index(it)
                        if it[1] == "k":
                            e.wait_ge(S("la_kr"), n + 1)
                            e.wait_ge(S("la_cp"), 4 * (n + 1))
                        act.settle(e)
                        if m > ib:
                            e.wait_ge(S("la_s"), m)
                        e.activation(SQ, buf(it), ACT.Square).then_inc(S("la_sq"), 1)
                        if j and (j - 1, it[1]) in items:
                            evac(e, [(j - 1, it[1])])
                evac(e, [x for x in items if x[0] == NJ - 1])
                for n, (j, h) in enumerate(at):
                    nk = NCTX if j < JC else T
                    e.wait_ge(S("at_m"), ab + n + 1)
                    if n >= 2:
                        e.wait_ge(S("at_t"), ab + n - 1)
                    for k, w in banks[n]:
                        e.activation(PB[n % 2][:, 512 * k:512 * k + w], ps[:, k, 0:w], ACT.Exp, bias=nm[:, n % 2:n % 2 + 1],
                                     scale=DQK ** 0.5, accum_out=sm[:, n % 2, k:k + 1]).then_inc(S("at_e"), 1)
                    if n:
                        turn(e, n - 1)
                turn(e, len(at) - 1)

            def columns(e, j):
                n = NJ * l + j
                e.wait_ge(S("la_t"), n + 1)
                if j:
                    e.wait_ge(S("la_mm"), n)
                e.activation(CT, ps[:, 0, 0:384].rearrange("p (k t) -> p k t", k=3), ACT.Copy).then_inc(S("la_ct"), 1)

            def buf(it):
                return XQ[it[0]] if it[1] == "q" else XK[it[0] % 2]

            def turn(e, n):
                nk = NCTX if at[n][0] < JC else T
                e.wait_ge(S("at_t"), ab + n + 1)
                if n >= 2:
                    e.wait_ge(S("at_o"), ab + n - 1)
                e.activation(PT[n % 2][:, 0:nk // P, :].rearrange("p k t -> p (k t)"), flat(3, nk), ACT.Copy).then_inc(S("at_pt"), 1)

            def evac(e, its):
                for it in its:
                    n = ib + items.index(it)
                    e.wait_ge(S("la_xt"), n + 1)
                    dst = (QT if it[1] == "q" else KT)[0:DQK, :, it[0] * P:(it[0] + 1) * P]
                    e.activation(dst, ps[0:DQK, 5:7, :].rearrange("p b (h t) -> p (b h) t", h=4), ACT.Copy).then_inc(S("la_xo"), 1)

            def flat(b, n):
                return ps[:, b:b + 3, :].rearrange("p b c -> p (b c)")[:, 0:n]

            def po(e):
                e.wait_ge(S("la_ss"), l + 1)
                for c_, (o, w) in enumerate(parts):
                    ins = rsqrt(e, cr[:, c_, :], cs[:, c_, :], EPS * w)
                    ins.then_inc(S("la_rs"), 1)
                for n, (j, w) in enumerate(items):
                    if n == 0 or items[n - 1][0] != j:
                        if j >= 2:
                            e.wait_ge(S("la_xt"), ib + items.index((j - 2, "k")) + 1)
                        kr = TM[:, j, TM_KR:TM_KR + DR].unsqueeze(1).broadcast_to([P, MH, DR])
                        e.tensor_copy(XK[j % 2][:, :, DN:DQK], kr).then_inc(S("la_kr"), 1)
                    e.wait_ge(S("la_s"), ib + n + 1)
                    if n:
                        e.wait_ge(S("la_x"), ib + n)
                    rsqrt(e, rx, sx, EPS * DQK).then_inc(S("la_r"), 1)

            def ve(e):
                e.wait_ge(S("la_in"), 96 * (l + 1))
                for k in range(2):
                    e.tensor_scalar(wq[:, k, :], wq[:, k, :], gq[:, k:k + 1], None, ALU.mult).then_inc(S("la_w"), 1)
                e.tensor_scalar(wkv, wkv, gkv, None, ALU.mult).then_inc(S("la_w"), 1)
                e.wait_ge(S("la_rs"), 2 * (l + 1))
                for j in range(NJ):
                    for c_, (o, w) in enumerate(parts):
                        v = TM[:, j, o:o + w]
                        e.tensor_scalar(v, v, cr[:, c_, j:j + 1], float(w) ** 0.5, ALU.mult, ALU.mult).then_inc(S("la_c"), 1)
                for n, (j, w) in enumerate(items):
                    X = buf((j, w))
                    e.wait_ge(S("la_sq"), ib + n + 1)
                    e.tensor_reduce(sx, SQ, AX.X, ALU.add).then_inc(S("la_s"), 1)
                    dve.step(e, e.tensor_tensor(X, X, gains[w].unsqueeze(1).broadcast_to([P, MH, DQK]), ALU.mult))
                    if j >= JC:
                        cos, sin = ropes[:, j - JC, 0:DR], ropes[:, j - JC, DR:2 * DR]
                        xr = X[:, :, DN:DQK]
                        x4, t4 = (v.rearrange("p h (g s q) -> p h g s q", g=2, s=2) for v in (xr, RT))
                        s4 = sin.rearrange("p (g s q) -> p g s q", g=2, s=2)
                        for s in range(2):
                            dve.did(e.tensor_tensor(t4[:, :, :, s, :], x4[:, :, :, 1 - s, :],
                                                    s4[:, :, s, :].unsqueeze(1).broadcast_to([P, MH, 2, 8]), ALU.mult))
                        dve.settle(e)
                        dve.step(e, e.tensor_tensor(xr, xr, cos.unsqueeze(1).broadcast_to([P, MH, DR]), ALU.mult))
                        dve.step(e, e.tensor_tensor(xr, xr, RT, ALU.add))
                    e.wait_ge(S("la_r"), ib + n + 1)
                    e.tensor_tensor(X, X, rx.unsqueeze(2).broadcast_to([P, MH, DQK]), ALU.mult).then_inc(S("la_x"), 1)

                def scale(n):
                    nk = NCTX if at[n][0] < JC else T
                    b = n % 2
                    e.wait_ge(S("at_e"), bb + cum[n + 1])
                    if len(banks[n]) > 1:
                        dve.step(e, e.tensor_reduce(sm[:, b, 3:4], sm[:, b, 0:len(banks[n])], AX.X, ALU.add))
                    total = sm[:, b, 3:4] if len(banks[n]) > 1 else sm[:, b, 0:1]
                    dve.step(e, e.reciprocal(rc[:, b:b + 1], total))
                    e.tensor_scalar(PB[b][:, 0:nk], PB[b][:, 0:nk], rc[:, b:b + 1], None, ALU.mult).then_inc(S("at_p"), 1)

                def head_out(n):
                    j, h = at[n]
                    if h % 2:
                        e.wait_ge(S("at_o"), ab + n + 1)
                        y = TM[:, j, 256 + P * (h // 2):256 + P * (h // 2) + P]
                        e.tensor_copy(y, ps[:, 6 + (n // 2) % 2, 0:P]).then_inc(S("at_y"), 1)

                for n, (j, h) in enumerate(at):
                    nk = NCTX if j < JC else T
                    b = n % 2
                    for k, w in banks[n]:
                        e.wait_ge(S("at_s"), bb + cum[n] + k + 1)
                        dve.did(e.tensor_reduce(mx[:, b, k:k + 1], ps[:, k, 0:w], AX.X, ALU.max))
                    dve.settle(e)
                    top = mx[:, b, 0:1]
                    if len(banks[n]) > 1:
                        top = mx[:, b, 3:4]
                        dve.step(e, e.tensor_reduce(top, mx[:, b, 0:len(banks[n])], AX.X, ALU.max))
                    if n >= 2:
                        e.wait_ge(S("at_e"), bb + cum[n - 1])
                    e.tensor_scalar(nm[:, b:b + 1], top, -(DQK ** 0.5), None, ALU.mult).then_inc(S("at_m"), 1)
                    scale(n)
                    if n >= 2:
                        head_out(n - 2)
                head_out(len(at) - 1)

            def pe(e):
                e.wait_ge(S("la_w"), 3 * (l + 1))

                def turned(j):
                    n = NJ * l + j
                    e.wait_ge(S("la_c"), 2 * (n + 1))
                    if j:
                        e.wait_ge(S("la_ct"), n)
                    for k in range(3):
                        mm = e.transpose(ps[:, 0, k * P:(k + 1) * P], TM[:, j, TM_CQ + k * P:TM_CQ + (k + 1) * P], ident)
                    mm.then_inc(S("la_t"), 1)

                def front(j):
                    n = NJ * l + j
                    e.wait_ge(S("la_ct"), n + 1)
                    if j:
                        e.wait_ge(S("la_cp"), 4 * n)
                    for b in range(2):
                        if j >= jo:
                            for k in range(2):
                                e.matmul(ps[:, 1 + b, 0:384], CT[:, k, :], wq[:, k, 384 * b:384 * b + 384], start=k == 0, stop=k == 1)
                        mm = e.matmul(ps[:, 3 + b, :], CT[:, 2, :], wkv[:, 512 * b:512 * b + 512], start=True, stop=True)
                    mm.then_inc(S("la_mm"), 1)
                    if j + 1 < NJ:
                        turned(j + 1)

                def back(j):
                    for it in [x for x in items if x[0] == j]:
                        n = ib + items.index(it)
                        e.wait_ge(S("la_x"), n + 1)
                        if n > ib:
                            e.wait_ge(S("la_xo"), n)
                        for h in range(MH):
                            mm = e.transpose(ps[0:DQK, 5 + h // 4, P * (h % 4):P * (h % 4) + P], buf(it)[:, h, :], ident)
                        mm.then_inc(S("la_xt"), 1)

                turned(0)
                front(0)
                for j in range(1, NJ):
                    front(j)
                    back(j - 1)
                back(NJ - 1)
                e.wait_ge(S("la_xo"), ib + len(items))

                def scores(n):
                    j, h = at[n]
                    for k, w in banks[n]:
                        if n:
                            e.wait_ge(S("at_e"), bb + cum[n - 1] + min(k + 1, len(banks[n - 1])))
                        e.matmul(ps[:, k, 0:w], QT[0:DQK, h, j * P:(j + 1) * P], KT[0:DQK, h, 512 * k:512 * k + w], start=True, stop=True)\
                         .then_inc(S("at_s"), 1)

                def outs(n):
                    j, h = at[n]
                    nk = (NCTX if j < JC else T) // P
                    e.wait_ge(S("at_pt"), ab + n + 1)
                    pair = (ab + n) // 2
                    if h % 2 == 0 and pair - ab // 2 >= 2:
                        e.wait_ge(S("at_y"), pair - 1)
                    r = slice(64 * (h % 2), 64 * (h % 2) + 64)
                    if h % 2:
                        e.wait_ge(S("at_o"), ab + n)
                    for k in range(nk):
                        mm = e.matmul(ps[r, 6 + (n // 2) % 2, 0:P], VV[:, k, h, :], PT[n % 2][:, k, :], start=k == 0, stop=k == nk - 1)
                    mm.then_inc(S("at_o"), 1)

                scores(0)
                for n, (j, h) in enumerate(at):
                    nk = (NCTX if j < JC else T) // P
                    if n + 1 < len(at):
                        scores(n + 1)
                    e.wait_ge(S("at_p"), ab + n + 1)
                    if n:
                        e.wait_ge(S("at_pt"), ab + n)
                    for k in range(nk):
                        mm = e.transpose(ps[:, 3 + k // 4, P * (k % 4):P * (k % 4) + P], PB[n % 2][:, k * P:(k + 1) * P], ident)
                    mm.then_inc(S("at_t"), 1)
                    if n:
                        outs(n - 1)
                outs(len(at) - 1)

            stage(sync=sp, gpsimd=po, scalar=sc, vector=ve, tensor=pe)

        def wout(l):
            wo = V(0, (KD, D))
            G1 = V(8192, (2, D))
            yt = [V(37600 + n * 512, (4, P)) for n in range(2)]
            xt = [V(38624 + n * 1024, (D,)) for n in range(2)]
            pt = [V(40672 + n * 1024, (D,)) for n in range(2)]
            jo = 0 if l == 0 else JC
            nout = NJ - jo
            ob = (0, NJ)[l]

            def tile_of(j, src):
                if src and l == 0:
                    t, q = (a["ctx"][0], j) if j < JC else (a["x"][0], j - JC)
                elif not src and l == 1:
                    t, q = out[0], j - JC
                else:
                    t, q = xres, j
                return t[q * P:(q + 1) * P, :]

            def sp(e):
                e.dma_start(wo, a["w_out"][l].rearrange("(k p) n -> p k n", p=P)).then_inc(S("wo_in"), 16)
                for s in range(2):
                    e.dma_start(G1[:, s, :], modd[2 * l + s, 2 * D:3 * D].partition_broadcast(P)).then_inc(S("wo_in"), 16)
                def store(m, j):
                    e.wait_ge(S("wo_x"), ob + m + 1)
                    e.dma_start(tile_of(j, False), xt[m % 2]).then_inc(S(f"wo_st{m % 2}"), 16)
                for m, j in enumerate(range(jo, NJ)):
                    if m >= 2:
                        e.wait_ge(S(f"wo_st{m % 2}"), 16 * (ob // 2 + m // 2))
                    e.dma_start(xt[m % 2], tile_of(j, True)).then_inc(S(f"wo_ld{m % 2}"), 16)
                    if m:
                        store(m - 1, j - 1)
                store(nout - 1, NJ - 1)
                for b in range(2):
                    e.wait_ge(S(f"wo_st{b}"), 16 * (ob + nout) // 2)

            def pe(e):
                def prod(m, j):
                    e.wait_ge(S("wo_y"), ob + m + 1)
                    if m == 0:
                        e.wait_ge(S("wo_in"), 48 * (l + 1))
                    if m >= 2:
                        e.wait_ge(S("wo_p"), ob + m - 1)
                    for n in range(2):
                        for k in range(KD):
                            y = yt[m % 2][:, k, :] if k < 4 else TM[:, j, 256 + P * (k - 4):256 + P * (k - 3)]
                            mm = e.matmul(ps[:, 2 + 2 * (m % 2) + n, :], y, wo[:, k, n * 512:(n + 1) * 512], start=k == 0, stop=k == KD - 1)
                    mm.then_inc(S("wo_mm"), 1)
                for m, j in enumerate(range(jo, NJ)):
                    if m >= 2:
                        e.wait_ge(S("wo_y"), ob + m - 1)
                    for k in range(4):
                        y = (YM if k < 2 else YH)[:, j, P * (k % 2):P * (k % 2) + P]
                        mm = e.transpose(ps[:, m % 2, k * P:(k + 1) * P], y, ident)
                    mm.then_inc(S("wo_t"), 1)
                    if m:
                        prod(m - 1, j - 1)
                prod(nout - 1, NJ - 1)

            def sc(e):
                for m in range(nout):
                    e.wait_ge(S("wo_t"), ob + m + 1)
                    if m >= 2:
                        e.wait_ge(S("wo_mm"), ob + m - 1)
                    e.activation(yt[m % 2], ps[:, m % 2, :].rearrange("p (k t) -> p k t", k=4), ACT.Copy).then_inc(S("wo_y"), 1)

            def ve(e):
                for m, j in enumerate(range(jo, NJ)):
                    e.wait_ge(S("wo_mm"), ob + m + 1)
                    if m >= 2:
                        e.wait_ge(S("wo_x"), ob + m - 1)
                    b = 2 + 2 * (m % 2)
                    e.tensor_tensor(pt[m % 2], ps[:, b:b + 2, :].rearrange("p b c -> p (b c)"), G1[:, 0 if j < JC else 1, :], ALU.mult)\
                     .then_inc(S("wo_p"), 1)
                    e.wait_ge(S("wo_p"), ob + m + 1)
                    e.wait_ge(S(f"wo_ld{m % 2}"), 16 * (ob // 2 + m // 2 + 1))
                    e.tensor_tensor(xt[m % 2], xt[m % 2], pt[m % 2], ALU.add).then_inc(S("wo_x"), 1)

            stage(sync=sp, tensor=pe, scalar=sc, vector=ve)

        EXPERT_W = [V(19456 + 8192 * n, (KD, D)) for n in range(3)]
        HEAD = 1

        def load_up(e, l, i, h, over):
            if over:
                e.wait_ge(S("ff_gu"), i * 8 + (8 * NE * l - 8 + 4 * (h + 1)))
            for w, src in ((EXPERT_W[0], "ex_w_gate"), (EXPERT_W[1], "ex_w_up")):
                v = a[src][l].rearrange("e (k p) n -> e p k n", p=P)
                e.dma_start(w[:, :, 512 * h:512 * h + 512], v[i, :, :, 512 * h:512 * h + 512]).then_inc(S(f"ff_wg{h}"), 16)

        def load_down(e, l, i, h, over):
            if over:
                e.wait_ge(S("ff_dn"), i * 8 + (8 * NE * l - 8 + 4 * (h + 1) + HEAD))
            v = a["ex_w_down"][l].rearrange("e (k p) n -> e p k n", p=P)
            e.dma_start(EXPERT_W[2][:, :, 512 * h:512 * h + 512], v[i, :, :, 512 * h:512 * h + 512]).then_inc(S(f"ff_wd{h}"), 16)

        GL, GC = small[:, 0:16], small[:, 16:32]
        IG, IS, CG = (small[:, 32 + 16 * n:48 + 16 * n].bitcast(U32) for n in range(3))

        def route(l):
            hT = V(0, (KD, T))
            rw = V(12288, (KD, NE))
            LR = V(12448, (T,))[0:NE]
            AT = V(13748, (NJ, NE))
            EX = V(13948, (NJ, NE))
            AF = V(14448, (T,))[0:NE]
            VL = V(17048, (CAP,))[0:NE]
            IX = V(17248, (CAP,))[0:NE].bitcast(U32)
            IF = V(17448, (CAP,))[0:NE]
            col = V(17648, (80,))
            r1, r2 = small[:, 100:100 + NJ], small[:, 112:112 + NJ]
            j0 = 0 if l == 0 else JC
            nj = NJ - j0
            t0 = j0 * P
            toks = [(x, min(512, T - x)) for x in range(t0, T, 512)]
            nb = (0, len([x for x in range(0, T, 512)]))[l]

            if l == 0:
                def room(e):
                    e.wait_ge(S("rt_l"), nb + len(toks))

                def between(e, n):
                    if n in (4, 8):
                        load_up(e, l, 0, n // 8, False)

                ada_sp, ada_silu, ada_sc, ada_pe, ada_po, ada_ve = ada_parts(
                    1, [V(35840 + 4096 * n, (KD, 512)) for n in range(2)], V(0, (6 * D,)), V(6 * D, (6 * D,)),
                    V(17800, (KD, 2)), (1, 2), 7, room, between)

            def sp(e):
                e.dma_start(rw, a["router_w"][l].rearrange("(k p) n -> p k n", p=P)).then_inc(S("rw_in"), 16)
                if l == 0:
                    ada_sp(e)
                else:
                    for h in range(2):
                        load_up(e, l, 0, h, False)
                    for h in range(2):
                        load_down(e, l, 0, h, False)

            def po(e):
                if l == 0:
                    for name in ("ff_hd", "ff_ol", "ff_ot", "ff_bt", "ff_dn", "ff_add"):
                        e.sem_inc(S(name), HEAD)
                    ada_po(e)

            def pe(e):
                e.wait_ge(S("rw_in"), 16 * (l + 1))
                for n, (x, w) in enumerate(toks):
                    for k in range(KD):
                        mm = e.matmul(ps[0:NE, n, 0:w], rw[:, k, :], hT[:, k, x:x + w], start=k == 0, stop=k == KD - 1)
                    mm.then_inc(S("rt_l"), 1)
                e.wait_ge(S("rt_lr"), nb + len(toks))
                for j in range(j0, NJ):
                    mm = e.transpose(ps[:, 3, NE * j:NE * j + NE], LR[:, j * P:(j + 1) * P], ident[0:NE, 0:NE])
                mm.then_inc(S("rt_t"), 1)
                e.wait_ge(S("rt_a"), l + 1)
                for j in range(j0, NJ):
                    mm = e.transpose(ps[0:NE, 4 + j // 4, P * (j % 4):P * (j % 4) + P], AT[:, j, :], ident)
                mm.then_inc(S("rt_t"), 1)
                if l == 0:
                    ada_pe(e)
                e.wait_ge(S("rt_if"), l + 1)
                for n, v in enumerate((VL, IF)):
                    e.transpose(ps[:, 0, 16 * n:16 * n + 16], v[:, 0:CAPL], ident[0:NE, 0:NE])
                    if l == 0:
                        e.transpose(ps[0:CAPC, 0, 32 + 16 * n:48 + 16 * n], v[:, CAPL:CAP], ident[0:NE, 0:NE])
                e.transpose(ps[:, 0, 64:80], IF[:, 0:CAPL], ident[0:NE, 0:NE]).then_inc(S("rt_t"), 1)

            def sc(e):
                if l == 0:
                    ada_silu(e)
                for n, (x, w) in enumerate(toks):
                    e.wait_ge(S("rt_l"), nb + n + 1)
                    e.activation(LR[:, x:x + w], ps[0:NE, n, 0:w], ACT.Copy).then_inc(S("rt_lr"), 1)
                e.wait_ge(S("rt_s"), l + 1)
                e.activation(EX[:, j0:, :], EX[:, j0:, :], ACT.Exp).then_inc(S("rt_e"), 1)
                if l == 0:
                    ada_sc(e)

            def ve(e):
                e.wait_ge(S("rt_t"), 3 * l + 1)
                lg = ps[:, 3, 0:NJ * NE].rearrange("p (j n) -> p j n", n=NE)[:, j0:, :]
                a_, x_ = AT[:, j0:, :], EX[:, j0:, :]
                m_, s_ = r1[:, 0:nj], r2[:, 0:nj]
                dve.step(e, e.tensor_reduce(m_, lg, AX.X, ALU.max))
                e.tensor_tensor(x_, lg, m_.unsqueeze(2).broadcast_to([P, nj, NE]), ALU.subtract).then_inc(S("rt_s"), 1)
                e.wait_ge(S("rt_e"), l + 1)
                dve.step(e, e.tensor_reduce(s_, x_, AX.X, ALU.add))
                dve.step(e, e.reciprocal(m_, s_))
                e.tensor_tensor(a_, x_, m_.unsqueeze(2).broadcast_to([P, nj, NE]), ALU.mult).then_inc(S("rt_a"), 1)
                e.wait_ge(S("rt_t"), 3 * l + 2)
                src = ps[0:NE, 4:7, :].rearrange("p b c -> p (b c)")
                dve.step(e, e.tensor_copy(AF[:, t0:T], src[:, t0:T]))
                for x0, x1, o, n in ((NCTX, T, 0, CAPL), (0, NCTX, CAPL, CAPC))[:2 - l]:
                    w = AF[:, x0:x1]
                    for q in range(o, o + n, 8):
                        dve.step(e, e.max(VL[:, q:q + 8], w))
                        dve.did(e.max_index(IX[:, q:q + 8], VL[:, q:q + 8], w))
                        dve.settle(e)
                        dve.step(e, e.match_replace(w, VL[:, q:q + 8], w, -1.0))
                nn = CAP if l == 0 else CAPL
                e.tensor_copy(IF[:, 0:nn], IX[:, 0:nn]).then_inc(S("rt_if"), 1)
                e.wait_ge(S("rt_t"), 3 * l + 3)
                dve.step(e, e.tensor_copy(col[:, 0:32], ps[:, 0, 0:32]))
                dve.did(e.tensor_copy(GL, col[:, 0:16]))
                dve.did(e.tensor_scalar(IG, col[:, 16:32], float(NCTX), None, ALU.add))
                dve.did(e.tensor_scalar(IS, col[:, 16:32], float(0 if l else NCTX), None, ALU.add))
                if l == 0:
                    dve.did(e.tensor_copy(GC[0:CAPC, :], ps[0:CAPC, 0, 32:48]))
                    dve.did(e.tensor_copy(CG[0:CAPC, :], ps[0:CAPC, 0, 48:64]))
                dve.settle(e)
                if l == 0:
                    ada_ve(e)

            stage(sync=sp, gpsimd=po, tensor=pe, scalar=sc, vector=ve)

        def ffn(l):
            wg, wu, wd = EXPERT_W
            G2 = V(0, (2, D))
            XL, XC = V(2048, (D,)), V(3072, (D,))
            tw = CAP if l == 0 else CAPL
            XT, HD, OT = (V(4096 + 1280 * n, (KD, CAP)) for n in range(3))
            OL, OC = V(7936, (D,)), V(8960, (D,))
            SG = [V(9984 + CAP * n, (CAP,)) for n in range(2)]
            slots = small[:, 96:104]
            ig, is_, cg, cs_ = (slots[:, n:n + 1].bitcast(U32) for n in range(4))
            gl, gc = slots[:, 4:5], slots[:, 5:6]
            dst = xres if l == 0 else out[0]
            E0 = NE * l
            per = 4 if l == 0 else 2

            def sp(e):
                for s in range(2):
                    e.dma_start(G2[:, s, :], modd[2 * l + s, 5 * D:6 * D].partition_broadcast(P)).then_inc(S("ff_g2"), 16)
                if l == 0:
                    for h in range(2):
                        load_down(e, l, 0, h, False)
                with e.Fori(1, NE) as i:
                    for h in range(2):
                        load_up(e, l, i, h, True)
                    for h in range(2):
                        load_down(e, l, i, h, True)

            def gather(e, i):
                c1 = lambda v, k=P: v[0:k, i:i + 1] if isinstance(i, int) else v[0:k, bass.ds(i, 1)]
                e.tensor_copy(ig, c1(IG)).then_inc(S("ff_ix"), 1)
                if l == 0:
                    e.tensor_copy(cg[0:CAPC], c1(CG, CAPC)).then_inc(S("ff_ix"), 1)
                e.wait_ge(S("ff_ix"), (i + 1) * ixn + ix0)
                e.sem_inc(S("ff_go"), 1)
                e.indirect_dma_start(out=XL, out_offset=None, in_=xnd, in_offset=bass.IndirectOffsetOnAxis(ap=ig, axis=0)).then_inc(S("ff_xl"), 16)
                if l == 0:
                    e.indirect_dma_start(out=XC[0:CAPC], out_offset=None, in_=xnd,
                                         in_offset=bass.IndirectOffsetOnAxis(ap=cg[0:CAPC], axis=0)).then_inc(S("ff_xl"), 16)

            ixn, ix0 = (2, 0) if l == 0 else (1, 2 * NE)
            dn, d0 = 16 * ixn, 16 * ix0

            def scatter(e, i):
                c1 = lambda v, k=P: v[0:k, i:i + 1] if isinstance(i, int) else v[0:k, bass.ds(i, 1)]
                e.tensor_copy(is_, c1(IS)).then_inc(S("ff_iy"), 1)
                if l == 0:
                    e.tensor_copy(cs_[0:CAPC], c1(CG, CAPC)).then_inc(S("ff_iy"), 1)
                e.wait_ge(S("ff_iy"), (i + 1) * ixn + ix0)
                e.wait_ge(S("ff_ol"), (i + 1) * ixn + ix0 + HEAD)
                e.sem_inc(S("ff_go"), 1)
                e.indirect_dma_start(out=dst, out_offset=bass.IndirectOffsetOnAxis(ap=is_, axis=0), in_=OL, in_offset=None,
                                     compute_op=ALU.add).then_inc(S("ff_st"), 16)
                if l == 0:
                    e.indirect_dma_start(out=dst, out_offset=bass.IndirectOffsetOnAxis(ap=cs_[0:CAPC], axis=0), in_=OC[0:CAPC], in_offset=None,
                                         compute_op=ALU.add).then_inc(S("ff_st"), 16)
                e.wait_ge(S("ff_st"), (i + 1) * dn + d0)
                e.sem_inc(S("ff_add"), 1)

            def po(e):
                gather(e, 0)
                with e.Fori(0, NE - 1) as i:
                    e.wait_ge(S("ff_xtt"), i + (E0 + 1))
                    gather(e, i + 1)
                    scatter(e, i)
                scatter(e, NE - 1)

            def turn(e, i):
                e.wait_ge(S("ff_xl"), (i + 1) * dn + d0)
                for k in range(KD):
                    mm = e.transpose(ps[:, k // 4, P * (k % 4):P * (k % 4) + P], XL[:, k * P:(k + 1) * P], ident)
                    if l == 0:
                        mm = e.transpose(ps[:, 2, CAPC * k:CAPC * (k + 1)], XC[0:CAPC, k * P:(k + 1) * P], ident[0:CAPC, 0:CAPC])
                mm.then_inc(S("ff_xtt"), 1)

            def pe(e):
                def expert(i, last):
                    b8 = i * 8 + 8 * E0
                    e.wait_ge(S("ff_xt"), (i + 1) * ixn + ix0)
                    e.wait_ge(S("ff_hd"), b8 + HEAD)
                    for f in range(8):
                        if f % 4 == 0:
                            e.wait_ge(S(f"ff_wg{f // 4}"), (i + 1) * 32 + 32 * E0)
                        if f >= 3:
                            e.wait_ge(S("ff_hd"), b8 + (f - 2) + HEAD)
                        for n, w in enumerate((wg, wu)):
                            for k in range(KD):
                                mm = e.matmul(ps[:, 3 + f % 3, 256 * n:256 * n + tw], w[:, k, f * P:(f + 1) * P], XT[:, k, 0:tw],
                                              start=k == 0, stop=k == KD - 1)
                        mm.then_inc(S("ff_gu"), 1)
                    if not last:
                        e.wait_ge(S("ff_ol"), i * ixn + ix0 + HEAD)
                        turn(e, i + 1)
                    e.wait_ge(S("ff_ot"), b8 + HEAD)
                    e.wait_ge(S("ff_hd"), b8 + 8 + HEAD)
                    e.wait_ge(S("ff_ol"), i * ixn + ix0 + HEAD)
                    for d in range(8):
                        if d % 4 == 0:
                            e.wait_ge(S(f"ff_wd{d // 4}"), (i + 1) * 16 + 16 * E0)
                        if d >= 2:
                            e.wait_ge(S("ff_ot"), b8 + (d - 1) + HEAD)
                        for k in range(KD):
                            mm = e.matmul(ps[:, 6 + d % 2, 0:tw], wd[:, k, d * P:(d + 1) * P], HD[:, k, 0:tw], start=k == 0, stop=k == KD - 1)
                        mm.then_inc(S("ff_dn"), 1)
                    e.wait_ge(S("ff_ot"), b8 + 8 + HEAD)
                    if not last:
                        e.wait_ge(S("ff_xt"), (i + 2) * ixn + ix0)
                    for d in range(8):
                        mm = e.transpose(ps[:, d // 4, P * (d % 4):P * (d % 4) + P], OT[:, d, 0:CAPL], ident)
                        if l == 0:
                            mm = e.transpose(ps[0:CAPC, 6 + d // 4, P * (d % 4):P * (d % 4) + P], OT[:, d, CAPL:CAP], ident)
                    mm.then_inc(S("ff_bt"), 1)

                turn(e, 0)
                with e.Fori(0, NE - 1) as i:
                    expert(i, False)
                expert(NE - 1, True)

            def sc(e):
                with e.Fori(0, NE) as i:
                    b8 = i * 8 + 8 * E0
                    for f in range(8):
                        e.wait_ge(S("ff_gu"), b8 + (f + 1))
                        e.wait_ge(S("ff_hd"), b8 + max(f - 1, 0) + HEAD)
                        e.activation(SG[f % 2][:, 0:tw], ps[:, 3 + f % 3, 0:tw], ACT.Silu).then_inc(S("ff_sg"), 1)
                    e.wait_ge(S("ff_bt"), i + E0 + HEAD)
                    for d in range(8):
                        e.wait_ge(S("ff_dn"), b8 + (d + 1) + HEAD)
                        e.activation(OT[:, d, 0:tw], ps[:, 6 + d % 2, 0:tw], ACT.Copy).then_inc(S("ff_ot"), 1)

            def modulate(e, i):
                e.wait_ge(S("ff_xtt"), i + (E0 + 1))
                for s, k0, w, src in ((1, 0, CAPL, ps[:, 0:2, :].rearrange("p b (k t) -> p (b k) t", k=4)),
                                      (0, CAPL, CAPC, ps[:, 2, 0:256].rearrange("p (k t) -> p k t", k=KD)))[:2 - l]:
                    o = XT[:, :, k0:k0 + w]
                    sc_, sh = (AB[:, 1, s, q, :].unsqueeze(2).broadcast_to([P, KD, w]) for q in range(2))
                    dve.step(e, e.tensor_tensor(o, src, sc_, ALU.mult))
                    e.tensor_tensor(o, o, sh, ALU.add).then_inc(S("ff_xt"), 1)

            def ve(e):
                def expert(i, last):
                    b8 = i * 8 + 8 * E0
                    e.wait_ge(S("ff_dn"), b8 + HEAD)
                    for f in range(8):
                        e.wait_ge(S("ff_sg"), b8 + (f + 1))
                        e.tensor_tensor(HD[:, f, 0:tw], SG[f % 2][:, 0:tw], ps[:, 3 + f % 3, 256:256 + tw], ALU.mult).then_inc(S("ff_hd"), 1)
                    if not last:
                        modulate(e, i + 1)
                    c1 = lambda v, k=P: v[0:k, i:i + 1] if isinstance(i, int) else v[0:k, bass.ds(i, 1)]
                    e.wait_ge(S("ff_ol"), i * ixn + ix0 + HEAD)
                    dve.did(e.tensor_copy(gl, c1(GL)))
                    if l == 0:
                        dve.did(e.tensor_copy(gc[0:CAPC], c1(GC, CAPC)))
                    dve.settle(e)
                    e.wait_ge(S("ff_bt"), i + (E0 + 1) + HEAD)
                    e.wait_ge(S("ff_add"), i + E0 + HEAD)
                    e.scalar_tensor_tensor(OL, ps[:, 0:2, :].rearrange("p b c -> p (b c)"), gl, G2[:, 1, :], ALU.mult, ALU.mult)\
                     .then_inc(S("ff_ol"), 1)
                    if l == 0:
                        e.scalar_tensor_tensor(OC[0:CAPC], ps[0:CAPC, 6:8, :].rearrange("p b c -> p (b c)"), gc[0:CAPC], G2[0:CAPC, 0, :],
                                               ALU.mult, ALU.mult).then_inc(S("ff_ol"), 1)

                e.wait_ge(S("ff_g2"), 32 * (l + 1))
                modulate(e, 0)
                n0 = dve.n
                with e.Fori(0, NE - 1) as i:
                    dve.more = i * per
                    expert(i, False)
                assert dve.n == n0 + per
                dve.more, dve.n = 0, n0 + per * (NE - 1)
                expert(NE - 1, True)

            stage(sync=sp, gpsimd=po, tensor=pe, scalar=sc, vector=ve)

        def run(e, name):
            for n, st in enumerate(stages):
                if n:
                    e.wait_ge(ended, 5 * n)
                if name in st:
                    st[name](e)
                e.drain().then_inc(ended, 1)

        for l in range(DEPTH):
            ada(l)
            norm(l, 0)
            proj(l)
            mlstm(l)
            hgrn(l)
            mla(l)
            wout(l)
            norm(l, 1)
            route(l)
            ffn(l)

        block = c.enter_context(nc.Block())

        @block.sync
        def _(e):
            e.dma_start(cst[:, :], a["const"]).then_inc(const_in, 16)
            e.dma_start(ropes[:, :, :], a["rope"].rearrange("(j p) c -> p j c", p=P)).then_inc(const_in, 16)
            e.wait_ge(const_in, 32)
            run(e, "sync")

        @block.scalar
        def _(e):
            e.wait_ge(const_in, 32)
            run(e, "scalar")

        @block.gpsimd
        def _(e):
            e.wait_ge(const_in, 32)
            run(e, "gpsimd")

        @block.vector
        def _(e):
            e.wait_ge(const_in, 32)
            run(e, "vector")

        @block.tensor
        def _(e):
            e.wait_ge(const_in, 32)
            run(e, "tensor")


_INS = ["x", "c", "ctx", "c_ctx", "ada_w", "ada_b", "norm1_g", "norm2_g", "w_in", "b_in", "ml_conv_w", "ml_conv_b",
        "ml_norm_g", "hg_lb_logits", "hg_norm_g", "mla_q_norm_g", "mla_w_uq", "mla_kv_norm_g", "mla_w_ukv",
        "mla_q_qk_g", "mla_k_qk_g", "w_out", "router_w", "ex_w_gate", "ex_w_up", "ex_w_down"]


def kernel(**inputs):
    import concourse.bacc as _bacc
    from concourse.bass_utils import run_bass_kernel_spmd as _run

    nc = _bacc.Bacc("TRN2", target_bir_lowering=False, num_devices=1)
    given = {n: np.ascontiguousarray(inputs[n]) for n in _INS}
    given |= {"const": consts()[0], "rope": rope_table()}
    arrays, aps = {}, {}
    for name, v in given.items():
        arrays[f"in_{name}"] = v
        aps[name] = nc.dram_tensor(f"in_{name}", v.shape, mybir.dt.from_np(v.dtype), kind="ExternalInput").ap()
    out = nc.dram_tensor("out_0", (1, NLAT, D), F32, kind="ExternalOutput").ap()
    build(nc, aps, out)
    r = _run(nc, [arrays], core_ids=[0])
    return r.results[0]["out_0"]
```
